# Optimizing a Trainium2 kernel written in Bass

```python
import math
import jax, jax.numpy as jnp
from jax import lax
import numpy as np

D_MODEL = 2048
BATCH = 1
SEQ = 512
DEPTH = 1

ATTN_HEADS = 16
HEAD_DIM = 64
ATTN_WIDTH = ATTN_HEADS * HEAD_DIM
SSM_GROUP = 16
SSM_GROUPS = (D_MODEL - ATTN_WIDTH) // SSM_GROUP
SSM_WIDTH = SSM_GROUPS * SSM_GROUP
MIX_WIDTH = ATTN_WIDTH + SSM_WIDTH
IN_WIDTH = 3 * ATTN_WIDTH + SSM_WIDTH
SSM_STATE = 64
DILATED_PATTERNS = ((128, 1), (512, 4), (2048, 16))
ATTN_BLOCK = 128
ROPE_THETA = 10000.0
NEG_INF = -1e30
PEER_HEADS = 8
PEER_KEY_DIM = 256
PEER_SUB_DIM = PEER_KEY_DIM // 2
PEER_N_KEYS = 128
PEER_N_EXPERTS = PEER_N_KEYS * PEER_N_KEYS
PEER_TOPK = 16
PEER_CHUNK = 128
LN_EPS = 1e-5
DEEPNORM_ALPHA = (2.0 * DEPTH) ** 0.25
DEEPNORM_BETA = (8.0 * DEPTH) ** -0.25
ADA_SCALE = 0.3

kernel_name = "hymba_dilated_s5_peer_deepnorm_block"

def _layernorm(x, g=None, b=None):
    xf = x.astype(jnp.float32)
    mu = jnp.mean(xf, axis=-1, keepdims=True)
    var = jnp.mean(jnp.square(xf - mu), axis=-1, keepdims=True)
    y = (xf - mu) * lax.rsqrt(var + LN_EPS)
    if g is not None:
        y = y * g.astype(jnp.float32) + b.astype(jnp.float32)
    return y.astype(x.dtype)

def _rmsnorm(x, g):
    xf = x.astype(jnp.float32)
    y = xf * lax.rsqrt(jnp.mean(jnp.square(xf), axis=-1, keepdims=True) + LN_EPS)
    return (y * g.astype(jnp.float32)).astype(x.dtype)

def _rope(x, positions):
    half = HEAD_DIM // 2
    inv_freq = ROPE_THETA ** (-jnp.arange(half, dtype=jnp.float32) / half)
    ang = positions.astype(jnp.float32)[..., None] * inv_freq
    cos = jnp.cos(ang)[:, :, None, :]
    sin = jnp.sin(ang)[:, :, None, :]
    xf = x.astype(jnp.float32)
    x1, x2 = xf[..., :half], xf[..., half:]
    return jnp.concatenate([x1 * cos - x2 * sin, x2 * cos + x1 * sin], axis=-1).astype(x.dtype)

def _dilated_window_attention(q, k, v, window, dilation):
    B, S, H, E = q.shape
    L = S // dilation
    W = window // dilation
    nb = -(-L // ATTN_BLOCK)
    Lp = nb * ATTN_BLOCK

    def to_blocks(t):
        t = t.reshape(B, L, dilation, H, E).transpose(0, 2, 1, 3, 4)
        t = jnp.pad(t, ((0, 0), (0, 0), (0, Lp - L), (0, 0), (0, 0)))
        return t.reshape(B, dilation, nb, ATTN_BLOCK, H, E)

    def with_prev(t):
        prev = jnp.pad(t, ((0, 0), (0, 0), (1, 0), (0, 0), (0, 0), (0, 0)))[:, :, :-1]
        return jnp.concatenate([prev, t], axis=3)

    qb, kb, vb = to_blocks(q), to_blocks(k), to_blocks(v)
    kw, vw = with_prev(kb), with_prev(vb)
    s = jnp.einsum('bdnqhe,bdnkhe->bdnhqk', qb, kw,
                   preferred_element_type=jnp.float32) * (E ** -0.5)
    qi = jnp.arange(ATTN_BLOCK)[:, None] + ATTN_BLOCK
    kj = jnp.arange(2 * ATTN_BLOCK)[None, :]
    rel = qi - kj
    band = (rel >= 0) & (rel <= W)
    has_prev = (jnp.arange(nb)[:, None, None] > 0) | (kj >= ATTN_BLOCK)[None]
    mask = band[None] & has_prev
    s = jnp.where(mask[None, None, :, None], s, NEG_INF)
    m = jnp.max(s, axis=-1, keepdims=True)
    p = jnp.exp(s - m)
    l = jnp.sum(p, axis=-1, keepdims=True)
    o = jnp.einsum('bdnhqk,bdnkhe->bdnqhe', p / l, vw.astype(jnp.float32))
    lse = (m + jnp.log(l))[..., 0]
    o = o.reshape(B, dilation, Lp, H, E)[:, :, :L].transpose(0, 2, 1, 3, 4).reshape(B, S, H, E)
    lse = lse.transpose(0, 1, 2, 4, 3).reshape(B, dilation, Lp, H)[:, :, :L]
    lse = lse.transpose(0, 2, 1, 3).reshape(B, S, H)
    return o, lse

def _complex_affine_combine(e1, e2):
    a1r, a1i, b1r, b1i = e1
    a2r, a2i, b2r, b2i = e2
    ar = a2r * a1r - a2i * a1i
    ai = a2r * a1i + a2i * a1r
    br = a2r * b1r - a2i * b1i + b2r
    bi = a2r * b1i + a2i * b1r + b2i
    return (ar, ai, br, bi)

def _s5(u, lam_re, lam_im, log_dt, b_re, b_im, c_re, c_im, d_skip):
    uf = u.astype(jnp.float32)
    dt = jnp.exp(log_dt.astype(jnp.float32))[:, None]
    lr = lam_re.astype(jnp.float32)
    li = lam_im.astype(jnp.float32)
    mag = jnp.exp(lr * dt)
    ar = mag * jnp.cos(li * dt)
    ai = mag * jnp.sin(li * dt)
    den = lr * lr + li * li
    cr = ((ar - 1.0) * lr + ai * li) / den
    ci = (ai * lr - (ar - 1.0) * li) / den
    br = b_re.astype(jnp.float32)
    bi = b_im.astype(jnp.float32)
    bbar_re = cr[..., None] * br - ci[..., None] * bi
    bbar_im = cr[..., None] * bi + ci[..., None] * br
    bu_re = jnp.einsum('bsgp,gnp->bsgn', uf, bbar_re)
    bu_im = jnp.einsum('bsgp,gnp->bsgn', uf, bbar_im)
    a_re = jnp.broadcast_to(ar, bu_re.shape)
    a_im = jnp.broadcast_to(ai, bu_im.shape)
    _, _, h_re, h_im = lax.associative_scan(_complex_affine_combine,
                                            (a_re, a_im, bu_re, bu_im), axis=1)
    y = (jnp.einsum('bsgn,gpn->bsgp', h_re, c_re.astype(jnp.float32))
         - jnp.einsum('bsgn,gpn->bsgp', h_im, c_im.astype(jnp.float32))
         + d_skip.astype(jnp.float32) * uf)
    return y

def _peer(h, w_qp, sub_keys, expert_u, expert_v):
    B, S, D = h.shape
    T = B * S
    t = h.reshape(T, D)
    q = (t @ w_qp).reshape(T, PEER_HEADS, 2, PEER_SUB_DIM)
    s = jnp.einsum('thic,ikc->thik', q, sub_keys,
                   preferred_element_type=jnp.float32)
    top_s, top_i = lax.top_k(s, PEER_TOPK)
    cand = top_s[:, :, 0, :, None] + top_s[:, :, 1, None, :]
    best_s, best = lax.top_k(cand.reshape(T, PEER_HEADS, PEER_TOPK * PEER_TOPK), PEER_TOPK)
    i0 = jnp.take_along_axis(top_i[:, :, 0], best // PEER_TOPK, axis=-1)
    i1 = jnp.take_along_axis(top_i[:, :, 1], best % PEER_TOPK, axis=-1)
    experts = i0 * PEER_N_KEYS + i1
    gates = jax.nn.softmax(best_s, axis=-1)
    nc = T // PEER_CHUNK

    def chunk(args):
        tc, ec, gc = args
        u = expert_u[ec]
        v = expert_v[ec]
        act = jax.nn.gelu(jnp.einsum('td,thkd->thk', tc, u,
                                     preferred_element_type=jnp.float32), approximate=False)
        return jnp.einsum('thk,thkd->td', gc * act, v.astype(jnp.float32))

    y = lax.map(chunk, (t.reshape(nc, PEER_CHUNK, D),
                        experts.reshape(nc, PEER_CHUNK, PEER_HEADS, PEER_TOPK),
                        gates.reshape(nc, PEER_CHUNK, PEER_HEADS, PEER_TOPK)))
    return y.reshape(B, S, D).astype(h.dtype)

def setup_inputs(seed: int = 0) -> dict:
    key = jax.random.key(seed)
    ks = jax.random.split(key, 32)
    f32 = jnp.float32
    nrm = lambda k, shape, scale: jax.random.normal(k, shape, f32) * scale
    L, D = DEPTH, D_MODEL
    x = nrm(ks[0], (BATCH, SEQ, D), 1.0)
    c = nrm(ks[1], (BATCH, D), 1.0)
    positions = jnp.broadcast_to(jnp.arange(SEQ, dtype=jnp.int32), (BATCH, SEQ))
    w_ada = nrm(ks[2], (L, D, 6 * D), ADA_SCALE * D ** -0.5)
    b_ada = nrm(ks[3], (L, 6 * D), 0.02)
    col_scale = jnp.concatenate([jnp.ones((2 * ATTN_WIDTH,), f32),
                                 jnp.full((ATTN_WIDTH,), DEEPNORM_BETA, f32),
                                 jnp.ones((SSM_WIDTH,), f32)])
    w_in = nrm(ks[4], (L, D, IN_WIDTH), D ** -0.5) * col_scale
    lam_re = -0.5 + nrm(ks[5], (L, SSM_GROUPS, SSM_STATE), 0.01)
    lam_im = math.pi * jnp.arange(SSM_STATE, dtype=f32) + nrm(ks[6], (L, SSM_GROUPS, SSM_STATE), 0.01)
    log_dt = jax.random.uniform(ks[7], (L, SSM_GROUPS), f32, math.log(1e-3), math.log(1e-1))
    ssm_b_re = nrm(ks[8], (L, SSM_GROUPS, SSM_STATE, SSM_GROUP), (2 * SSM_GROUP) ** -0.5)
    ssm_b_im = nrm(ks[9], (L, SSM_GROUPS, SSM_STATE, SSM_GROUP), (2 * SSM_GROUP) ** -0.5)
    ssm_c_re = nrm(ks[10], (L, SSM_GROUPS, SSM_GROUP, SSM_STATE), (2 * SSM_STATE) ** -0.5)
    ssm_c_im = nrm(ks[11], (L, SSM_GROUPS, SSM_GROUP, SSM_STATE), (2 * SSM_STATE) ** -0.5)
    ssm_d = nrm(ks[12], (L, SSM_GROUPS, SSM_GROUP), 1.0)
    w_glu = nrm(ks[13], (L, SSM_WIDTH, SSM_WIDTH), SSM_WIDTH ** -0.5)
    b_glu = nrm(ks[14], (L, SSM_WIDTH), 0.02)
    g_attn = 1.0 + nrm(ks[15], (L, ATTN_WIDTH), 0.02)
    g_ssm = 1.0 + nrm(ks[16], (L, SSM_WIDTH), 0.02)
    w_out = nrm(ks[17], (L, MIX_WIDTH, D), DEEPNORM_BETA * MIX_WIDTH ** -0.5)
    ln1_g = 1.0 + nrm(ks[18], (L, D), 0.02)
    ln1_b = nrm(ks[19], (L, D), 0.02)
    w_qp = nrm(ks[20], (L, D, PEER_HEADS * PEER_KEY_DIM), D ** -0.5)
    sub_keys = nrm(ks[21], (L, 2, PEER_N_KEYS, PEER_SUB_DIM), PEER_SUB_DIM ** -0.5)
    expert_u = nrm(ks[22], (L, PEER_N_EXPERTS, D), D ** -0.5)
    expert_v = nrm(ks[23], (L, PEER_N_EXPERTS, D), DEEPNORM_BETA)
    ln2_g = 1.0 + nrm(ks[24], (L, D), 0.02)
    ln2_b = nrm(ks[25], (L, D), 0.02)
    return {"x": x, "c": c, "positions": positions, "w_ada": w_ada, "b_ada": b_ada,
            "w_in": w_in, "lam_re": lam_re, "lam_im": lam_im, "log_dt": log_dt,
            "ssm_b_re": ssm_b_re, "ssm_b_im": ssm_b_im, "ssm_c_re": ssm_c_re,
            "ssm_c_im": ssm_c_im, "ssm_d": ssm_d, "w_glu": w_glu, "b_glu": b_glu,
            "g_attn": g_attn, "g_ssm": g_ssm, "w_out": w_out, "ln1_g": ln1_g,
            "ln1_b": ln1_b, "w_qp": w_qp, "sub_keys": sub_keys, "expert_u": expert_u,
            "expert_v": expert_v, "ln2_g": ln2_g, "ln2_b": ln2_b}

def reference(x, c, positions, w_ada, b_ada, w_in, lam_re, lam_im, log_dt,
              ssm_b_re, ssm_b_im, ssm_c_re, ssm_c_im, ssm_d, w_glu, b_glu,
              g_attn, g_ssm, w_out, ln1_g, ln1_b, w_qp, sub_keys, expert_u,
              expert_v, ln2_g, ln2_b):
    B, S, D = x.shape
    for l in range(DEPTH):
        mod = jax.nn.silu(c) @ w_ada[l] + b_ada[l]
        sh1, sc1, gt1, sh2, sc2, gt2 = [m[:, None, :] for m in jnp.split(mod, 6, axis=-1)]

        h = _layernorm(x) * (1.0 + sc1) + sh1
        z = h @ w_in[l]
        q, k, v, u = jnp.split(z, [ATTN_WIDTH, 2 * ATTN_WIDTH, 3 * ATTN_WIDTH], axis=-1)
        q = _rope(q.reshape(B, S, ATTN_HEADS, HEAD_DIM), positions)
        k = _rope(k.reshape(B, S, ATTN_HEADS, HEAD_DIM), positions)
        v = v.reshape(B, S, ATTN_HEADS, HEAD_DIM)
        outs, lses = [], []
        for window, dilation in DILATED_PATTERNS:
            o_p, lse_p = _dilated_window_attention(q, k, v, window, dilation)
            outs.append(o_p)
            lses.append(lse_p)
        wts = jax.nn.softmax(jnp.stack(lses, axis=0), axis=0)
        attn = jnp.sum(wts[..., None] * jnp.stack(outs, axis=0), axis=0)
        attn = attn.reshape(B, S, ATTN_WIDTH).astype(x.dtype)

        y = _s5(u.reshape(B, S, SSM_GROUPS, SSM_GROUP), lam_re[l], lam_im[l], log_dt[l],
                ssm_b_re[l], ssm_b_im[l], ssm_c_re[l], ssm_c_im[l], ssm_d[l])
        y = jax.nn.gelu(y.reshape(B, S, SSM_WIDTH), approximate=False)
        y = (y * jax.nn.sigmoid(y @ w_glu[l] + b_glu[l])).astype(x.dtype)

        mixed = jnp.concatenate([_rmsnorm(attn, g_attn[l]), _rmsnorm(y, g_ssm[l])], axis=-1)
        mix_out = mixed @ w_out[l]
        x = _layernorm(DEEPNORM_ALPHA * x + (1.0 + gt1) * mix_out, ln1_g[l], ln1_b[l])

        h2 = _layernorm(x) * (1.0 + sc2) + sh2
        ffn = _peer(h2, w_qp[l], sub_keys[l], expert_u[l], expert_v[l])
        x = _layernorm(DEEPNORM_ALPHA * x + (1.0 + gt2) * ffn, ln2_g[l], ln2_b[l])
    return x


_drawn_inputs = setup_inputs


def setup_inputs(seed=0):
    import zlib

    import numpy as np

    out = dict(_drawn_inputs(seed))
    spreads = {}
    factors = {'lam_re': 64.0,
     'b_glu': 3.959,
     'ln2_g': 8.099,
     'ln2_b': 7.772,
     'ssm_b_re': 2.721,
     'ssm_b_im': 2.681,
     'ssm_c_re': 2.792,
     'ssm_c_im': 2.743}
    for name, (base, spread) in spreads.items():
        noise = np.random.default_rng([zlib.crc32(name.encode()), seed]).standard_normal(out[name].shape)
        drawn = base * np.exp(spread * noise) if base else spread * noise
        out[name] = __import__('jax').numpy.asarray(drawn.astype(out[name].dtype))
    for name, factor in factors.items():
        out[name] = (out[name] * factor).astype(out[name].dtype)
    return out
```

```python
from contextlib import ExitStack

import numpy as np

import concourse.bass as bass
from concourse import mybir

F32 = mybir.dt.float32
I32 = mybir.dt.int32
U32 = mybir.dt.uint32
ALU = mybir.AluOpType
ACT = mybir.ActivationFunctionType
AX = mybir.AxisListType.X

P = 128
T = 512
TT = T // P
D = 2048
KD = D // P
HEADS, HD = 16, 64
AW = HEADS * HD
SW = D - AW
G, GP, NS = 64, 16, 64
ST = G * NS // P
SC = SW // P
PH, TOPK, NK = 8, 16, 128
SLOTS = PH * TOPK
EPS = 1e-5
ALPHA = 2.0 ** 0.25
NEG = -1e30
TWO_PI = 6.283185307179586
C1 = 6.28125
C2 = 0.0019350051879882812
C3 = TWO_PI - C1 - C2
PI_LOW = 3.1415925
HALF_TURN = 0.49999997
ROUND = 12582912.0
ROUND13 = 1536.0
PC = 256
RING = 3
NB = 8

K_ID = 0
K_MASK = K_ID + P
K_SWAP = K_MASK + TT * T
K_TIME = K_SWAP + P
K_FREQ = K_TIME + T
K_IOTA = K_FREQ + 1
K_ONE = K_IOTA + TOPK
K_END = K_ONE + P


def constants():
    a = np.zeros((P, K_END), np.float32)
    a[:, K_ID:K_ID + P] = np.eye(P)
    t = np.arange(T)[:, None]
    s = np.arange(T)[None, :]
    d = t - s
    count = ((d >= 0) & (d <= 128)).astype(np.int64)
    count += (d >= 0) & (d % 4 == 0)
    count += (d >= 0) & (d % 16 == 0)
    bias = np.where(count > 0, HD ** 0.5 * np.log(np.maximum(count, 1)), NEG).astype(np.float32)
    for i in range(TT):
        a[:, K_MASK + i * T:K_MASK + (i + 1) * T] = bias[i * P:(i + 1) * P]
    for m in range(P):
        half = HD // 2
        if m % HD < half:
            a[m + half, K_SWAP + m] = -1.0
        else:
            a[m - half, K_SWAP + m] = 1.0
    a[:, K_TIME:K_TIME + T] = np.arange(T)
    half = HD // 2
    a[:, K_FREQ] = np.power(np.float32(10000.0), -np.arange(half, dtype=np.float32) / np.float32(half))[np.arange(P) % half]
    a[:, K_IOTA:K_IOTA + TOPK] = np.arange(TOPK)
    a[:, K_ONE:K_ONE + P] = 1.0
    return a


def hybrid_layer(nc, consts, x, c, positions, w_ada, b_ada, w_in, lam_re, lam_im, log_dt, ssm_b_re, ssm_b_im,
                 ssm_c_re, ssm_c_im, ssm_d, w_glu, b_glu, g_attn, g_ssm, w_out, ln1_g, ln1_b, w_qp, sub_keys,
                 expert_u, expert_v, ln2_g, ln2_b, mod_rows, out):
    ctx = ExitStack()

    def sb(name, shape, dt=F32):
        return ctx.enter_context(nc.sbuf_tensor(name, shape, dt))

    def sem(name):
        return ctx.enter_context(nc.semaphore(name))

    with ctx:
        kc = sb("kc", [P, K_END])
        ident = kc[:, K_ID:K_ID + P]
        ones = kc[:, K_ONE:K_ONE + P]
        swap = kc[:, K_SWAP:K_SWAP + P]
        times = kc[:, K_TIME:K_TIME + T]
        small = sb("small", [P, 1024])
        resid = sb("resid", [P, TT, D])
        region_a = sb("region_a", [P, 8192])
        wring = sb("wring", [P, RING, KD, PC])
        region_b = sb("region_b", [P, 8192])
        region_c = sb("region_c", [P, 8192])
        ps = ctx.enter_context(nc.psum_tensor("ps", [P, 8, 512], F32))

        modT = small[:, 0:96]
        cT = small[:, 96:112]
        csig = small[:, 112:128]
        vecs = small[:, 128:160]
        g_attn_c, g_ssm_c, b_glu_c, d_c = (vecs[:, 8 * n:8 * n + 8] for n in range(4))
        lam = small[:, 160:256]
        s5c = small[:, 256:256 + 32 * 16].rearrange("p (n s) -> p n s", s=32)
        stats = small[:, 768:792].rearrange("p (n s) -> p n s", s=6)
        mv = small[:, 792:800].rearrange("p (n s) -> p n s", s=2)
        rstd = small[:, 800:804]
        tiny = small[:, 804:820]

        hT = region_a[:, :].rearrange("p (k t) -> p k t", k=KD)
        xhat = region_b[:, :].rearrange("p (t d) -> p t d", t=TT)
        v_tok = region_c[:, 0:4096].rearrange("p (t d) -> p t d", t=TT)
        uT = region_c[:, 4096:8192].rearrange("p (m t) -> p m t", m=SC)
        qT = region_b[:, 0:4096].rearrange("p (m t) -> p m t", m=8)
        kT = region_b[:, 4096:8192].rearrange("p (m t) -> p m t", m=8)

        def panels_of(w, cols, rows=KD):
            v = w.rearrange("(k p) n -> p k n", p=P)
            return [(v[:, :, n:n + PC], rows) for n in cols]

        ada = w_ada.rearrange("l a b -> (l a) b")
        win = w_in.rearrange("l a b -> (l a) b")
        ADA1 = panels_of(ada, range(0, 2 * D, PC))
        UP = panels_of(win, range(3 * AW, 3 * AW + SW, PC))
        ADA2 = panels_of(ada, range(2 * D, 6 * D, PC))
        QKV = panels_of(win, range(0, 3 * AW, PC))
        GLU = panels_of(w_glu.rearrange("l a b -> (l a) b"), range(0, SW, PC), SC)
        OUT = panels_of(w_out.rearrange("l a b -> (l a) b"), range(0, D, PC))
        QP = panels_of(w_qp.rearrange("l a b -> (l a) b"), range(0, PH * 2 * P, PC))
        panels = ADA1 + UP + ADA2 + QKV + GLU + OUT + QP
        first = {}
        at = 0
        for name, lot in (("ada1", ADA1), ("u", UP), ("ada2", ADA2), ("qkv", QKV), ("glu", GLU), ("out", OUT), ("qp", QP)):
            first[name] = at
            at += len(lot)
        first["end"] = at
        panel_in = [sem(f"panel_in{s}") for s in range(RING)]
        panel_used = sem("panel_used")

        def load_panels(sp, lo, hi):
            for g in range(lo, min(hi, len(panels))):
                src, rows = panels[g]
                if g >= RING:
                    sp.wait_ge(panel_used, g - RING + 1)
                sp.dma_start(wring[:, g % RING, 0:rows, :], src).then_inc(panel_in[g % RING], 16)

        def panel(pe, g):
            pe.wait_ge(panel_in[g % RING], 16 * (g // RING + 1))
            return wring[:, g % RING, :, :]

        def ada_panel(pe, g, col):
            w = panel(pe, g)
            for n in range(2):
                for k in range(KD):
                    mm = pe.matmul(ps[:, 7, col + n:col + n + 1], w[:, k, n * P:(n + 1) * P], csig[:, k:k + 1],
                                   start=(col % 96 == 0 and n == 0 and k == 0), stop=(k == KD - 1),
                                   skip_group_check=True)
            mm.then_inc(panel_used, 1)

        class Chain:

            def __init__(self, eng, s):
                self.eng, self.s, self.n = eng, s, 0

            def __call__(self, ins):
                ins.then_inc(self.s, 1)
                self.n += 1
                self.eng.wait_ge(self.s, self.n)
                return self.n

        x_v = x.rearrange("b (t p) d -> p (b t) d", p=P)
        BT = [region_c[:, 1024 * n:1024 * (n + 1)].rearrange("p (q s) -> p q s", q=SC) for n in (0, 1)]
        CT = [region_c[:, 1024 * n:1024 * (n + 1)].rearrange("p (q s) -> p q s", q=SC) for n in (2, 3)]

        with ExitStack() as one:
            def sem1(name):
                return one.enter_context(nc.semaphore(name))

            rows_in = sem1("rows_in")
            const_in = sem1("const_in")
            x_in = sem1("x_in")
            b_in = sem1("b_in")
            c_in = sem1("c_in")
            cz = sem1("cd_zeroed")
            ldt_wide = sem1("ldt_wide")
            rows_T = sem1("rows_T")
            rows_c = sem1("rows_copied")
            silu_e = sem1("silu_exp")
            silu_d = sem1("silu_done")
            dch = sem1("dve_chain1")
            var_ok = sem1("var_ready")
            sq_ok = sem1("sqrt_ready")
            xh_ok = sem1("xhat_ready")
            tr_ok = sem1("xT_in_psum")
            ev_ok = sem1("xT_copied")
            s5_ask = sem1("s5_asks_act")
            s5_act = sem1("s5_act_done")
            bd_ok = sem1("bd_ready")
            bt_ps = sem1("bt_in_psum")
            bt_ev = sem1("bt_copied")
            ct_ps = sem1("ct_in_psum")
            h_ok = sem1("hT_ready")
            rows = one.enter_context(nc.sbuf_tensor("rows", [P, 3, P], F32))
            Bn = one.enter_context(nc.sbuf_tensor("Bn", [P, 2, ST, GP], F32))
            Bt = region_a[:, 0:2048].rearrange("p (n f) -> p n f", n=4)
            Bd = region_a[:, 2048:4096].rearrange("p (n i e) -> p n i e", n=2, e=2 * GP)
            Cd = region_a[:, 4096:6144].rearrange("p (n q e) -> p n q e", n=2, e=P)

            with nc.Block() as block:
                @block.sync
                def _(sp):
                    sp.dma_start(kc[:, :], consts).then_inc(const_in, 16)
                    sp.dma_start(rows[0:96, 0, :], b_ada.rearrange("l (j p) -> (l j) p", p=P)).then_inc(rows_in, 16)
                    sp.dma_start(rows[96:112, 0, :], c.rearrange("b (j p) -> (b j) p", p=P)).then_inc(rows_in, 16)
                    sp.dma_start(rows[0:32, 1, :], lam_re.rearrange("l (i g) n -> (l i) (g n)", g=2)).then_inc(rows_in, 16)
                    sp.dma_start(rows[32:64, 1, :], lam_im.rearrange("l (i g) n -> (l i) (g n)", g=2)).then_inc(rows_in, 16)
                    sp.dma_start(small[64:96, 804:806], log_dt.rearrange("l (i g) -> (l i) g", g=2)).then_inc(rows_in, 16)
                    for n, vec in enumerate((g_attn, g_ssm, b_glu)):
                        sp.dma_start(rows[8 * n:8 * n + 8, 2, :], vec.rearrange("l (j p) -> (l j) p", p=P)).then_inc(rows_in, 16)
                    sp.dma_start(rows[24:32, 2, :], ssm_d.rearrange("l (j g) q -> (l j) (g q)", j=8)).then_inc(rows_in, 16)
                    load_panels(sp, 0, 2)
                    for t in range(TT):
                        sp.dma_start(resid[:, t, :], x_v[:, t, :]).then_inc(x_in, 16)
                    for n, b in enumerate((ssm_b_re, ssm_b_im)):
                        sp.dma_start(Bn[:, n], b.rearrange("l (i g) n q -> (g n) (l i) q", g=2)).then_inc(b_in, 16)
                    load_panels(sp, 2, 6)
                    sp.wait_ge(cz, 1)
                    for n, cc in enumerate((ssm_c_re, ssm_c_im)):
                        for r in range(8):
                            sp.dma_start(Cd[GP * r:GP * (r + 1), n, :, NS * (r % 2):NS * (r % 2) + NS],
                                         cc.rearrange("l (q r) e n -> r e (l q) n", r=8)[r]).then_inc(c_in, 16)
                    load_panels(sp, 6, first["u"] + RING)

                @block.gpsimd
                def _(pool):
                    pool.memset(Cd[:, :, :, :], 0.0).then_inc(cz, 1)
                    pool.memset(Bd[:, :, :, :], 0.0).then_inc(cz, 1)

                @block.scalar
                def _(act):
                    act.wait_ge(rows_T, 1)
                    act.copy(cT, ps[:, 0, 96:112]).then_inc(rows_c, 1)
                    act.wait_ge(rows_c, 1)
                    act.activation(csig, cT, ACT.Exp, scale=-1.0).then_inc(silu_e, 1)
                    act.wait_ge(s5_ask, 1)
                    act.activation(s5c[:, 0, :], lam[:, 64:96], ACT.Exp).then_inc(s5_act, 1)
                    act.wait_ge(s5_ask, 2)
                    act.activation(s5c[:, 3, :], s5c[:, 1, :], ACT.Exp).then_inc(s5_act, 1)
                    act.wait_ge(s5_ask, 3)
                    act.activation(s5c[:, 5, :], s5c[:, 4, :], ACT.Sin).then_inc(s5_act, 1)
                    act.activation(s5c[:, 6, :], s5c[:, 4, :], ACT.Sin, scale=0.5).then_inc(s5_act, 1)
                    act.wait_ge(var_ok, 1)
                    act.activation(rstd, rstd, ACT.Sqrt).then_inc(sq_ok, 1)
                    for n in range(16):
                        act.wait_ge(bt_ps, n + 1)
                        act.copy(BT[n // 8][:, n % 8, :], ps[:, n % 2, 0:P]).then_inc(bt_ev, 1)
                    for n in range(16):
                        act.wait_ge(ct_ps, n + 1)
                        q = n % 8
                        act.activation(CT[n // 8][:, q, :], ps[:, n % 2, 0:P], ACT.Copy,
                                       scale=1.0 - 2.0 * (n // 8)).then_inc(bt_ev, 1)
                    for k in range(KD):
                        act.wait_ge(tr_ok, k + 1)
                        act.copy(hT[:, k, :], ps[:, 2 + k % 4, :]).then_inc(ev_ok, 1)

                @block.vector
                def _(dve):
                    v = Chain(dve, dch)
                    dve.wait_ge(rows_in, 9 * 16)
                    for g in range(2):
                        ins = dve.tensor_copy(rows[64:96, 1, NS * g:NS * (g + 1)],
                                              small[64:96, 804 + g:805 + g].to_broadcast([32, NS]))
                        ins.then_inc(ldt_wide, 1)
                    dve.wait_ge(rows_T, 3)
                    v(dve.tensor_copy(lam, ps[:, 1, 0:96]))
                    v(dve.tensor_copy(vecs, ps[:, 2, 0:32]))
                    dve.wait_ge(silu_e, 1)
                    v(dve.tensor_scalar(csig, csig, 1.0, None, ALU.add))
                    v(dve.reciprocal(csig, csig))
                    v(dve.tensor_tensor(csig, csig, cT, ALU.mult))
                    v(dve.tensor_copy(modT, ps[:, 0, 0:96]))
                    dve.nop().then_inc(silu_d, 1)
                    dt, lrdt, th, mag, r = (s5c[:, n, :] for n in range(5))
                    sn, hs, w0, w1, w2, cr, ci, fh, fl, ar, ai = (s5c[:, n, :] for n in range(5, 16))
                    lr, li = lam[:, 0:32], lam[:, 32:64]
                    dve.nop().then_inc(s5_ask, 1)
                    dve.wait_ge(s5_act, 1)
                    v(dve.tensor_tensor(lrdt, lr, dt, ALU.mult))
                    dve.nop().then_inc(s5_ask, 1)
                    v(dve.tensor_tensor(th, li, dt, ALU.mult))
                    v(dve.tensor_scalar(w0, th, 1.0 / TWO_PI, ROUND, ALU.mult, ALU.add))
                    v(dve.tensor_scalar(w0, w0, -ROUND, None, ALU.add))
                    v(dve.scalar_tensor_tensor(r, w0, -C1, th, ALU.mult, ALU.add))
                    v(dve.scalar_tensor_tensor(r, w0, -C2, r, ALU.mult, ALU.add))
                    v(dve.scalar_tensor_tensor(r, w0, -C3, r, ALU.mult, ALU.add))
                    v(dve.tensor_scalar(r, r, PI_LOW, -PI_LOW, ALU.min, ALU.max))
                    dve.nop().then_inc(s5_ask, 1)
                    v(dve.tensor_scalar(w1, r, 1.0 / TWO_PI, None, ALU.mult))
                    v(dve.tensor_scalar(fh, w1, ROUND13, -ROUND13, ALU.add, ALU.add))
                    v(dve.tensor_tensor(fl, w1, fh, ALU.subtract))
                    dve.wait_ge(s5_act, 4)
                    v(dve.tensor_tensor(w0, hs, hs, ALU.mult))
                    v(dve.tensor_scalar(w0, w0, -2.0, 1.0, ALU.mult, ALU.add))
                    v(dve.tensor_tensor(ar, mag, w0, ALU.mult))
                    v(dve.tensor_tensor(ai, mag, sn, ALU.mult))
                    v(dve.tensor_scalar(ar, ar, -1.0, None, ALU.add))
                    v(dve.tensor_tensor(w0, lr, lr, ALU.mult))
                    v(dve.tensor_tensor(w1, li, li, ALU.mult))
                    v(dve.tensor_tensor(w0, w0, w1, ALU.add))
                    v(dve.reciprocal(w0, w0))
                    v(dve.tensor_tensor(w1, ar, lr, ALU.mult))
                    v(dve.tensor_tensor(w2, ai, li, ALU.mult))
                    v(dve.tensor_tensor(w1, w1, w2, ALU.add))
                    v(dve.tensor_tensor(cr, w1, w0, ALU.mult))
                    v(dve.tensor_tensor(w1, ai, lr, ALU.mult))
                    v(dve.tensor_tensor(w2, ar, li, ALU.mult))
                    v(dve.tensor_tensor(w1, w1, w2, ALU.subtract))
                    v(dve.tensor_tensor(ci, w1, w0, ALU.mult))
                    dve.wait_ge(b_in, 32)
                    dve.wait_ge(cz, 2)
                    wide = [z.unsqueeze(2).broadcast_to([P, ST, GP]) for z in (cr, ci)]
                    bt = [Bt[:, n].rearrange("p (i q) -> p i q", q=GP) for n in range(4)]
                    dve.tensor_tensor(bt[0], Bn[:, 0], wide[0], ALU.mult)
                    dve.tensor_tensor(bt[1], Bn[:, 1], wide[1], ALU.mult)
                    dve.tensor_tensor(bt[2], Bn[:, 1], wide[0], ALU.mult)
                    v(dve.tensor_tensor(bt[3], Bn[:, 0], wide[1], ALU.mult))
                    for g in range(2):
                        rr = slice(64 * g, 64 * g + 64)
                        dve.tensor_tensor(Bd[rr, 0, :, GP * g:GP * (g + 1)], bt[0][rr], bt[1][rr], ALU.subtract)\
                           .then_inc(bd_ok, 1)
                        dve.tensor_tensor(Bd[rr, 1, :, GP * g:GP * (g + 1)], bt[2][rr], bt[3][rr], ALU.add)\
                           .then_inc(bd_ok, 1)
                    for t in range(TT):
                        dve.wait_ge(x_in, 16 * TT)
                        for n in range(4):
                            ins = dve.bn_stats(stats[:, n, :], resid[:, t, 512 * n:512 * (n + 1)])
                        v(ins)
                        v(dve.bn_aggr(mv[:, t, :], stats[:, :, :]))
                    v(dve.tensor_scalar(rstd, mv[:, :, 1], EPS, None, ALU.add))
                    dve.nop().then_inc(var_ok, 1)
                    dve.wait_ge(sq_ok, 1)
                    v(dve.reciprocal(rstd, rstd))
                    for t in range(TT):
                        dve.tensor_scalar(xhat[:, t, :], resid[:, t, :], mv[:, t, 0:1], rstd[:, t:t + 1],
                                          ALU.subtract, ALU.mult).then_inc(xh_ok, 1)
                    dve.wait_ge(panel_used, first["u"])
                    v(dve.tensor_tensor(modT[:, 0:32], modT[:, 0:32], ps[:, 7, 0:32], ALU.add))
                    v(dve.tensor_scalar(modT[:, 16:32], modT[:, 16:32], 1.0, None, ALU.add))
                    for k in range(KD):
                        dve.wait_ge(ev_ok, k + 1)
                        dve.tensor_scalar(hT[:, k, :], hT[:, k, :], modT[:, 16 + k:17 + k], modT[:, k:k + 1],
                                          ALU.mult, ALU.add).then_inc(h_ok, 1)

                @block.tensor
                def _(pe):
                    pe.wait_ge(const_in, 16)
                    pe.wait_ge(rows_in, 9 * 16)
                    pe.transpose(ps[:, 0, 0:112], rows[0:112, 0, :], ident[0:112, 0:112]).then_inc(rows_T, 1)
                    pe.wait_ge(ldt_wide, 2)
                    pe.transpose(ps[:, 1, 0:96], rows[0:96, 1, :], ident[0:96, 0:96]).then_inc(rows_T, 1)
                    pe.transpose(ps[:, 2, 0:32], rows[0:32, 2, :], ident[0:32, 0:32]).then_inc(rows_T, 1)
                    pe.wait_ge(silu_d, 1)
                    for g in range(first["u"]):
                        ada_panel(pe, g, 2 * g)
                        if g == 6:
                            pe.wait_ge(bd_ok, 4)
                            for n in range(16):
                                if n >= 2:
                                    pe.wait_ge(bt_ev, n - 1)
                                pe.transpose(ps[:, n % 2, 0:P], Bd[:, n // 8, 4 * (n % 8):4 * (n % 8) + 4, :]
                                             .rearrange("p a b -> p (a b)"), ident).then_inc(bt_ps, 1)
                            pe.wait_ge(c_in, 16 * 16)
                            for n in range(16):
                                pe.wait_ge(bt_ev, 15 + n)
                                pe.transpose(ps[:, n % 2, 0:P], Cd[:, n // 8, n % 8, :], ident).then_inc(ct_ps, 1)
                    pe.wait_ge(xh_ok, TT)
                    for k in range(KD):
                        if k >= 4:
                            pe.wait_ge(ev_ok, k - 3)
                        if k == 0:
                            pe.wait_ge(bt_ev, 32)
                        for t in range(TT):
                            mm = pe.transpose(ps[:, 2 + k % 4, P * t:P * (t + 1)], xhat[:, t, P * k:P * (k + 1)], ident)
                        mm.then_inc(tr_ok, 1)

        if STOP == 1:
            return finish_debug(nc, sem, out, [("hT", hT), ("BT", BT[0]), ("CT", CT[1]), ("modT", modT), ("s5c", s5c)])
        with ExitStack() as two:
            def sem2(name):
                return two.enter_context(nc.semaphore(name))

            u_ps = sem2("u_in_psum")
            u_ok = sem2("u_copied")
            turns = sem2("turns_ready")
            frac = sem2("fraction_ready")
            trig = sem2("trig_ready")
            act_in = sem2("act_chain2")
            bu_ps = sem2("bu_in_psum")
            rot_in = sem2("bu_rotated")
            summed = sem2("rotated_summed")
            scanned = sem2("state_scanned")
            rot_out = sem2("state_rotated_back")
            y_ps = sem2("y_in_psum")
            y_ok = sem2("y_ready")
            dch = sem2("dve_chain2")
            mod_rT = sem2("mod_turned")
            mod_ev = sem2("mod_rows_copied")
            mod_st = sem2("mod_rows_stored")
            gelu = sem2("gelu_done")
            mag, fh, fl = (s5c[:, n, :] for n in (3, 12, 13))
            work = [[region_b[:, (8 * b + n) * T:(8 * b + n + 1) * T] for n in range(8)] for b in (0, 1)]
            modr = two.enter_context(nc.sbuf_tensor("modr", [96, P], F32))

            with nc.Block() as block:
                @block.sync
                def _(sp):
                    load_panels(sp, first["u"] + RING, first["qkv"] + RING)
                    sp.wait_ge(mod_ev, 1)
                    sp.dma_start(mod_rows, modr[:, :]).then_inc(mod_st, 16)
                    sp.wait_ge(mod_st, 16)

                @block.tensor
                def _(pe):
                    for m in range(SC):
                        w = panel(pe, first["u"] + m // 2)
                        if m >= 2:
                            pe.wait_ge(u_ok, m - 1)
                        for k in range(KD):
                            mm = pe.matmul(ps[:, m % 2, :], w[:, k, P * (m % 2):P * (m % 2) + P], hT[:, k, :],
                                           start=(k == 0), stop=(k == KD - 1))
                            if k == KD - 1:
                                mm.then_inc(u_ps, 1)
                        if m % 2:
                            pe.wait_ge(u_ps, m + 1)
                            pe.nop().then_inc(panel_used, 1)

                    def project_in(i):
                        q, j = divmod(i, 4)
                        r = slice(32 * j, 32 * j + 32)
                        if i >= 2:
                            pe.wait_ge(rot_in, 4 * (i - 1))
                        for n in range(2):
                            mm = pe.matmul(ps[:, 2 * (i % 2) + n, :], BT[n][r, q, :], uT[r, q, :], start=True, stop=True)
                        mm.then_inc(bu_ps, 1)

                    def project_out(i):
                        q, j = divmod(i, 4)
                        w = work[i % 2]
                        pe.wait_ge(rot_out, 4 * (i + 1))
                        if j == 0 and q >= 2:
                            pe.wait_ge(y_ok, q - 1)
                        r = slice(32 * j, 32 * j + 32)
                        terms = ((0, 5), (0, 7), (1, 4), (1, 6))
                        for n, (cc, s) in enumerate(terms):
                            mm = pe.matmul(ps[r, 4 + q % 2, :], CT[cc][:, q, 32 * j:32 * j + 32], w[s],
                                           start=(n == 0), stop=(n == 3))
                        mm.then_inc(y_ps, 1)

                    pe.wait_ge(u_ok, SC)
                    project_in(0)
                    for i in range(ST):
                        if i + 1 < ST:
                            project_in(i + 1)
                        ada_panel(pe, first["ada2"] + i, 32 + 2 * i)
                        project_out(i)
                    pe.wait_ge(mod_rT, 1)
                    pe.transpose(ps[0:96, 6, 0:P], modT, ident).then_inc(mod_rT, 1)

                @block.scalar
                def _(act):
                    for m in range(SC):
                        act.wait_ge(u_ps, m + 1)
                        act.copy(uT[:, m, :], ps[:, m % 2, :]).then_inc(u_ok, 1)

                    def whole_turns(i):
                        w = work[i % 2]
                        if i >= 2:
                            act.wait_ge(trig, 4 * (i - 1))
                        act.activation(w[0], times, ACT.Copy, bias=ROUND, scale=s5c[:, 14, i:i + 1]).then_inc(act_in, 1)
                        act.wait_ge(act_in, i + 1)
                        act.activation(w[0], w[0], ACT.Copy, bias=-ROUND).then_inc(turns, 1)

                    act.wait_ge(dch, 1)
                    for i in range(ST):
                        w = work[i % 2]
                        if i == 0:
                            whole_turns(0)
                        if i + 1 < ST:
                            whole_turns(i + 1)
                        act.wait_ge(frac, i + 1)
                        act.activation(w[0], w[1], ACT.Sin, scale=TWO_PI / 2).then_inc(trig, 1)
                        if i >= 2:
                            act.wait_ge(rot_out, 4 * (i - 1))
                        act.activation(w[2], w[1], ACT.Sin, scale=TWO_PI).then_inc(trig, 1)
                        act.wait_ge(trig, 4 * i + 2)
                        act.activation(w[0], w[0], ACT.Square).then_inc(trig, 1)
                        act.wait_ge(trig, 4 * i + 3)
                        act.activation(w[3], w[0], ACT.Copy, bias=1.0, scale=-2.0).then_inc(trig, 1)
                    act.wait_ge(mod_rT, 2)
                    act.copy(modr[:, :], ps[0:96, 6, 0:P]).then_inc(mod_ev, 1)
                    act.wait_ge(y_ok, SC)
                    for q in range(SC):
                        act.activation(uT[:, q, :], uT[:, q, :], ACT.Gelu).then_inc(gelu, 1)

                @block.gpsimd
                def _(pool):
                    for i in range(ST):
                        w = work[i % 2]
                        pool.wait_ge(rot_in, 4 * (i + 1))
                        pool.tensor_tensor(w[4], w[4], w[5], ALU.add).then_inc(summed, 1)
                        pool.tensor_tensor(w[6], w[6], w[7], ALU.subtract).then_inc(summed, 1)

                @block.vector
                def _(dve):
                    v = Chain(dve, dch)
                    v(dve.tensor_tensor(s5c[:, 14, :], fh, fl, ALU.add))

                    def fraction(i):
                        w = work[i % 2]
                        dve.wait_ge(turns, i + 1)
                        v(dve.scalar_tensor_tensor(w[1], times, fh[:, i:i + 1], w[0], ALU.mult, ALU.subtract))
                        v(dve.scalar_tensor_tensor(w[1], times, fl[:, i:i + 1], w[1], ALU.mult, ALU.add))
                        dve.tensor_scalar(w[1], w[1], HALF_TURN, -HALF_TURN, ALU.min, ALU.max).then_inc(frac, 1)

                    def rotate_in(i):
                        w = work[i % 2]
                        dve.wait_ge(trig, 4 * (i + 1))
                        dve.wait_ge(bu_ps, i + 1)
                        if i >= 2:
                            dve.wait_ge(y_ps, i - 1)
                        br, bi = ps[:, 2 * (i % 2), :], ps[:, 2 * (i % 2) + 1, :]
                        for dst, tr, b in ((4, 3, br), (5, 2, bi), (6, 3, bi), (7, 2, br)):
                            dve.tensor_tensor(w[dst], w[tr], b, ALU.mult).then_inc(rot_in, 1)

                    def scan(i):
                        w = work[i % 2]
                        dve.wait_ge(summed, 2 * (i + 1))
                        m = mag[:, i:i + 1].to_broadcast([P, T])
                        for s in (4, 6):
                            dve.tensor_tensor_scan(w[s], m, w[s], 0.0, ALU.mult, ALU.add).then_inc(scanned, 1)

                    def rotate_out(i):
                        w = work[i % 2]
                        dve.wait_ge(scanned, 2 * (i + 1))
                        dve.tensor_tensor(w[5], w[3], w[4], ALU.mult).then_inc(rot_out, 1)
                        dve.scalar_tensor_tensor(w[7], w[2], -1.0, w[6], ALU.mult, ALU.mult).then_inc(rot_out, 1)
                        dve.tensor_tensor(w[4], w[2], w[4], ALU.mult).then_inc(rot_out, 1)
                        dve.tensor_tensor(w[6], w[3], w[6], ALU.mult).then_inc(rot_out, 1)

                    fraction(0)
                    rotate_in(0)
                    for i in range(ST):
                        if i + 1 < ST:
                            fraction(i + 1)
                        scan(i)
                        if i + 1 < ST:
                            rotate_in(i + 1)
                        rotate_out(i)
                        q = (i - 1) // 4
                        if i % 4 == 0 and i >= 4 or i == ST - 1:
                            q = q if i % 4 == 0 else SC - 1
                            dve.wait_ge(y_ps, 4 * (q + 1))
                            dve.scalar_tensor_tensor(uT[:, q, :], uT[:, q, :], d_c[:, q:q + 1], ps[:, 4 + q % 2, :],
                                                     ALU.mult, ALU.add).then_inc(y_ok, 1)
                    dve.wait_ge(panel_used, first["qkv"])
                    v(dve.tensor_tensor(modT[:, 32:96], modT[:, 32:96], ps[:, 7, 32:96], ALU.add))
                    v(dve.tensor_scalar(modT[:, 32:48], modT[:, 32:48], 1.0, None, ALU.add))
                    v(dve.tensor_scalar(modT[:, 64:96], modT[:, 64:96], 1.0, None, ALU.add))
                    dve.nop().then_inc(mod_rT, 1)

        if STOP == 2:
            return finish_debug(nc, sem, out, [("uT", uT), ("modT", modT)])

        with ExitStack() as three:
            def sem3(name):
                return three.enter_context(nc.semaphore(name))

            rope = three.enter_context(nc.sbuf_tensor("rope", [P, 6, T], F32))
            sinT, cosT = rope[:, 0, :], rope[:, 1, :]
            raw = [rope[:, 2 + n, :] for n in range(2)]
            prod = [rope[:, 4 + n, :] for n in range(2)]
            pos_in = sem3("positions_in")
            dch = sem3("dve_chain3")
            angle = sem3("angle_ready")
            sines = sem3("sines_ready")
            z_ps = sem3("z_in_psum")
            raw_ok = sem3("raw_copied")
            swap_ps = sem3("swapped_in_psum")
            p1_ok = sem3("cos_product")
            roped = sem3("rotary_done")
            v_ps = sem3("v_in_psum")
            v_ok = sem3("v_copied")

            with nc.Block() as block:
                @block.sync
                def _(sp):
                    sp.dma_start(prod[0].bitcast(I32), positions.broadcast_to([P, T])).then_inc(pos_in, 16)
                    load_panels(sp, first["qkv"] + RING, first["glu"] + RING)

                @block.vector
                def _(dve):
                    v = Chain(dve, dch)
                    dve.wait_ge(pos_in, 16)
                    a, w = raw[0], raw[1]
                    v(dve.tensor_copy(a, prod[0].bitcast(I32)))
                    v(dve.tensor_scalar(a, a, kc[:, K_FREQ:K_FREQ + 1], None, ALU.mult))
                    v(dve.tensor_scalar(w, a, 1.0 / TWO_PI, ROUND, ALU.mult, ALU.add))
                    v(dve.tensor_scalar(w, w, -ROUND, None, ALU.add))
                    for part in (C1, C2, C3):
                        v(dve.scalar_tensor_tensor(a, w, -part, a, ALU.mult, ALU.add))
                    dve.tensor_scalar(sinT, a, PI_LOW, -PI_LOW, ALU.min, ALU.max).then_inc(angle, 1)
                    dve.wait_ge(sines, 2)
                    v(dve.tensor_tensor(cosT, cosT, cosT, ALU.mult))
                    v(dve.tensor_scalar(cosT, cosT, -2.0, 1.0, ALU.mult, ALU.add))
                    for m in range(16):
                        dst = (qT if m < 8 else kT)[:, m % 8, :]
                        dve.wait_ge(raw_ok, m + 1)
                        if m >= 1:
                            dve.wait_ge(roped, m)
                        dve.tensor_tensor(prod[0], raw[m % 2], cosT, ALU.mult).then_inc(p1_ok, 1)
                        dve.wait_ge(swap_ps, m + 1)
                        v(dve.tensor_tensor(prod[1], ps[:, 2 + m % 2, :], sinT, ALU.mult))
                        dve.wait_ge(p1_ok, m + 1)
                        dve.tensor_tensor(dst, prod[0], prod[1], ALU.add).then_inc(roped, 1)

                @block.scalar
                def _(act):
                    act.wait_ge(angle, 1)
                    act.activation(cosT, sinT, ACT.Sin, scale=0.5).then_inc(sines, 1)
                    act.wait_ge(sines, 1)
                    act.activation(sinT, sinT, ACT.Sin).then_inc(sines, 1)
                    for m in range(16):
                        act.wait_ge(z_ps, m + 1)
                        if m >= 2:
                            act.wait_ge(p1_ok, m - 1)
                            act.wait_ge(swap_ps, m - 1)
                        if m == 0:
                            act.wait_ge(dch, 7)
                        act.copy(raw[m % 2], ps[:, m % 2, :]).then_inc(raw_ok, 1)
                    for n in range(16):
                        act.wait_ge(v_ps, n + 1)
                        pv, t = divmod(n, TT)
                        act.copy(v_tok[:, t, PC * pv:PC * (pv + 1)], ps[:, 4 + n % 2, 0:PC]).then_inc(v_ok, 1)

                @block.tensor
                def _(pe):
                    def turn_pairs(m):
                        pe.wait_ge(raw_ok, m + 1)
                        if m >= 2:
                            pe.wait_ge(roped, m - 1)
                        pe.matmul(ps[:, 2 + m % 2, :], swap, raw[m % 2], start=True, stop=True).then_inc(swap_ps, 1)

                    for m in range(16):
                        w = panel(pe, first["qkv"] + m // 2)
                        if m >= 2:
                            pe.wait_ge(raw_ok, m - 1)
                        for k in range(KD):
                            mm = pe.matmul(ps[:, m % 2, :], w[:, k, P * (m % 2):P * (m % 2) + P], hT[:, k, :],
                                           start=(k == 0), stop=(k == KD - 1))
                        mm.then_inc(z_ps, 1)
                        if m % 2:
                            pe.wait_ge(z_ps, m + 1)
                            pe.nop().then_inc(panel_used, 1)
                        if m >= 1:
                            turn_pairs(m - 1)
                    turn_pairs(15)
                    for n in range(16):
                        pv, t = divmod(n, TT)
                        w = panel(pe, first["qkv"] + 8 + pv)
                        if n >= 2:
                            pe.wait_ge(v_ok, n - 1)
                        for k in range(KD):
                            mm = pe.matmul(ps[:, 4 + n % 2, 0:PC], hT[:, k, P * t:P * (t + 1)], w[:, k, :],
                                           start=(k == 0), stop=(k == KD - 1))
                        mm.then_inc(v_ps, 1)
                        if t == TT - 1:
                            pe.wait_ge(v_ps, n + 1)
                            pe.nop().then_inc(panel_used, 1)

        if STOP == 3:
            return finish_debug(nc, sem, out, [("qT", qT), ("kT", kT), ("v", v_tok)])
        attn = region_a[:, 0:4096].rearrange("p (t d) -> p t d", t=TT)
        attnT = region_a[:, 4096:8192].rearrange("p (m t) -> p m t", m=8)
        with ExitStack() as four:
            def sem4(name):
                return four.enter_context(nc.semaphore(name))

            buf = four.enter_context(nc.sbuf_tensor("attn_buf", [P, 4, T], F32))
            prob = [buf[:, n, :] for n in range(2)]
            probT = [buf[:, 2 + n, :] for n in range(2)]
            s_ps = sem4("scores_in_psum")
            masked = sem4("scores_masked")
            negmax = sem4("negmax_ready")
            p_ok = sem4("probs_ready")
            t_ps = sem4("probsT_in_psum")
            t_ok = sem4("probsT_copied")
            o_ps = sem4("out_in_psum")
            o_ok = sem4("out_scaled")
            inv = sem4("inverse_sum")
            dch = sem4("dve_chain4")
            var_ok = sem4("attn_square_mean")
            sq_ok = sem4("attn_root")
            norm_ok = sem4("attn_normed")
            aT_ps = sem4("attnT_in_psum")
            aT_ok = sem4("attnT_copied")
            N = HEADS * TT
            mx, nm, lsum, linv = (tiny[:, 4 * n:4 * n + 4] for n in range(4))

            with nc.Block() as block:
                @block.tensor
                def _(pe):
                    def scores(n):
                        h, i = divmod(n, TT)
                        r = slice(HD * (h % 2), HD * (h % 2) + HD)
                        if n >= 2:
                            pe.wait_ge(masked, n - 1)
                        pe.matmul(ps[:, n % 2, 0:P * (i + 1)], qT[r, h // 2, P * i:P * (i + 1)],
                                  kT[r, h // 2, 0:P * (i + 1)], start=True, stop=True).then_inc(s_ps, 1)

                    def turn(n):
                        i = n % TT
                        pe.wait_ge(p_ok, n + 1)
                        if n >= 2:
                            pe.wait_ge(t_ok, n - 1)
                        for b in range(i + 1):
                            mm = pe.transpose(ps[:, 2 + n % 2, P * b:P * (b + 1)], prob[n % 2][:, P * b:P * (b + 1)], ident)
                        mm.then_inc(t_ps, 1)

                    def weigh(n):
                        h, i = divmod(n, TT)
                        pe.wait_ge(t_ok, n + 1)
                        if n >= 2:
                            pe.wait_ge(o_ok, n - 1)
                        for b in range(i + 1):
                            mm = pe.matmul(ps[:, 4 + n % 2, 0:HD], probT[n % 2][:, P * b:P * (b + 1)],
                                           v_tok[:, b, HD * h:HD * (h + 1)], start=(b == 0), stop=(b == i))
                        mm.then_inc(o_ps, 1)

                    for n in range(N + 2):
                        if n < N:
                            scores(n)
                        if 1 <= n <= N:
                            turn(n - 1)
                        if n >= 2:
                            weigh(n - 2)
                    pe.wait_ge(norm_ok, TT)
                    for m in range(8):
                        if m >= 2:
                            pe.wait_ge(aT_ok, m - 1)
                        for t in range(TT):
                            mm = pe.transpose(ps[:, 6 + m % 2, P * t:P * (t + 1)], attn[:, t, P * m:P * (m + 1)], ident)
                        mm.then_inc(aT_ps, 1)

                @block.scalar
                def _(act):
                    for n in range(N + 1):
                        if n < N:
                            w = P * (n % TT + 1)
                            act.wait_ge(negmax, n + 1)
                            if n >= 4:
                                act.wait_ge(inv, n - 3)
                            act.activation(prob[n % 2][:, 0:w], prob[n % 2][:, 0:w], ACT.Exp, bias=nm[:, n % 4:n % 4 + 1],
                                           accum_out=lsum[:, n % 4:n % 4 + 1]).then_inc(p_ok, 1)
                        if n >= 1:
                            w = P * ((n - 1) % TT + 1)
                            act.wait_ge(t_ps, n)
                            if n >= 3:
                                act.wait_ge(o_ps, n - 2)
                            act.copy(probT[(n - 1) % 2][:, 0:w], ps[:, 2 + (n - 1) % 2, 0:w]).then_inc(t_ok, 1)
                    act.wait_ge(var_ok, 1)
                    act.activation(rstd, rstd, ACT.Sqrt).then_inc(sq_ok, 1)
                    for m in range(8):
                        act.wait_ge(aT_ps, m + 1)
                        act.activation(attnT[:, m, :], ps[:, 6 + m % 2, :], ACT.Copy, scale=g_attn_c[:, m:m + 1]).then_inc(aT_ok, 1)

                @block.vector
                def _(dve):
                    v = Chain(dve, dch)

                    def mask(n):
                        i = n % TT
                        w = P * (i + 1)
                        dve.wait_ge(s_ps, n + 1)
                        if n >= 2:
                            dve.wait_ge(t_ps, n - 1)
                        if n >= 4:
                            dve.wait_ge(p_ok, n - 3)
                        dve.tensor_tensor_reduce(prob[n % 2][:, 0:w], ps[:, n % 2, 0:w],
                                                 kc[:, K_MASK + T * i:K_MASK + T * i + w], HD ** -0.5, 3.0 * NEG,
                                                 ALU.add, ALU.max, mx[:, n % 4:n % 4 + 1]).then_inc(masked, 1)
                        dve.wait_ge(masked, n + 1)
                        dve.tensor_scalar(nm[:, n % 4:n % 4 + 1], mx[:, n % 4:n % 4 + 1], -1.0, None, ALU.mult).then_inc(negmax, 1)

                    def scale(n):
                        h, i = divmod(n, TT)
                        dve.wait_ge(p_ok, n + 1)
                        dve.reciprocal(linv[:, n % 4:n % 4 + 1], lsum[:, n % 4:n % 4 + 1]).then_inc(inv, 1)
                        dve.wait_ge(inv, n + 1)
                        dve.wait_ge(o_ps, n + 1)
                        dve.tensor_scalar(attn[:, i, HD * h:HD * (h + 1)], ps[:, 4 + n % 2, 0:HD], linv[:, n % 4:n % 4 + 1],
                                          None, ALU.mult).then_inc(o_ok, 1)

                    for n in range(N + 2):
                        if n < N:
                            mask(n)
                        if n >= 2:
                            scale(n - 2)
                    dve.wait_ge(o_ok, N)
                    dve.wait_ge(t_ps, N)
                    junk = buf[:, 0:2, :].rearrange("p a b -> p (a b)")
                    for t in range(TT):
                        v(dve.tensor_tensor_reduce(junk, attn[:, t, :], attn[:, t, :], 1.0 / AW, 0.0, ALU.mult, ALU.add,
                                                   rstd[:, t:t + 1]))
                    v(dve.tensor_scalar(rstd, rstd, EPS, None, ALU.add))
                    dve.nop().then_inc(var_ok, 1)
                    dve.wait_ge(sq_ok, 1)
                    v(dve.reciprocal(rstd, rstd))
                    for t in range(TT):
                        dve.tensor_scalar(attn[:, t, :], attn[:, t, :], rstd[:, t:t + 1], None, ALU.mult).then_inc(norm_ok, 1)

        if STOP == 4:
            return finish_debug(nc, sem, out, [("attn", attn), ("attnT", attnT), ("y", uT)])

        y2T = region_c[:, 0:4096].rearrange("p (m t) -> p m t", m=SC)
        h2 = region_c[:, :].rearrange("p (t d) -> p t d", t=TT)
        h2T = hT
        row_g1, row_lg, row_lb, row_s2 = (region_b[:, D * n:D * (n + 1)] for n in range(4))
        mod_flat = mod_rows.rearrange("a b -> (a b)").rearrange("(o n) -> o n", o=1)
        with ExitStack() as five:
            def sem5(name):
                return five.enter_context(nc.semaphore(name))

            buf = five.enter_context(nc.sbuf_tensor("mix_buf", [P, 4, T], F32))
            row_h2 = buf[:, :, :].rearrange("p a b -> p (a b)")
            sg = [buf[:, n, :] for n in range(2)]
            sq = [buf[:, 2 + n, :] for n in range(2)]
            mixw = five.enter_context(nc.sbuf_tensor("mixw", [P, 2, PC], F32))
            gate_ps = sem5("gate_in_psum")
            gate_ok = sem5("gate_ready")
            y2_ok = sem5("gated")
            sq2_ok = sem5("squares_ready")
            sum_ps = sem5("square_sums")
            dch = sem5("dve_chain5")
            rows_in = sem5("rows_in5")
            shift_in = sem5("shift_in5")
            ask = sem5("root_asked")
            root = sem5("root_ready")
            mix_ps = sem5("mix_in_psum")
            mix_ok = sem5("mix_used")
            scaled = sem5("mix_scaled")
            xh_ok = sem5("xhat2_ready")
            tr_ok = sem5("h2T_in_psum")
            ev_ok = sem5("h2T_copied")

            with nc.Block() as block:
                @block.sync
                def _(sp):
                    for n, src in enumerate((mod_flat[:, 32 * P:32 * P + D], ln1_g, ln1_b, mod_flat[:, 64 * P:64 * P + D])):
                        sp.dma_start(region_b[:, D * n:D * (n + 1)], src.broadcast_to([P, D])).then_inc(rows_in, 16)
                    load_panels(sp, first["glu"] + RING, first["qp"] + RING)
                    sp.wait_ge(y2_ok, 2 * SC)
                    sp.dma_start(row_h2, mod_flat[:, 48 * P:48 * P + D].broadcast_to([P, D])).then_inc(shift_in, 16)

                @block.tensor
                def _(pe):
                    def sum_squares(m):
                        pe.wait_ge(sq2_ok, m + 1)
                        mm = pe.matmul(ps[:, 2, :], ones, sq[m % 2], start=(m == 0), stop=(m == SC - 1))
                        mm.then_inc(sum_ps, 1)

                    for m in range(SC):
                        w = panel(pe, first["glu"] + m // 2)
                        if m >= 2:
                            pe.wait_ge(gate_ok, m - 1)
                        for k in range(SC):
                            mm = pe.matmul(ps[:, m % 2, :], w[:, k, P * (m % 2):P * (m % 2) + P], uT[:, k, :],
                                           start=(k == 0), stop=(k == SC - 1))
                        mm.then_inc(gate_ps, 1)
                        if m % 2:
                            pe.wait_ge(gate_ps, m + 1)
                            pe.nop().then_inc(panel_used, 1)
                        if m >= 1:
                            sum_squares(m - 1)
                    sum_squares(SC - 1)
                    pe.wait_ge(y2_ok, 2 * SC)
                    for n in range(8 * TT):
                        pn, t = divmod(n, TT)
                        w = panel(pe, first["out"] + pn)
                        if n >= 4:
                            pe.wait_ge(scaled, n - 3)
                        for k in range(KD):
                            lhs = attnT[:, k, P * t:P * (t + 1)] if k < 8 else y2T[:, k - 8, P * t:P * (t + 1)]
                            mm = pe.matmul(ps[:, 3 + n % 4, 0:PC], lhs, w[:, k, :], start=(k == 0), stop=(k == KD - 1))
                        mm.then_inc(mix_ps, 1)
                        if t == TT - 1:
                            pe.wait_ge(mix_ps, n + 1)
                            pe.nop().then_inc(panel_used, 1)
                    pe.wait_ge(xh_ok, TT)
                    for k in range(KD):
                        if k >= 4:
                            pe.wait_ge(ev_ok, k - 3)
                        for t in range(TT):
                            mm = pe.transpose(ps[:, k % 4, P * t:P * (t + 1)], h2[:, t, P * k:P * (k + 1)], ident)
                        mm.then_inc(tr_ok, 1)

                @block.scalar
                def _(act):
                    for m in range(SC):
                        act.wait_ge(gate_ps, m + 1)
                        if m >= 2:
                            act.wait_ge(y2_ok, m - 1)
                        act.activation(sg[m % 2], ps[:, m % 2, :], ACT.Sigmoid, bias=b_glu_c[:, m:m + 1]).then_inc(gate_ok, 1)
                        act.wait_ge(y2_ok, m + 1)
                        if m >= 2:
                            act.wait_ge(sum_ps, m - 1)
                        act.activation(sq[m % 2], y2T[:, m, :], ACT.Square).then_inc(sq2_ok, 1)
                    act.wait_ge(ask, 1)
                    act.activation(sq[0], sq[0], ACT.Sqrt).then_inc(root, 1)
                    for n in range(2):
                        act.wait_ge(ask, 2 + n)
                        act.activation(rstd, rstd, ACT.Sqrt).then_inc(root, 1)
                    for k in range(KD):
                        act.wait_ge(tr_ok, k + 1)
                        act.activation(h2T[:, k, :], ps[:, k % 4, :], ACT.Identity, bias=modT[:, 48 + k:49 + k],
                                       scale=modT[:, 64 + k:65 + k]).then_inc(ev_ok, 1)

                @block.vector
                def _(dve):
                    v = Chain(dve, dch)
                    for m in range(SC):
                        dve.wait_ge(gate_ok, m + 1)
                        dve.tensor_tensor(y2T[:, m, :], uT[:, m, :], sg[m % 2], ALU.mult).then_inc(y2_ok, 1)
                    dve.wait_ge(sum_ps, SC)
                    v(dve.tensor_scalar(sq[0], ps[:, 2, :], 1.0 / SW, EPS, ALU.mult, ALU.add))
                    dve.nop().then_inc(ask, 1)
                    dve.wait_ge(root, 1)
                    v(dve.reciprocal(sq[0], sq[0]))
                    for m in range(SC):
                        dve.scalar_tensor_tensor(y2T[:, m, :], y2T[:, m, :], g_ssm_c[:, m:m + 1], sq[0], ALU.mult, ALU.mult)\
                           .then_inc(y2_ok, 1)
                    dve.wait_ge(rows_in, 64)
                    for n in range(8 * TT):
                        pn, t = divmod(n, TT)
                        cols = slice(PC * pn, PC * (pn + 1))
                        dve.wait_ge(mix_ps, n + 1)
                        if n >= 2:
                            dve.wait_ge(mix_ok, n - 1)
                        dve.tensor_tensor(mixw[:, n % 2, :], ps[:, 3 + n % 4, 0:PC], row_g1[:, cols], ALU.mult).then_inc(scaled, 1)
                        dve.wait_ge(scaled, n + 1)
                        dve.scalar_tensor_tensor(resid[:, t, cols], resid[:, t, cols], ALPHA, mixw[:, n % 2, :],
                                                 ALU.mult, ALU.add).then_inc(mix_ok, 1)
                    dve.wait_ge(mix_ok, 8 * TT)

                    def statistics(turn):
                        for t in range(TT):
                            for n in range(4):
                                ins = dve.bn_stats(stats[:, n, :], resid[:, t, 512 * n:512 * (n + 1)])
                            v(ins)
                            v(dve.bn_aggr(mv[:, t, :], stats[:, :, :]))
                        v(dve.tensor_scalar(rstd, mv[:, :, 1], EPS, None, ALU.add))
                        dve.nop().then_inc(ask, 1)
                        dve.wait_ge(root, 2 + turn)
                        v(dve.reciprocal(rstd, rstd))

                    statistics(0)
                    for t in range(TT):
                        r = resid[:, t, :]
                        v(dve.tensor_scalar(r, r, mv[:, t, 0:1], rstd[:, t:t + 1], ALU.subtract, ALU.mult))
                        v(dve.tensor_tensor(r, r, row_lg, ALU.mult))
                        v(dve.tensor_tensor(r, r, row_lb, ALU.add))
                    statistics(1)
                    for t in range(TT):
                        dve.tensor_scalar(h2[:, t, :], resid[:, t, :], mv[:, t, 0:1], rstd[:, t:t + 1],
                                          ALU.subtract, ALU.mult).then_inc(xh_ok, 1)
                    dve.wait_ge(shift_in, 16)
                    v(dve.tensor_scalar(row_s2, row_s2, 0.0, None, ALU.add))
                    dve.wait_ge(tr_ok, KD)
                    for t in range(TT):
                        v(dve.tensor_tensor(h2[:, t, :], h2[:, t, :], row_s2, ALU.mult))
                        v(dve.tensor_tensor(h2[:, t, :], h2[:, t, :], row_h2, ALU.add))

        if STOP == 5:
            return finish_debug(nc, sem, out, [("x1", resid), ("h2", h2), ("h2T", h2T), ("y2T", y2T)])

        scores = region_b[:, :].rearrange("p (t m k) -> p t m k", t=TT, m=2 * PH)
        gates = small[:, 256:256 + TT * SLOTS].rearrange("p (t s) -> p t s", t=TT)
        picks = sb("picks", [P, TT, SLOTS], U32)
        with ExitStack() as six:
            def sem6(name):
                return six.enter_context(nc.semaphore(name))

            def sb6(name, shape, dt=F32):
                return six.enter_context(nc.sbuf_tensor(name, shape, dt))

            keys = sb6("keys", [P, 2, NK])
            keysT = sb6("keysT", [P, 2, NK])
            qm = sb6("qm", [P, 2, T])
            topi = sb6("topi", [P, 2 * PH, TOPK], U32)
            free_ring = wring[:, :, :, :].rearrange("p r k c -> p (r k c)")
            cand = free_ring[:, 0:2048].rearrange("p (h a b) -> p h a b", h=PH, a=TOPK)
            top = free_ring[:, 2048:2304].rearrange("p (m s) -> p m s", m=2 * PH)
            topf = free_ring[:, 2304:2560].rearrange("p (m s) -> p m s", m=2 * PH)
            best = free_ring[:, 2560:2688].rearrange("p (h s) -> p h s", h=PH)
            besti = free_ring[:, 2688:2816].bitcast(U32).rearrange("p (h s) -> p h s", h=PH)
            half_u = free_ring[:, 2816:2944].bitcast(U32).rearrange("p (h s) -> p h s", h=PH)
            half_f = free_ring[:, 2944:3072].rearrange("p (h s) -> p h s", h=PH)
            side = [free_ring[:, 3072 + 128 * n:3200 + 128 * n].rearrange("p (h s) -> p h s", h=PH) for n in range(2)]
            gsum = free_ring[:, 3328:3336].rearrange("p (h s) -> p h s", h=PH)
            keys_in = sem6("keys_in")
            keys_ps = sem6("keysT_in_psum")
            keys_ok = sem6("keysT_copied")
            q_ps = sem6("query_in_psum")
            q_ok = sem6("query_copied")
            k_ps = sem6("key_scores_in_psum")
            k_ok = sem6("key_scores_copied")
            dch = sem6("dve_chain6")
            gate_e = sem6("gate_exp")
            gate_a = sem6("gate_asked")

            with nc.Block() as block:
                @block.sync
                def _(sp):
                    sp.dma_start(keys[:, :, :], sub_keys.rearrange("l i k c -> k (l i) c")).then_inc(keys_in, 16)
                    load_panels(sp, first["qp"] + RING, first["end"])

                @block.tensor
                def _(pe):
                    pe.wait_ge(keys_in, 16)
                    for n in range(2):
                        pe.transpose(ps[:, 4 + n, 0:NK], keys[:, n, :], ident).then_inc(keys_ps, 1)

                    def score(m):
                        pe.wait_ge(q_ok, m + 1)
                        if m >= 2:
                            pe.wait_ge(k_ok, m - 1)
                        for t in range(TT):
                            mm = pe.matmul(ps[:, 2 + m % 2, P * t:P * (t + 1)], qm[:, m % 2, P * t:P * (t + 1)],
                                           keysT[:, m % 2, :], start=True, stop=True)
                        mm.then_inc(k_ps, 1)

                    for m in range(2 * PH):
                        w = panel(pe, first["qp"] + m // 2)
                        if m >= 2:
                            pe.wait_ge(q_ok, m - 1)
                        for k in range(KD):
                            mm = pe.matmul(ps[:, m % 2, :], w[:, k, P * (m % 2):P * (m % 2) + P], h2T[:, k, :],
                                           start=(k == 0), stop=(k == KD - 1))
                        mm.then_inc(q_ps, 1)
                        if m % 2:
                            pe.wait_ge(q_ps, m + 1)
                            pe.nop().then_inc(panel_used, 1)
                        if m == 0:
                            pe.wait_ge(keys_ok, 2)
                        if m >= 1:
                            score(m - 1)
                    score(2 * PH - 1)

                @block.scalar
                def _(act):
                    for n in range(2):
                        act.wait_ge(keys_ps, n + 1)
                        act.copy(keysT[:, n, :], ps[:, 4 + n, 0:NK]).then_inc(keys_ok, 1)
                    for m in range(2 * PH + 1):
                        if m < 2 * PH:
                            act.wait_ge(q_ps, m + 1)
                            if m >= 2:
                                act.wait_ge(k_ps, m - 1)
                            act.copy(qm[:, m % 2, :], ps[:, m % 2, :]).then_inc(q_ok, 1)
                        if m >= 1:
                            act.wait_ge(k_ps, m)
                            act.copy(scores[:, :, m - 1, :], ps[:, 2 + (m - 1) % 2, :].rearrange("p (t k) -> p t k", t=TT))\
                               .then_inc(k_ok, 1)
                    for t in range(TT):
                        act.wait_ge(gate_a, t + 1)
                        act.activation(best, best, ACT.Exp).then_inc(gate_e, 1)

                @block.vector
                def _(dve):
                    v = Chain(dve, dch)
                    dve.wait_ge(k_ok, 2 * PH)
                    dve.wait_ge(panel_used, first["end"])
                    for t in range(TT):
                        for m in range(2 * PH):
                            s = scores[:, t, m, :]
                            v(dve.max(top[:, m, 0:8], s))
                            dve.max_index(topi[:, m, 0:8], top[:, m, 0:8], s).then_inc(dch, 1)
                            v.n += 1
                            v(dve.match_replace(s, top[:, m, 0:8], s, -3.0e38))
                            v(dve.max(top[:, m, 8:16], s))
                            dve.max_index(topi[:, m, 8:16], top[:, m, 8:16], s).then_inc(dch, 1)
                            v.n += 1
                        dve.wait_ge(dch, v.n)
                        v(dve.tensor_copy(topf, topi[:, :, :]))
                        pair = top.rearrange("p (h i) s -> p h i s", i=2)
                        v(dve.tensor_tensor(cand, pair[:, :, 0, :].unsqueeze(3).broadcast_to([P, PH, TOPK, TOPK]),
                                            pair[:, :, 1, :].unsqueeze(2).broadcast_to([P, PH, TOPK, TOPK]), ALU.add))
                        for h in range(PH):
                            s = cand[:, h].rearrange("p a b -> p (a b)")
                            v(dve.max(best[:, h, 0:8], s))
                            v(dve.max_index(besti[:, h, 0:8], best[:, h, 0:8], s))
                            v(dve.match_replace(s, best[:, h, 0:8], s, -3.0e38))
                            v(dve.max(best[:, h, 8:16], s))
                            v(dve.max_index(besti[:, h, 8:16], best[:, h, 8:16], s))
                        v(dve.tensor_copy(gsum, best[:, :, 0:1]))
                        v(dve.tensor_tensor(best, best, gsum.broadcast_to([P, PH, TOPK]), ALU.subtract))
                        dve.nop().then_inc(gate_a, 1)
                        for n in range(2):
                            if n == 0:
                                v(dve.tensor_scalar(half_u, besti, 4, None, ALU.logical_shift_right))
                            else:
                                v(dve.tensor_scalar(half_u, besti, 15, None, ALU.bitwise_and))
                            v(dve.tensor_copy(half_f, half_u))
                            iota = kc[:, K_IOTA:K_IOTA + TOPK].unsqueeze(1).unsqueeze(1).broadcast_to([P, PH, TOPK, TOPK])
                            v(dve.tensor_tensor(cand, half_f.unsqueeze(3).broadcast_to([P, PH, TOPK, TOPK]), iota, ALU.is_equal))
                            fi = topf.rearrange("p (h i) s -> p h i s", i=2)[:, :, n, :]
                            v(dve.tensor_tensor(cand, cand, fi.unsqueeze(2).broadcast_to([P, PH, TOPK, TOPK]), ALU.mult))
                            v(dve.tensor_reduce(side[n], cand, AX, ALU.add))
                        v(dve.scalar_tensor_tensor(side[0], side[0], float(NK), side[1], ALU.mult, ALU.add))
                        v(dve.tensor_copy(picks[:, t, :].rearrange("p (h s) -> p h s", h=PH), side[0]))
                        dve.wait_ge(gate_e, t + 1)
                        v(dve.tensor_reduce(gsum, best, AX, ALU.add))
                        v(dve.reciprocal(gsum, gsum))
                        v(dve.tensor_tensor(gates[:, t, :].rearrange("p (h s) -> p h s", h=PH), best,
                                            gsum.broadcast_to([P, PH, TOPK]), ALU.mult))

        if STOP == 6:
            return finish_debug(nc, sem, out, [("s", scores), ("gate", gates), ("ex", picks[:, :, :])])

        with ExitStack() as seven:
            def sem7(name):
                return seven.enter_context(nc.semaphore(name))

            rows = [r[:, D * n:D * (n + 1)] for r in (region_a, region_b) for n in range(4)]
            wflat = wring[:, :, :, :].rearrange("p r k c -> p (r k c)")
            acc = [wflat[:, D * n:D * (n + 1)] for n in range(2)]
            row_g2, row_lg2, row_lb2 = (wflat[:, D * (2 + n):D * (3 + n)] for n in range(3))
            outb = wflat[:, D * 5:D * 6]
            dots = seven.enter_context(nc.sbuf_tensor("dots", [P, NB], F32))
            hidden = seven.enter_context(nc.sbuf_tensor("hidden", [P, SLOTS], F32))
            coef = seven.enter_context(nc.sbuf_tensor("coef", [P, SLOTS], F32))
            index = seven.enter_context(nc.sbuf_tensor("index", [P, NB], U32))
            spare = seven.enter_context(nc.sbuf_tensor("spare", [1, 2], F32))
            spare_ok = sem7("spare_zeroed")
            row_in = [sem7(f"row_in{b}") for b in range(NB)]
            row_used = sem7("row_used")
            index_ok = sem7("index_ready")
            dot_ok = sem7("dots_kept")
            act_ok = sem7("gelu_ready7")
            hid_ok = sem7("hidden_ready")
            dch = sem7("dve_chain7")
            rows_in = sem7("rows_in7")
            ask = sem7("root_asked7")
            root = sem7("root_ready7")
            out_ok = sem7("out_ready")
            out_st = sem7("out_stored")
            ITS = SLOTS // NB
            tables = (expert_u.rearrange("l e d -> (l e) d"), expert_v.rearrange("l e d -> (l e) d"))
            out_v = out.rearrange("b (t p) d -> p (b t) d", p=P)

            with nc.Block() as block:
                @block.sync
                def _(sp):
                    for dst, src in ((row_g2, mod_flat[:, 80 * P:80 * P + D]), (row_lg2, ln2_g), (row_lb2, ln2_b)):
                        sp.dma_start(dst, src.broadcast_to([P, D])).then_inc(rows_in, 16)
                    for t in range(TT):
                        sp.wait_ge(out_ok, t + 1)
                        sp.dma_start(out_v[:, t, :], outb).then_inc(out_st, 16)
                    sp.wait_ge(out_st, 16 * TT)

                @block.gpsimd
                def _(pool):
                    pool.memset(spare[:, :], 0.0).then_inc(spare_ok, 1)
                    pool.wait_ge(spare_ok, 1)
                    for t in range(TT):
                        for side_n, table in enumerate(tables):
                            turn = (2 * t + side_n) * ITS

                            def turn_of(it):
                                for b in range(NB):
                                    done = (turn + it) * NB + b
                                    if not (isinstance(it, int) and turn + it == 0):
                                        pool.wait_ge(row_used, done - NB + 1)
                                    pool.tensor_copy(index[:, b:b + 1], picks[:, t, bass.ds(it * NB + b, 1)]).then_inc(index_ok, 1)
                                    pool.wait_ge(index_ok, done + 1)
                                    pool.tensor_tensor(spare[:, 0:1], spare[:, 1:2], spare[:, 1:2], ALU.add)
                                    pool.indirect_dma_start(rows[b], None, table,
                                                            bass.IndirectOffsetOnAxis(ap=index[:, b:b + 1], axis=0))\
                                        .then_inc(row_in[b], 16)

                            turn_of(0)
                            with pool.Fori(1, ITS) as it:
                                turn_of(it)

                @block.scalar
                def _(act):
                    for t in range(TT):
                        act.wait_ge(hid_ok, t + 1)
                        act.activation(hidden[:, :], hidden[:, :], ACT.Gelu).then_inc(act_ok, 1)
                        act.wait_ge(ask, t + 1)
                        act.activation(rstd[:, 0:1], rstd[:, 0:1], ACT.Sqrt).then_inc(root, 1)

                @block.vector
                def _(dve):
                    v = Chain(dve, dch)
                    for t in range(TT):
                        turn = 2 * t * ITS
                        with dve.Fori(0, ITS) as it:
                            for b in range(NB):
                                dve.wait_ge(row_in[b], (turn + it + 1) * 16)
                                dve.tensor_tensor_reduce(rows[b], rows[b], h2[:, t, :], 1.0, 0.0, ALU.mult, ALU.add,
                                                         dots[:, b:b + 1]).then_inc(row_used, 1)
                            dve.wait_ge(row_used, (turn + it + 1) * NB)
                            dve.tensor_copy(hidden[:, bass.ds(it * NB, NB)], dots[:, :]).then_inc(dot_ok, 1)
                            dve.wait_ge(dot_ok, it + (t * ITS + 1))
                        dve.nop().then_inc(hid_ok, 1)
                        if t >= 1:
                            dve.wait_ge(out_st, 16 * t)
                        for a in range(2):
                            v(dve.memset(acc[a], 0.0))
                        dve.wait_ge(act_ok, t + 1)
                        v(dve.tensor_tensor(coef[:, :], hidden[:, :], gates[:, t, :], ALU.mult))
                        turn = (2 * t + 1) * ITS
                        with dve.Fori(0, ITS) as it:
                            for b in range(NB):
                                dve.wait_ge(row_in[b], (turn + it + 1) * 16)
                                a = acc[b % 2]
                                dve.wait_ge(row_used, (turn + it) * NB + (b - 1))
                                dve.scalar_tensor_tensor(a, rows[b], coef[:, bass.ds(it * NB + b, 1)], a,
                                                         ALU.mult, ALU.add).then_inc(row_used, 1)
                        dve.wait_ge(row_used, (turn + ITS) * NB)
                        if t == 0:
                            dve.wait_ge(rows_in, 48)
                        a, r = acc
                        v(dve.tensor_tensor(a, acc[0], acc[1], ALU.add))
                        v(dve.tensor_tensor(a, a, row_g2, ALU.mult))
                        v(dve.scalar_tensor_tensor(a, resid[:, t, :], ALPHA, a, ALU.mult, ALU.add))
                        for n in range(4):
                            ins = dve.bn_stats(stats[:, n, :], a[:, 512 * n:512 * (n + 1)])
                        v(ins)
                        v(dve.bn_aggr(mv[:, 0, :], stats[:, :, :]))
                        v(dve.tensor_scalar(rstd[:, 0:1], mv[:, 0, 1:2], EPS, None, ALU.add))
                        dve.nop().then_inc(ask, 1)
                        dve.wait_ge(root, t + 1)
                        v(dve.reciprocal(rstd[:, 0:1], rstd[:, 0:1]))
                        v(dve.tensor_scalar(outb, a, mv[:, 0, 0:1], rstd[:, 0:1], ALU.subtract, ALU.mult))
                        v(dve.tensor_tensor(outb, outb, row_lg2, ALU.mult))
                        dve.tensor_tensor(outb, outb, row_lb2, ALU.add).then_inc(out_ok, 1)


STOP = 99
DEBUG = {}


def finish_debug(nc, sem, out, items):
    done = sem("dbg")
    with nc.Block() as block:
        @block.sync
        def _(sp):
            for n, (name, ap) in enumerate(items):
                o = nc.dram_tensor("dbg_" + name, list(ap.shape), ap.dtype, kind="ExternalOutput").ap()
                sp.dma_start(o, ap).then_inc(done, 16)
            sp.wait_ge(done, 16 * len(items))


_INS = ['x', 'c', 'positions', 'w_ada', 'b_ada', 'w_in', 'lam_re', 'lam_im', 'log_dt', 'ssm_b_re', 'ssm_b_im',
        'ssm_c_re', 'ssm_c_im', 'ssm_d', 'w_glu', 'b_glu', 'g_attn', 'g_ssm', 'w_out', 'ln1_g', 'ln1_b', 'w_qp',
        'sub_keys', 'expert_u', 'expert_v', 'ln2_g', 'ln2_b']


def kernel(**inputs):
    import concourse.bacc as _bacc
    from concourse.bass_utils import run_bass_kernel_spmd as _run

    nc = _bacc.Bacc("TRN2", target_bir_lowering=False, num_devices=1)
    arrays, args = {}, []
    for name in _INS:
        a = np.ascontiguousarray(inputs[name])
        arrays[f"in_{name}"] = a
        args.append(nc.dram_tensor(f"in_{name}", a.shape, mybir.dt.from_np(a.dtype), kind="ExternalInput").ap())
    arrays["in_constants"] = constants()
    consts = nc.dram_tensor("in_constants", (P, K_END), F32, kind="ExternalInput").ap()
    mod_rows = nc.dram_tensor("mod_rows", (96, P), F32, kind="Internal").ap()
    out = nc.dram_tensor("out_x", (1, T, D), F32, kind="ExternalOutput").ap()
    hybrid_layer(nc, consts, *args, mod_rows, out)
    r = _run(nc, [arrays], core_ids=[0])
    return r.results[0]["out_x"]
```

```python
from contextlib import ExitStack

import numpy as np

import concourse.bass as bass
from concourse import mybir

F32 = mybir.dt.float32
I32 = mybir.dt.int32
U32 = mybir.dt.uint32
ALU = mybir.AluOpType
ACT = mybir.ActivationFunctionType
AX = mybir.AxisListType.X

P = 128
T = 512
TT = T // P
D = 2048
KD = D // P
HEADS, HD = 16, 64
AW = HEADS * HD
SW = D - AW
G, GP, NS = 64, 16, 64
ST = G * NS // P
SC = SW // P
PH, TOPK, NK = 8, 16, 128
SLOTS = PH * TOPK
EPS = 1e-5
ALPHA = 2.0 ** 0.25
NEG = -1e30
TWO_PI = 6.283185307179586
C1 = 6.28125
C2 = 0.0019350051879882812
C3 = TWO_PI - C1 - C2
PI_LOW = 3.1415925
HALF_TURN = 0.49999997
ROUND = 12582912.0
ROUND13 = 1536.0
PC = 256
RING = 3
NB = 8
RINGS = (4, NB, NB, NB)

K_ID = 0
K_MASK = K_ID + P
K_SWAP = K_MASK + TT * T
K_TIME = K_SWAP + P
K_FREQ = K_TIME + T
K_IOTA = K_FREQ + 1
K_ONE = K_IOTA + TOPK
K_END = K_ONE + P


def constants():
    a = np.zeros((P, K_END), np.float32)
    a[:, K_ID:K_ID + P] = np.eye(P)
    t = np.arange(T)[:, None]
    s = np.arange(T)[None, :]
    d = t - s
    count = ((d >= 0) & (d <= 128)).astype(np.int64)
    count += (d >= 0) & (d % 4 == 0)
    count += (d >= 0) & (d % 16 == 0)
    bias = np.where(count > 0, HD ** 0.5 * np.log(np.maximum(count, 1)), NEG).astype(np.float32)
    for i in range(TT):
        a[:, K_MASK + i * T:K_MASK + (i + 1) * T] = bias[i * P:(i + 1) * P]
    for m in range(P):
        half = HD // 2
        if m % HD < half:
            a[m + half, K_SWAP + m] = -1.0
        else:
            a[m - half, K_SWAP + m] = 1.0
    a[:, K_TIME:K_TIME + T] = np.arange(T)
    half = HD // 2
    a[:, K_FREQ] = np.power(np.float32(10000.0), -np.arange(half, dtype=np.float32) / np.float32(half))[np.arange(P) % half]
    a[:, K_IOTA:K_IOTA + TOPK] = np.arange(TOPK)
    a[:, K_ONE:K_ONE + P] = 1.0
    return a


def hybrid_layer(nc, consts, x, c, positions, w_ada, b_ada, w_in, lam_re, lam_im, log_dt, ssm_b_re, ssm_b_im,
                 ssm_c_re, ssm_c_im, ssm_d, w_glu, b_glu, g_attn, g_ssm, w_out, ln1_g, ln1_b, w_qp, sub_keys,
                 expert_u, expert_v, ln2_g, ln2_b, mod_rows, x1_rows, h2_rows, out):
    ctx = ExitStack()

    def sb(name, shape, dt=F32):
        return ctx.enter_context(nc.sbuf_tensor(name, shape, dt))

    def sem(name):
        return ctx.enter_context(nc.semaphore(name))

    with ctx:
        kc = sb("kc", [P, K_END])
        ident = kc[:, K_ID:K_ID + P]
        ones = kc[:, K_ONE:K_ONE + P]
        swap = kc[:, K_SWAP:K_SWAP + P]
        times = kc[:, K_TIME:K_TIME + T]
        small = sb("small", [P, 1024])
        resid = sb("resid", [P, TT, D])
        area = sb("area", [P, 16384])
        region_a = area[:, 0:8192]
        region_c = area[:, 8192:16384]
        ada_acc = sb("ada_acc", [P, 2, PC])
        wring = sb("wring", [P, RING, KD, PC])
        region_b = sb("region_b", [P, 8192])
        ps = ctx.enter_context(nc.psum_tensor("ps", [P, 8, 512], F32))

        modT = small[:, 0:96]
        cT = small[:, 96:112]
        csig = small[:, 112:128]
        vecs = small[:, 128:160]
        g_attn_c, g_ssm_c, b_glu_c, d_c = (vecs[:, 8 * n:8 * n + 8] for n in range(4))
        lam = small[:, 160:256]
        s5c = small[:, 256:256 + 32 * 16].rearrange("p (n s) -> p n s", s=32)
        stats = small[:, 768:792].rearrange("p (n s) -> p n s", s=6)
        mv = small[:, 792:800].rearrange("p (n s) -> p n s", s=2)
        rstd = small[:, 800:804]
        tiny = small[:, 804:820]

        hT = region_a[:, :].rearrange("p (k t) -> p k t", k=KD)
        xhat = region_b[:, :].rearrange("p (t d) -> p t d", t=TT)
        v_tok = region_c[:, 0:4096].rearrange("p (t d) -> p t d", t=TT)
        uT = region_c[:, 4096:8192].rearrange("p (m t) -> p m t", m=SC)

        def panels_of(w, cols, rows=KD):
            v = w.rearrange("(k p) n -> p k n", p=P)
            return [(v[:, :, n:n + PC], rows) for n in cols]

        ada = w_ada.rearrange("l a b -> (l a) b")
        win = w_in.rearrange("l a b -> (l a) b")
        ADA1 = panels_of(ada, range(0, 2 * D, PC))
        UP = panels_of(win, range(3 * AW, 3 * AW + SW, PC))
        ADA2 = panels_of(ada, range(2 * D, 6 * D, PC))
        QKV = panels_of(win, range(0, 3 * AW, PC))
        GLU = panels_of(w_glu.rearrange("l a b -> (l a) b"), range(0, SW, PC), SC)
        OUT = panels_of(w_out.rearrange("l a b -> (l a) b"), range(0, D, PC))
        QP = panels_of(w_qp.rearrange("l a b -> (l a) b"), range(0, PH * 2 * P, PC))
        order = [("ada", n) for n in range(len(ADA1))]
        for n in range(len(UP)):
            order += [("u", n), ("ada", 16 + n)]
        for n in range(8):
            order += [("qkv", n), ("ada", 20 + n)]
        for n in range(4):
            order += [("qkv", 8 + n), ("ada", 28 + n)]
        order += [("ada", n) for n in range(32, 48)]
        order += [("glu", n) for n in range(len(GLU))]
        for grp in range(2):
            order += [("out", 8 * grp + n) for n in range(8)]
            order += [("rows", 2 * grp), ("rows", 2 * grp + 1)]
            order += [("qp", 8 * grp + n) for n in range(8)]
        mod_flat = mod_rows.rearrange("a b -> (a b)").rearrange("(o n) -> o n", o=1)
        ROWS = [((ln1_g, ln1_b), 0), ((mod_flat[:, 48 * P:48 * P + 2 * D],), 0)]
        lots = {"ada": ADA1 + ADA2, "u": UP, "qkv": QKV, "glu": GLU, "out": OUT + OUT, "qp": QP + QP, "rows": ROWS + ROWS}
        panels = [lots[kind][n] for kind, n in order]
        where = {key: g for g, key in enumerate(order)}
        first = {"u": where["u", 0], "glu": where["glu", 0], "out": where["out", 0], "qp": where["qp", 0],
                 "ada3": where["ada", 32], "end": len(order)}
        by_pe = (2, 5, 8, 11, 13, 15)
        ada_sum = sem("ada_summed")
        panel_in = [sem(f"panel_in{s}") for s in range(RING)]
        panel_used = sem("panel_used")

        def load_panels(sp, lo, hi):
            for g in range(lo, min(hi, len(panels))):
                src, rows = panels[g]
                if g >= RING:
                    sp.wait_ge(panel_used, g - RING + 1)
                if rows:
                    sp.dma_start(wring[:, g % RING, 0:rows, :], src).then_inc(panel_in[g % RING], 16)
                else:
                    flat = wring[:, g % RING, :, :].rearrange("p k c -> p (k c)")
                    width = 2 * D // len(src)
                    for n, row in enumerate(src):
                        sp.dma_start(flat[:, width * n:width * (n + 1)], row.broadcast_to([P, width]))\
                            .then_inc(panel_in[g % RING], 16)

        def panel(eng, g):
            loads = sum(1 if panels[m][1] else len(panels[m][0]) for m in range(g % RING, g + 1, RING))
            eng.wait_ge(panel_in[g % RING], 16 * loads)
            return wring[:, g % RING, :, :]

        def ada_columns(pe, n):
            g = where["ada", n]
            w = panel(pe, g)
            if n in by_pe:
                for c2 in range(2):
                    for k in range(KD):
                        mm = pe.matmul(ps[:, 7, 2 * n + c2:2 * n + c2 + 1], w[:, k, c2 * P:(c2 + 1) * P], csig[:, k:k + 1],
                                       start=False, stop=(k == KD - 1), skip_group_check=True)
            else:
                pe.wait_ge(ada_sum, len([m for m in range(n + 1) if m not in by_pe]))
                for c2 in range(2):
                    mm = pe.matmul(ps[:, 7, 2 * n + c2:2 * n + c2 + 1], w[:, 0, c2 * P:(c2 + 1) * P], ones[:, 0:1],
                                   start=(n == 0 and c2 == 0), stop=True, skip_group_check=True)
            mm.then_inc(panel_used, 1)

        def ada_sums(dve, v, n):
            w = panel(dve, where["ada", n])
            before = len([m for m in range(n) if m not in by_pe])
            if before:
                dve.wait_ge(ada_sum, before)
            for k in range(KD):
                if k < 2:
                    ins = dve.tensor_scalar(ada_acc[:, k, :], w[:, k, :], csig[:, k:k + 1], None, ALU.mult)
                else:
                    dve.wait_ge(v.s, v.n - 1)
                    ins = dve.scalar_tensor_tensor(ada_acc[:, k % 2, :], w[:, k, :], csig[:, k:k + 1],
                                                   ada_acc[:, k % 2, :], ALU.mult, ALU.add)
                ins.then_inc(v.s, 1)
                v.n += 1
            dve.wait_ge(v.s, v.n)
            dve.tensor_tensor(w[:, 0, :], ada_acc[:, 0, :], ada_acc[:, 1, :], ALU.add).then_inc(ada_sum, 1)

        class Chain:

            def __init__(self, eng, s):
                self.eng, self.s, self.n = eng, s, 0

            def __call__(self, ins):
                ins.then_inc(self.s, 1)
                self.n += 1
                self.eng.wait_ge(self.s, self.n)
                return self.n

        x_v = x.rearrange("b (t p) d -> p (b t) d", p=P)
        BT = [region_c[:, 1024 * n:1024 * (n + 1)].rearrange("p (q s) -> p q s", q=SC) for n in (0, 1)]
        CT = [region_c[:, 1024 * n:1024 * (n + 1)].rearrange("p (q s) -> p q s", q=SC) for n in (2, 3)]

        with ExitStack() as one:
            def sem1(name):
                return one.enter_context(nc.semaphore(name))

            rows_in = sem1("rows_in")
            const_in = sem1("const_in")
            x_in = sem1("x_in")
            b_in = sem1("b_in")
            c_in = sem1("c_in")
            cz = sem1("cd_zeroed")
            ldt_wide = sem1("ldt_wide")
            rows_T = sem1("rows_T")
            rows_c = sem1("rows_copied")
            silu_e = sem1("silu_exp")
            silu_d = sem1("silu_done")
            dch = sem1("dve_chain1")
            var_ok = sem1("var_ready")
            sq_ok = sem1("sqrt_ready")
            xh_ok = sem1("xhat_ready")
            tr_ok = sem1("xT_in_psum")
            ev_ok = sem1("xT_copied")
            s5_ask = sem1("s5_asks_act")
            s5_act = sem1("s5_act_done")
            bd_ok = sem1("bd_ready")
            bt_ps = sem1("bt_in_psum")
            bt_ev = sem1("bt_copied")
            ct_ps = sem1("ct_in_psum")
            h_ok = sem1("hT_ready")
            rows = one.enter_context(nc.sbuf_tensor("rows", [P, 3, P], F32))
            Bn = one.enter_context(nc.sbuf_tensor("Bn", [P, 2, ST, GP], F32))
            Bt = region_a[:, 0:2048].rearrange("p (n f) -> p n f", n=4)
            Bd = region_a[:, 2048:4096].rearrange("p (n i e) -> p n i e", n=2, e=2 * GP)
            Cd = region_a[:, 4096:6144].rearrange("p (n q e) -> p n q e", n=2, e=P)

            with nc.Block() as block:
                @block.sync
                def _(sp):
                    sp.dma_start(kc[:, :], consts).then_inc(const_in, 16)
                    sp.dma_start(rows[0:96, 0, :], b_ada.rearrange("l (j p) -> (l j) p", p=P)).then_inc(rows_in, 16)
                    sp.dma_start(rows[96:112, 0, :], c.rearrange("b (j p) -> (b j) p", p=P)).then_inc(rows_in, 16)
                    sp.dma_start(rows[0:32, 1, :], lam_re.rearrange("l (i g) n -> (l i) (g n)", g=2)).then_inc(rows_in, 16)
                    sp.dma_start(rows[32:64, 1, :], lam_im.rearrange("l (i g) n -> (l i) (g n)", g=2)).then_inc(rows_in, 16)
                    sp.dma_start(small[64:96, 804:806], log_dt.rearrange("l (i g) -> (l i) g", g=2)).then_inc(rows_in, 16)
                    for n, vec in enumerate((g_attn, g_ssm, b_glu)):
                        sp.dma_start(rows[8 * n:8 * n + 8, 2, :], vec.rearrange("l (j p) -> (l j) p", p=P)).then_inc(rows_in, 16)
                    sp.dma_start(rows[24:32, 2, :], ssm_d.rearrange("l (j g) q -> (l j) (g q)", j=8)).then_inc(rows_in, 16)
                    load_panels(sp, 0, 1)
                    for t in range(TT):
                        sp.dma_start(resid[:, t, :], x_v[:, t, :]).then_inc(x_in, 16)
                    for n, b in enumerate((ssm_b_re, ssm_b_im)):
                        sp.dma_start(Bn[:, n], b.rearrange("l (i g) n q -> (g n) (l i) q", g=2)).then_inc(b_in, 16)
                    load_panels(sp, 1, 6)
                    sp.wait_ge(cz, 1)
                    for n, cc in enumerate((ssm_c_re, ssm_c_im)):
                        for r in range(8):
                            sp.dma_start(Cd[GP * r:GP * (r + 1), n, :, NS * (r % 2):NS * (r % 2) + NS],
                                         cc.rearrange("l (q r) e n -> r e (l q) n", r=8)[r]).then_inc(c_in, 16)
                    load_panels(sp, 6, first["u"] + RING)

                @block.gpsimd
                def _(pool):
                    pool.memset(Cd[:, :, :, :], 0.0).then_inc(cz, 1)
                    pool.memset(Bd[:, :, :, :], 0.0).then_inc(cz, 1)

                @block.scalar
                def _(act):
                    act.wait_ge(rows_T, 1)
                    act.copy(cT, ps[:, 0, 96:112]).then_inc(rows_c, 1)
                    act.wait_ge(rows_c, 1)
                    act.activation(csig, cT, ACT.Exp, scale=-1.0).then_inc(silu_e, 1)
                    act.wait_ge(s5_ask, 1)
                    act.activation(s5c[:, 0, :], lam[:, 64:96], ACT.Exp).then_inc(s5_act, 1)
                    act.wait_ge(s5_ask, 2)
                    act.activation(s5c[:, 3, :], s5c[:, 1, :], ACT.Exp).then_inc(s5_act, 1)
                    act.wait_ge(s5_ask, 3)
                    act.activation(s5c[:, 5, :], s5c[:, 4, :], ACT.Sin).then_inc(s5_act, 1)
                    act.activation(s5c[:, 6, :], s5c[:, 4, :], ACT.Sin, scale=0.5).then_inc(s5_act, 1)
                    act.wait_ge(var_ok, 1)
                    act.activation(rstd, rstd, ACT.Sqrt).then_inc(sq_ok, 1)
                    for n in range(16):
                        act.wait_ge(bt_ps, n + 1)
                        act.copy(BT[n // 8][:, n % 8, :], ps[:, n % 2, 0:P]).then_inc(bt_ev, 1)
                    for n in range(16):
                        act.wait_ge(ct_ps, n + 1)
                        q = n % 8
                        act.activation(CT[n // 8][:, q, :], ps[:, n % 2, 0:P], ACT.Copy,
                                       scale=1.0 - 2.0 * (n // 8)).then_inc(bt_ev, 1)
                    for k in range(KD):
                        act.wait_ge(tr_ok, k + 1)
                        act.copy(hT[:, k, :], ps[:, 2 + k % 4, :]).then_inc(ev_ok, 1)

                @block.vector
                def _(dve):
                    v = Chain(dve, dch)
                    dve.wait_ge(rows_in, 9 * 16)
                    for g in range(2):
                        ins = dve.tensor_copy(rows[64:96, 1, NS * g:NS * (g + 1)],
                                              small[64:96, 804 + g:805 + g].to_broadcast([32, NS]))
                        ins.then_inc(ldt_wide, 1)
                    dve.wait_ge(rows_T, 3)
                    v(dve.tensor_copy(lam, ps[:, 1, 0:96]))
                    v(dve.tensor_copy(vecs, ps[:, 2, 0:32]))
                    dve.wait_ge(silu_e, 1)
                    v(dve.tensor_scalar(csig, csig, 1.0, None, ALU.add))
                    v(dve.reciprocal(csig, csig))
                    v(dve.tensor_tensor(csig, csig, cT, ALU.mult))
                    v(dve.tensor_copy(modT, ps[:, 0, 0:96]))
                    dve.nop().then_inc(silu_d, 1)
                    ada_sums(dve, v, 0)
                    ada_sums(dve, v, 1)
                    dt, lrdt, th, mag, r = (s5c[:, n, :] for n in range(5))
                    sn, hs, w0, w1, w2, cr, ci, fh, fl, ar, ai = (s5c[:, n, :] for n in range(5, 16))
                    lr, li = lam[:, 0:32], lam[:, 32:64]
                    dve.nop().then_inc(s5_ask, 1)
                    dve.wait_ge(s5_act, 1)
                    v(dve.tensor_tensor(lrdt, lr, dt, ALU.mult))
                    dve.nop().then_inc(s5_ask, 1)
                    v(dve.tensor_tensor(th, li, dt, ALU.mult))
                    v(dve.tensor_scalar(w0, th, 1.0 / TWO_PI, ROUND, ALU.mult, ALU.add))
                    v(dve.tensor_scalar(w0, w0, -ROUND, None, ALU.add))
                    v(dve.scalar_tensor_tensor(r, w0, -C1, th, ALU.mult, ALU.add))
                    v(dve.scalar_tensor_tensor(r, w0, -C2, r, ALU.mult, ALU.add))
                    v(dve.scalar_tensor_tensor(r, w0, -C3, r, ALU.mult, ALU.add))
                    v(dve.tensor_scalar(r, r, PI_LOW, -PI_LOW, ALU.min, ALU.max))
                    dve.nop().then_inc(s5_ask, 1)
                    v(dve.tensor_scalar(w1, r, 1.0 / TWO_PI, None, ALU.mult))
                    v(dve.tensor_scalar(fh, w1, ROUND13, -ROUND13, ALU.add, ALU.add))
                    v(dve.tensor_tensor(fl, w1, fh, ALU.subtract))
                    dve.wait_ge(s5_act, 4)
                    v(dve.tensor_tensor(w0, hs, hs, ALU.mult))
                    v(dve.tensor_scalar(w0, w0, -2.0, 1.0, ALU.mult, ALU.add))
                    v(dve.tensor_tensor(ar, mag, w0, ALU.mult))
                    v(dve.tensor_tensor(ai, mag, sn, ALU.mult))
                    v(dve.tensor_scalar(ar, ar, -1.0, None, ALU.add))
                    v(dve.tensor_tensor(w0, lr, lr, ALU.mult))
                    v(dve.tensor_tensor(w1, li, li, ALU.mult))
                    v(dve.tensor_tensor(w0, w0, w1, ALU.add))
                    v(dve.reciprocal(w0, w0))
                    v(dve.tensor_tensor(w1, ar, lr, ALU.mult))
                    v(dve.tensor_tensor(w2, ai, li, ALU.mult))
                    v(dve.tensor_tensor(w1, w1, w2, ALU.add))
                    v(dve.tensor_tensor(cr, w1, w0, ALU.mult))
                    v(dve.tensor_tensor(w1, ai, lr, ALU.mult))
                    v(dve.tensor_tensor(w2, ar, li, ALU.mult))
                    v(dve.tensor_tensor(w1, w1, w2, ALU.subtract))
                    v(dve.tensor_tensor(ci, w1, w0, ALU.mult))
                    ada_sums(dve, v, 3)
                    ada_sums(dve, v, 4)
                    dve.wait_ge(b_in, 32)
                    dve.wait_ge(cz, 2)
                    wide = [z.unsqueeze(2).broadcast_to([P, ST, GP]) for z in (cr, ci)]
                    bt = [Bt[:, n].rearrange("p (i q) -> p i q", q=GP) for n in range(4)]
                    dve.tensor_tensor(bt[0], Bn[:, 0], wide[0], ALU.mult)
                    dve.tensor_tensor(bt[1], Bn[:, 1], wide[1], ALU.mult)
                    dve.tensor_tensor(bt[2], Bn[:, 1], wide[0], ALU.mult)
                    v(dve.tensor_tensor(bt[3], Bn[:, 0], wide[1], ALU.mult))
                    for g in range(2):
                        rr = slice(64 * g, 64 * g + 64)
                        dve.tensor_tensor(Bd[rr, 0, :, GP * g:GP * (g + 1)], bt[0][rr], bt[1][rr], ALU.subtract)\
                           .then_inc(bd_ok, 1)
                        dve.tensor_tensor(Bd[rr, 1, :, GP * g:GP * (g + 1)], bt[2][rr], bt[3][rr], ALU.add)\
                           .then_inc(bd_ok, 1)
                    for t in range(TT):
                        dve.wait_ge(x_in, 16 * TT)
                        for n in range(4):
                            ins = dve.bn_stats(stats[:, n, :], resid[:, t, 512 * n:512 * (n + 1)])
                        v(ins)
                        v(dve.bn_aggr(mv[:, t, :], stats[:, :, :]))
                        ada_sums(dve, v, (6, 7, 9, 10)[t])
                    v(dve.tensor_scalar(rstd, mv[:, :, 1], EPS, None, ALU.add))
                    dve.nop().then_inc(var_ok, 1)
                    dve.wait_ge(sq_ok, 1)
                    v(dve.reciprocal(rstd, rstd))
                    for t in range(TT):
                        dve.tensor_scalar(xhat[:, t, :], resid[:, t, :], mv[:, t, 0:1], rstd[:, t:t + 1],
                                          ALU.subtract, ALU.mult).then_inc(xh_ok, 1)
                    ada_sums(dve, v, 12)
                    ada_sums(dve, v, 14)
                    dve.wait_ge(panel_used, first["u"])
                    v(dve.tensor_tensor(modT[:, 0:32], modT[:, 0:32], ps[:, 7, 0:32], ALU.add))
                    v(dve.tensor_scalar(modT[:, 16:32], modT[:, 16:32], 1.0, None, ALU.add))
                    for k in range(KD):
                        dve.wait_ge(ev_ok, k + 1)
                        dve.tensor_scalar(hT[:, k, :], hT[:, k, :], modT[:, 16 + k:17 + k], modT[:, k:k + 1],
                                          ALU.mult, ALU.add).then_inc(h_ok, 1)

                @block.tensor
                def _(pe):
                    pe.wait_ge(const_in, 16)
                    pe.wait_ge(rows_in, 9 * 16)
                    pe.transpose(ps[:, 0, 0:112], rows[0:112, 0, :], ident[0:112, 0:112]).then_inc(rows_T, 1)
                    pe.wait_ge(ldt_wide, 2)
                    pe.transpose(ps[:, 1, 0:96], rows[0:96, 1, :], ident[0:96, 0:96]).then_inc(rows_T, 1)
                    pe.transpose(ps[:, 2, 0:32], rows[0:32, 2, :], ident[0:32, 0:32]).then_inc(rows_T, 1)
                    pe.wait_ge(silu_d, 1)
                    for g in range(first["u"]):
                        ada_columns(pe, g)
                        if g == 8:
                            pe.wait_ge(bd_ok, 4)
                            for n in range(16):
                                if n >= 2:
                                    pe.wait_ge(bt_ev, n - 1)
                                pe.transpose(ps[:, n % 2, 0:P], Bd[:, n // 8, 4 * (n % 8):4 * (n % 8) + 4, :]
                                             .rearrange("p a b -> p (a b)"), ident).then_inc(bt_ps, 1)
                            pe.wait_ge(c_in, 16 * 16)
                            for n in range(16):
                                pe.wait_ge(bt_ev, 15 + n)
                                pe.transpose(ps[:, n % 2, 0:P], Cd[:, n // 8, n % 8, :], ident).then_inc(ct_ps, 1)
                    pe.wait_ge(xh_ok, TT)
                    for k in range(KD):
                        if k >= 4:
                            pe.wait_ge(ev_ok, k - 3)
                        if k == 0:
                            pe.wait_ge(bt_ev, 32)
                        for t in range(TT):
                            mm = pe.transpose(ps[:, 2 + k % 4, P * t:P * (t + 1)], xhat[:, t, P * k:P * (k + 1)], ident)
                        mm.then_inc(tr_ok, 1)

        qT = resid[:, 0:2, :].rearrange("p a (m t) -> p (a m) t", t=T)
        kT = resid[:, 2:4, :].rearrange("p a (m t) -> p (a m) t", t=T)
        with ExitStack() as two:
            def sem2(name):
                return two.enter_context(nc.semaphore(name))

            u_ps = sem2("u_in_psum")
            u_ok = sem2("u_copied")
            turns = sem2("turns_ready")
            frac = sem2("fraction_ready")
            trig = sem2("trig_ready")
            act_in = sem2("act_chain2")
            bu_ps = sem2("bu_in_psum")
            rot_in = sem2("bu_rotated")
            summed = sem2("rotated_summed")
            scanned = sem2("state_scanned")
            rot_out = sem2("state_times_cos_and_sin")
            rot_pool = sem2("state_times_sin_and_cos")
            state = sem2("state_rotated_back")
            y_ps = sem2("y_in_psum")
            y_ok = sem2("y_ready")
            dch = sem2("dve_chain2")
            gelu = sem2("gelu_done")
            pos_in = sem2("positions_in")
            angle = sem2("angle_ready")
            sines = sem2("sines_ready")
            z_ps = sem2("z_in_psum")
            raw_ok = sem2("raw_copied")
            swap_ps = sem2("swapped_in_psum")
            roped = sem2("rotary_done")
            v_ps = sem2("v_in_psum")
            v_ok = sem2("v_copied")
            mag, fh, fl = (s5c[:, n, :] for n in (3, 12, 13))
            work = [[region_b[:, (8 * b + n) * T:(8 * b + n + 1) * T] for n in range(8)] for b in (0, 1)]
            rope = two.enter_context(nc.sbuf_tensor("rope", [P, 5, T], F32))
            sinT, cosT = rope[:, 0, :], rope[:, 1, :]
            raw = [rope[:, 2 + n, :] for n in range(2)]
            prod = rope[:, 4, :]

            with nc.Block() as block:
                @block.sync
                def _(sp):
                    sp.dma_start(prod.bitcast(I32), positions.broadcast_to([P, T])).then_inc(pos_in, 16)
                    load_panels(sp, first["u"] + RING, first["ada3"] + RING)

                @block.tensor
                def _(pe):
                    for m in range(SC):
                        w = panel(pe, where["u", m // 2])
                        if m >= 2:
                            pe.wait_ge(u_ok, m - 1)
                        for k in range(KD):
                            mm = pe.matmul(ps[:, m % 2, :], w[:, k, P * (m % 2):P * (m % 2) + P], hT[:, k, :],
                                           start=(k == 0), stop=(k == KD - 1))
                        mm.then_inc(u_ps, 1)
                        if m % 2:
                            pe.wait_ge(u_ps, m + 1)
                            pe.nop().then_inc(panel_used, 1)
                            ada_columns(pe, 16 + m // 2)

                    def project_in(i):
                        q, j = divmod(i, 4)
                        r = slice(32 * j, 32 * j + 32)
                        if i >= 2:
                            pe.wait_ge(rot_in, 4 * (i - 1))
                        for n in range(2):
                            mm = pe.matmul(ps[:, 2 * (i % 2) + n, :], BT[n][r, q, :], uT[r, q, :], start=True, stop=True)
                        mm.then_inc(bu_ps, 1)

                    def project_out(i):
                        q, j = divmod(i, 4)
                        w = work[i % 2]
                        pe.wait_ge(state, 2 * (i + 1))
                        if j == 0 and q >= 1:
                            pe.wait_ge(y_ok, q)
                        r = slice(32 * j, 32 * j + 32)
                        for n, s in enumerate((5, 4)):
                            mm = pe.matmul(ps[r, 4, :], CT[n][:, q, 32 * j:32 * j + 32], w[s], start=(n == 0), stop=(n == 1))
                        mm.then_inc(y_ps, 1)

                    def project_qk(m, half):
                        w = panel(pe, where["qkv", m // 2])
                        if half == 0 and m >= 1:
                            pe.wait_ge(raw_ok, m)
                        for k in range(8 * half, 8 * half + 8):
                            mm = pe.matmul(ps[:, 5, :], w[:, k, P * (m % 2):P * (m % 2) + P], hT[:, k, :],
                                           start=(k == 0), stop=(k == KD - 1))
                        if half:
                            mm.then_inc(z_ps, 1)

                    def turn_pairs(m):
                        pe.wait_ge(raw_ok, m + 1)
                        if m >= 1:
                            pe.wait_ge(roped, m)
                        pe.matmul(ps[:, 6, :], swap, raw[m % 2], start=True, stop=True).then_inc(swap_ps, 1)

                    pe.wait_ge(u_ok, SC)
                    project_in(0)
                    for i in range(ST):
                        m = i // 2
                        if i + 1 < ST:
                            project_in(i + 1)
                        project_qk(m, i % 2)
                        if i >= 1:
                            project_out(i - 1)
                        if i % 2 == 0 and m >= 1:
                            turn_pairs(m - 1)
                        if i % 4 == 3:
                            pe.wait_ge(z_ps, m + 1)
                            pe.nop().then_inc(panel_used, 1)
                            ada_columns(pe, 20 + i // 4)
                    project_out(ST - 1)
                    turn_pairs(15)
                    pe.wait_ge(y_ps, ST)
                    for n in range(16):
                        pv, t = divmod(n, TT)
                        w = panel(pe, where["qkv", 8 + pv])
                        if n >= 2:
                            pe.wait_ge(v_ok, n - 1)
                        if n == 0:
                            pe.wait_ge(roped, 15)
                        bank = 5 if n % 2 == 0 else 3
                        for k in range(KD):
                            mm = pe.matmul(ps[:, bank, 0:PC], hT[:, k, P * t:P * (t + 1)], w[:, k, :],
                                           start=(k == 0), stop=(k == KD - 1))
                        mm.then_inc(v_ps, 1)
                        if t == TT - 1:
                            pe.wait_ge(v_ps, n + 1)
                            pe.nop().then_inc(panel_used, 1)
                            ada_columns(pe, 28 + pv)

                @block.scalar
                def _(act):
                    act.wait_ge(angle, 1)
                    act.activation(cosT, sinT, ACT.Sin, scale=0.5).then_inc(sines, 1)
                    act.wait_ge(sines, 1)
                    act.activation(sinT, sinT, ACT.Sin).then_inc(sines, 1)

                    def whole_turns(i):
                        w = work[i % 2]
                        if i >= 2:
                            act.wait_ge(trig, 4 * (i - 1))
                        act.activation(w[0], times, ACT.Copy, bias=ROUND, scale=s5c[:, 14, i:i + 1]).then_inc(act_in, 1)
                        act.wait_ge(act_in, i + 1)
                        act.activation(w[0], w[0], ACT.Copy, bias=-ROUND).then_inc(turns, 1)

                    def sine_cosine(i):
                        w = work[i % 2]
                        act.wait_ge(frac, i + 1)
                        act.activation(w[0], w[1], ACT.Sin, scale=TWO_PI / 2).then_inc(trig, 1)
                        if i >= 2:
                            act.wait_ge(rot_out, 2 * (i - 1))
                            act.wait_ge(rot_pool, 2 * (i - 1))
                        act.activation(w[2], w[1], ACT.Sin, scale=TWO_PI).then_inc(trig, 1)
                        act.wait_ge(trig, 4 * i + 2)
                        act.activation(w[0], w[0], ACT.Square).then_inc(trig, 1)
                        act.wait_ge(trig, 4 * i + 3)
                        act.activation(w[3], w[0], ACT.Copy, bias=1.0, scale=-2.0).then_inc(trig, 1)

                    act.wait_ge(dch, 1)
                    whole_turns(0)
                    whole_turns(1)
                    sine_cosine(0)
                    for m in range(SC):
                        act.wait_ge(u_ps, m + 1)
                        act.copy(uT[:, m, :], ps[:, m % 2, :]).then_inc(u_ok, 1)
                    for i in range(ST):
                        if i + 1 < ST:
                            sine_cosine(i + 1)
                        if i + 2 < ST:
                            whole_turns(i + 2)
                        if i % 2:
                            m = i // 2
                            act.wait_ge(z_ps, m + 1)
                            if m >= 2:
                                act.wait_ge(roped, m - 1)
                                act.wait_ge(swap_ps, m - 1)
                            act.copy(raw[m % 2], ps[:, 5, :]).then_inc(raw_ok, 1)
                    for n in range(16):
                        act.wait_ge(v_ps, n + 1)
                        pv, t = divmod(n, TT)
                        act.copy(v_tok[:, t, PC * pv:PC * (pv + 1)], ps[:, 5 if n % 2 == 0 else 3, 0:PC]).then_inc(v_ok, 1)
                    act.wait_ge(y_ok, SC)
                    for q in range(SC):
                        act.activation(uT[:, q, :], uT[:, q, :], ACT.Gelu).then_inc(gelu, 1)

                @block.gpsimd
                def _(pool):
                    for i in range(ST):
                        w = work[i % 2]
                        pool.wait_ge(rot_in, 4 * (i + 1))
                        pool.tensor_tensor(w[4], w[4], w[5], ALU.add).then_inc(summed, 1)
                        pool.tensor_tensor(w[6], w[6], w[7], ALU.subtract).then_inc(summed, 1)
                        pool.wait_ge(rot_out, 2 * (i + 1))
                        pool.tensor_tensor(w[4], w[2], w[4], ALU.mult).then_inc(rot_pool, 1)
                        pool.tensor_tensor(w[6], w[3], w[6], ALU.mult).then_inc(rot_pool, 1)
                        pool.tensor_tensor(w[5], w[5], w[7], ALU.subtract).then_inc(state, 1)
                        pool.wait_ge(rot_pool, 2 * (i + 1))
                        pool.tensor_tensor(w[4], w[4], w[6], ALU.add).then_inc(state, 1)

                @block.vector
                def _(dve):
                    v = Chain(dve, dch)
                    v(dve.tensor_tensor(s5c[:, 14, :], fh, fl, ALU.add))

                    def fraction(i):
                        w = work[i % 2]
                        dve.wait_ge(turns, i + 1)
                        v(dve.scalar_tensor_tensor(w[1], times, fh[:, i:i + 1], w[0], ALU.mult, ALU.subtract))
                        v(dve.scalar_tensor_tensor(w[1], times, fl[:, i:i + 1], w[1], ALU.mult, ALU.add))
                        dve.tensor_scalar(w[1], w[1], HALF_TURN, -HALF_TURN, ALU.min, ALU.max).then_inc(frac, 1)

                    dve.wait_ge(pos_in, 16)
                    a, w = raw[0], raw[1]
                    v(dve.tensor_copy(a, prod.bitcast(I32)))
                    v(dve.tensor_scalar(a, a, kc[:, K_FREQ:K_FREQ + 1], None, ALU.mult))
                    v(dve.tensor_scalar(w, a, 1.0 / TWO_PI, ROUND, ALU.mult, ALU.add))
                    v(dve.tensor_scalar(w, w, -ROUND, None, ALU.add))
                    for part in (C1, C2, C3):
                        v(dve.scalar_tensor_tensor(a, w, -part, a, ALU.mult, ALU.add))
                    dve.tensor_scalar(sinT, a, PI_LOW, -PI_LOW, ALU.min, ALU.max).then_inc(angle, 1)
                    dve.wait_ge(sines, 2)
                    v(dve.tensor_tensor(cosT, cosT, cosT, ALU.mult))
                    v(dve.tensor_scalar(cosT, cosT, -2.0, 1.0, ALU.mult, ALU.add))
                    fraction(0)
                    fraction(1)
                    for n in range(16, 20):
                        ada_sums(dve, v, n)

                    def rotate_in(i):
                        w = work[i % 2]
                        dve.wait_ge(trig, 4 * (i + 1))
                        dve.wait_ge(bu_ps, i + 1)
                        if i >= 2:
                            dve.wait_ge(y_ps, i - 1)
                        br, bi = ps[:, 2 * (i % 2), :], ps[:, 2 * (i % 2) + 1, :]
                        for dst, tr, b in ((4, 3, br), (5, 2, bi), (6, 3, bi), (7, 2, br)):
                            dve.tensor_tensor(w[dst], w[tr], b, ALU.mult).then_inc(rot_in, 1)

                    def scan(i):
                        w = work[i % 2]
                        dve.wait_ge(summed, 2 * (i + 1))
                        m = mag[:, i:i + 1].to_broadcast([P, T])
                        for s in (4, 6):
                            dve.tensor_tensor_scan(w[s], m, w[s], 0.0, ALU.mult, ALU.add).then_inc(scanned, 1)

                    def rotate_out(i):
                        w = work[i % 2]
                        dve.wait_ge(scanned, 2 * (i + 1))
                        dve.tensor_tensor(w[5], w[3], w[4], ALU.mult).then_inc(rot_out, 1)
                        dve.tensor_tensor(w[7], w[2], w[6], ALU.mult).then_inc(rot_out, 1)

                    def rotary(m):
                        dst = (qT if m < 8 else kT)[:, m % 8, :]
                        dve.wait_ge(raw_ok, m + 1)
                        if m >= 1:
                            dve.wait_ge(roped, m)
                        v(dve.tensor_tensor(prod, raw[m % 2], cosT, ALU.mult))
                        dve.wait_ge(swap_ps, m + 1)
                        v(dve.tensor_tensor(dst, ps[:, 6, :], sinT, ALU.mult))
                        dve.tensor_tensor(dst, prod, dst, ALU.add).then_inc(roped, 1)

                    def add_skip(q):
                        dve.wait_ge(y_ps, 4 * (q + 1))
                        dve.scalar_tensor_tensor(uT[:, q, :], uT[:, q, :], d_c[:, q:q + 1], ps[:, 4, :],
                                                 ALU.mult, ALU.add).then_inc(y_ok, 1)

                    rotate_in(0)
                    for i in range(ST):
                        scan(i)
                        rotate_out(i)
                        if i % 4 == 0 and i >= 4:
                            add_skip(i // 4 - 1)
                        if i + 1 < ST:
                            rotate_in(i + 1)
                        if i + 2 < ST:
                            fraction(i + 2)
                        if i % 2 == 0 and i >= 4:
                            rotary(i // 2 - 2)
                        if i % 4 == 2:
                            ada_sums(dve, v, 20 + i // 4)
                    rotary(14)
                    rotary(15)
                    add_skip(SC - 1)
                    for n in range(28, 32):
                        ada_sums(dve, v, n)

        attn = region_a[:, 0:4096].rearrange("p (t d) -> p t d", t=TT)
        attnT = region_a[:, 4096:8192].rearrange("p (m t) -> p m t", m=8)
        with ExitStack() as four:
            def sem4(name):
                return four.enter_context(nc.semaphore(name))

            buf = four.enter_context(nc.sbuf_tensor("attn_buf", [P, 4, T], F32))
            prob = [buf[:, n, :] for n in range(2)]
            probT = [buf[:, 2 + n, :] for n in range(2)]
            s_ps = sem4("scores_in_psum")
            masked = sem4("scores_masked")
            negmax = sem4("negmax_ready")
            p_ok = sem4("probs_ready")
            t_ps = sem4("probsT_in_psum")
            t_ok = sem4("probsT_copied")
            o_ps = sem4("out_in_psum")
            o_ok = sem4("out_scaled")
            inv = sem4("inverse_sum")
            dch = sem4("dve_chain4")
            var_ok = sem4("attn_square_mean")
            sq_ok = sem4("attn_root")
            norm_ok = sem4("attn_normed")
            mod_rT = sem4("mod_turned")
            mod_ev = sem4("mod_rows_copied")
            mod_st = sem4("mod_rows_stored")
            modr = four.enter_context(nc.sbuf_tensor("modr", [96, P], F32))
            aT_ps = sem4("attnT_in_psum")
            aT_ok = sem4("attnT_copied")
            N = HEADS * TT
            mx, nm, lsum, linv = (tiny[:, 4 * n:4 * n + 4] for n in range(4))

            with nc.Block() as block:
                @block.sync
                def _(sp):
                    load_panels(sp, first["ada3"] + RING, first["glu"] + RING)
                    sp.wait_ge(mod_ev, 1)
                    sp.dma_start(mod_rows, modr[:, :]).then_inc(mod_st, 16)
                    sp.wait_ge(mod_st, 16)

                @block.tensor
                def _(pe):
                    def scores(n):
                        h, i = divmod(n, TT)
                        r = slice(HD * (h % 2), HD * (h % 2) + HD)
                        if n >= 2:
                            pe.wait_ge(masked, n - 1)
                        pe.matmul(ps[:, n % 2, 0:P * (i + 1)], qT[r, h // 2, P * i:P * (i + 1)],
                                  kT[r, h // 2, 0:P * (i + 1)], start=True, stop=True).then_inc(s_ps, 1)

                    def turn(n):
                        i = n % TT
                        pe.wait_ge(p_ok, n + 1)
                        if n >= 2:
                            pe.wait_ge(t_ok, n - 1)
                        for b in range(i + 1):
                            mm = pe.transpose(ps[:, 2 + n % 2, P * b:P * (b + 1)], prob[n % 2][:, P * b:P * (b + 1)], ident)
                        mm.then_inc(t_ps, 1)

                    def weigh(n):
                        h, i = divmod(n, TT)
                        pe.wait_ge(t_ok, n + 1)
                        if n >= 2:
                            pe.wait_ge(o_ok, n - 1)
                        for b in range(i + 1):
                            mm = pe.matmul(ps[:, 4 + n % 2, 0:HD], probT[n % 2][:, P * b:P * (b + 1)],
                                           v_tok[:, b, HD * h:HD * (h + 1)], start=(b == 0), stop=(b == i))
                        mm.then_inc(o_ps, 1)

                    for n in range(N + 2):
                        if n < N:
                            scores(n)
                        if 1 <= n <= N:
                            turn(n - 1)
                        if n >= 2:
                            weigh(n - 2)
                        if n % 4 == 3 and n < N:
                            ada_columns(pe, 32 + n // 4)
                    pe.wait_ge(mod_rT, 1)
                    pe.transpose(ps[0:96, 6, 0:P], modT, ident).then_inc(mod_rT, 1)
                    pe.wait_ge(norm_ok, TT)
                    for m in range(8):
                        if m >= 2:
                            pe.wait_ge(aT_ok, m - 1)
                        for t in range(TT):
                            mm = pe.transpose(ps[:, m % 2, P * t:P * (t + 1)], attn[:, t, P * m:P * (m + 1)], ident)
                        mm.then_inc(aT_ps, 1)

                @block.scalar
                def _(act):
                    for n in range(N + 1):
                        if n < N:
                            w = P * (n % TT + 1)
                            act.wait_ge(negmax, n + 1)
                            if n >= 4:
                                act.wait_ge(inv, n - 3)
                            act.activation(prob[n % 2][:, 0:w], prob[n % 2][:, 0:w], ACT.Exp, bias=nm[:, n % 4:n % 4 + 1],
                                           accum_out=lsum[:, n % 4:n % 4 + 1]).then_inc(p_ok, 1)
                        if n >= 1:
                            w = P * ((n - 1) % TT + 1)
                            act.wait_ge(t_ps, n)
                            if n >= 3:
                                act.wait_ge(o_ps, n - 2)
                            act.copy(probT[(n - 1) % 2][:, 0:w], ps[:, 2 + (n - 1) % 2, 0:w]).then_inc(t_ok, 1)
                    act.wait_ge(mod_rT, 2)
                    act.copy(modr[:, :], ps[0:96, 6, 0:P]).then_inc(mod_ev, 1)
                    act.wait_ge(var_ok, 1)
                    act.activation(rstd, rstd, ACT.Sqrt).then_inc(sq_ok, 1)
                    for m in range(8):
                        act.wait_ge(aT_ps, m + 1)
                        act.activation(attnT[:, m, :], ps[:, m % 2, :], ACT.Copy, scale=g_attn_c[:, m:m + 1]).then_inc(aT_ok, 1)

                @block.vector
                def _(dve):
                    v = Chain(dve, dch)

                    def mask(n):
                        i = n % TT
                        w = P * (i + 1)
                        dve.wait_ge(s_ps, n + 1)
                        if n >= 2:
                            dve.wait_ge(t_ps, n - 1)
                        if n >= 4:
                            dve.wait_ge(p_ok, n - 3)
                        dve.tensor_tensor_reduce(prob[n % 2][:, 0:w], ps[:, n % 2, 0:w],
                                                 kc[:, K_MASK + T * i:K_MASK + T * i + w], HD ** -0.5, 3.0 * NEG,
                                                 ALU.add, ALU.max, mx[:, n % 4:n % 4 + 1]).then_inc(masked, 1)
                        dve.wait_ge(masked, n + 1)
                        dve.tensor_scalar(nm[:, n % 4:n % 4 + 1], mx[:, n % 4:n % 4 + 1], -1.0, None, ALU.mult).then_inc(negmax, 1)

                    def scale(n):
                        h, i = divmod(n, TT)
                        dve.wait_ge(p_ok, n + 1)
                        dve.reciprocal(linv[:, n % 4:n % 4 + 1], lsum[:, n % 4:n % 4 + 1]).then_inc(inv, 1)
                        dve.wait_ge(inv, n + 1)
                        dve.wait_ge(o_ps, n + 1)
                        dve.tensor_scalar(attn[:, i, HD * h:HD * (h + 1)], ps[:, 4 + n % 2, 0:HD], linv[:, n % 4:n % 4 + 1],
                                          None, ALU.mult).then_inc(o_ok, 1)

                    for n in range(N + 2):
                        if n < N:
                            mask(n)
                        if n >= 2:
                            scale(n - 2)
                        if n % 4 == 1 and n < N:
                            ada_sums(dve, v, 32 + n // 4)
                    dve.wait_ge(panel_used, first["glu"])
                    v(dve.tensor_tensor(modT[:, 32:96], modT[:, 32:96], ps[:, 7, 32:96], ALU.add))
                    v(dve.tensor_scalar(modT[:, 32:48], modT[:, 32:48], 1.0, None, ALU.add))
                    v(dve.tensor_scalar(modT[:, 64:96], modT[:, 64:96], 1.0, None, ALU.add))
                    dve.nop().then_inc(mod_rT, 1)
                    dve.wait_ge(o_ok, N)
                    dve.wait_ge(t_ps, N)
                    junk = buf[:, 0:2, :].rearrange("p a b -> p (a b)")
                    for t in range(TT):
                        v(dve.tensor_tensor_reduce(junk, attn[:, t, :], attn[:, t, :], 1.0 / AW, 0.0, ALU.mult, ALU.add,
                                                   rstd[:, t:t + 1]))
                    v(dve.tensor_scalar(rstd, rstd, EPS, None, ALU.add))
                    dve.nop().then_inc(var_ok, 1)
                    dve.wait_ge(sq_ok, 1)
                    v(dve.reciprocal(rstd, rstd))
                    for t in range(TT):
                        dve.tensor_scalar(attn[:, t, :], attn[:, t, :], rstd[:, t:t + 1], None, ALU.mult).then_inc(norm_ok, 1)

        y2T = region_c[:, 0:4096].rearrange("p (m t) -> p m t", m=SC)
        row_g1 = region_a[:, 0:D]
        keysT = sb("keysT", [P, 2, NK])
        x_in2 = sem("x_in_again")
        row_in1 = sem("gate1_row_in")
        with ExitStack() as five:
            def sem5(name):
                return five.enter_context(nc.semaphore(name))

            buf = five.enter_context(nc.sbuf_tensor("glu_buf", [P, 4, T], F32))
            keys = five.enter_context(nc.sbuf_tensor("keys", [P, 2, NK], F32))
            sg = [buf[:, n, :] for n in range(2)]
            sq = [buf[:, 2 + n, :] for n in range(2)]
            gate_ps = sem5("gate_in_psum")
            gate_ok = sem5("gate_ready")
            y2_ok = sem5("gated")
            sq2_ok = sem5("squares_ready")
            sum_ps = sem5("square_sums")
            dch = sem5("dve_chain5")
            ask = sem5("root_asked")
            root = sem5("root_ready")
            keys_in = sem5("keys_in")
            keys_ps = sem5("keysT_in_psum")
            keys_ok = sem5("keysT_copied")

            with nc.Block() as block:
                @block.sync
                def _(sp):
                    sp.dma_start(keys[:, :, :], sub_keys.rearrange("l i k c -> k (l i) c")).then_inc(keys_in, 16)
                    load_panels(sp, first["glu"] + RING, first["glu"] + 4)
                    for t in range(TT):
                        sp.dma_start(resid[:, t, :], x_v[:, t, :]).then_inc(x_in2, 16)
                    sp.dma_start(row_g1, mod_flat[:, 32 * P:32 * P + D].broadcast_to([P, D])).then_inc(row_in1, 16)
                    load_panels(sp, first["glu"] + 4, first["out"] + RING)

                @block.tensor
                def _(pe):
                    def sum_squares(m):
                        pe.wait_ge(sq2_ok, m + 1)
                        mm = pe.matmul(ps[:, 2, :], ones, sq[m % 2], start=(m == 0), stop=(m == SC - 1))
                        mm.then_inc(sum_ps, 1)

                    pe.wait_ge(keys_in, 16)
                    for n in range(2):
                        pe.transpose(ps[:, 4 + n, 0:NK], keys[:, n, :], ident).then_inc(keys_ps, 1)
                    for m in range(SC):
                        w = panel(pe, where["glu", m // 2])
                        if m >= 2:
                            pe.wait_ge(gate_ok, m - 1)
                        for k in range(SC):
                            mm = pe.matmul(ps[:, m % 2, :], w[:, k, P * (m % 2):P * (m % 2) + P], uT[:, k, :],
                                           start=(k == 0), stop=(k == SC - 1))
                        mm.then_inc(gate_ps, 1)
                        if m % 2:
                            pe.wait_ge(gate_ps, m + 1)
                            pe.nop().then_inc(panel_used, 1)
                        if m >= 1:
                            sum_squares(m - 1)
                    sum_squares(SC - 1)

                @block.scalar
                def _(act):
                    for n in range(2):
                        act.wait_ge(keys_ps, n + 1)
                        act.copy(keysT[:, n, :], ps[:, 4 + n, 0:NK]).then_inc(keys_ok, 1)
                    for m in range(SC):
                        act.wait_ge(gate_ps, m + 1)
                        if m >= 2:
                            act.wait_ge(y2_ok, m - 1)
                        act.activation(sg[m % 2], ps[:, m % 2, :], ACT.Sigmoid, bias=b_glu_c[:, m:m + 1]).then_inc(gate_ok, 1)
                        act.wait_ge(y2_ok, m + 1)
                        if m >= 2:
                            act.wait_ge(sum_ps, m - 1)
                        act.activation(sq[m % 2], y2T[:, m, :], ACT.Square).then_inc(sq2_ok, 1)
                    act.wait_ge(ask, 1)
                    act.activation(sq[0], sq[0], ACT.Sqrt).then_inc(root, 1)

                @block.vector
                def _(dve):
                    v = Chain(dve, dch)
                    for m in range(SC):
                        dve.wait_ge(gate_ok, m + 1)
                        dve.tensor_tensor(y2T[:, m, :], uT[:, m, :], sg[m % 2], ALU.mult).then_inc(y2_ok, 1)
                    dve.wait_ge(sum_ps, SC)
                    v(dve.tensor_scalar(sq[0], ps[:, 2, :], 1.0 / SW, EPS, ALU.mult, ALU.add))
                    dve.nop().then_inc(ask, 1)
                    dve.wait_ge(root, 1)
                    v(dve.reciprocal(sq[0], sq[0]))
                    for m in range(SC):
                        dve.scalar_tensor_tensor(y2T[:, m, :], y2T[:, m, :], g_ssm_c[:, m:m + 1], sq[0], ALU.mult, ALU.mult)\
                           .then_inc(y2_ok, 1)

        GROUPS = ((0,), (1, 2, 3))
        acc = [region_a[:, D * n:D * (n + 1)] for n in range(2)]
        h2_cur = region_c[:, 4096:4096 + D]
        h2T_first = region_c[:, 4096 + D:8192].rearrange("p (k t) -> p k t", k=KD)
        h2T_rest = area[:, 4096:4096 + KD * 3 * P].rearrange("p (k t) -> p k t", k=KD)
        h2_work = [region_a[:, D:2 * D], region_c[:, D:2 * D]]
        scores = resid[:, :, :].rearrange("p t (m k) -> p t m k", k=NK)
        wflat = wring[:, :, :, :].rearrange("p r k c -> p (r k c)")
        row_g2, row_lg2, row_lb2, x1_cur, outb = (wflat[:, D * n:D * (n + 1)] for n in range(5))
        expert_rows = [region_b[:, D * n:D * (n + 1)] for n in range(4)]
        expert_rows += [area[:, 4096 + D * n:4096 + D * (n + 1)] for n in range(4)]
        mixw = ada_acc
        gates = small[:, 256:256 + TT * SLOTS].rearrange("p (t s) -> p t s", t=TT)
        x1_v = x1_rows.rearrange("(t p) d -> p t d", p=P)
        h2_v = h2_rows.rearrange("(t p) d -> p t d", p=P)
        out_v = out.rearrange("b (t p) d -> p (b t) d", p=P)
        tables = (expert_u.rearrange("l e d -> (l e) d"), expert_v.rearrange("l e d -> (l e) d"))
        with ExitStack() as six:
            def sem6(name):
                return six.enter_context(nc.semaphore(name))

            def sb6(name, shape, dt=F32):
                return six.enter_context(nc.sbuf_tensor(name, shape, dt))

            picks = sb6("picks", [P, TT, SLOTS], U32)
            qm = sb6("qm", [P, 2, 3 * P])
            cand = region_c[:, 4096 + D:8192].rearrange("p (h a b) -> p h a b", h=PH, a=TOPK)
            topi = sb6("topi", [P, 2 * PH, TOPK], U32)
            top = sb6("top", [P, 2 * PH, TOPK])
            topf = sb6("topf", [P, 2 * PH, TOPK])
            best = sb6("best", [P, PH, TOPK])
            besti = sb6("besti", [P, PH, TOPK], U32)
            half_u = sb6("half_u", [P, PH, TOPK], U32)
            half_f = sb6("half_f", [P, PH, TOPK])
            side = [sb6(f"side{n}", [P, PH, TOPK])[:, :, :] for n in range(2)]
            gsum = sb6("gsum", [P, PH, 1])[:, :, :]
            dots = sb6("dots", [P, NB])
            hidden = sb6("hidden", [P, SLOTS])
            coef = sb6("coef", [P, SLOTS])
            index = sb6("index", [P, NB], U32)
            spare = sb6("spare", [1, 2])
            mix_ps = sem6("mix_in_psum")
            scaled = sem6("mix_scaled")
            mix_ok = sem6("mix_used")
            ask = sem6("root_asked6")
            root = sem6("root_ready6")
            x1_ok = sem6("x1_ready")
            x1_st = sem6("x1_stored")
            xh_ok = sem6("xhat2_ready")
            tr_ok = sem6("h2T_in_psum")
            ev_ok = sem6("h2T_copied")
            h2_ok = sem6("h2_ready")
            h2_st = [sem6(f"h2_stored{n}") for n in range(2)]
            q_ps = sem6("query_in_psum")
            q_ok = sem6("query_copied")
            k_ps = sem6("key_scores_in_psum")
            k_ok = sem6("key_scores_copied")
            gate_a = sem6("gate_asked")
            gate_e = sem6("gate_exp")
            picked = sem6("experts_picked")
            spare_ok = sem6("spare_zeroed")
            row_in = [sem6(f"row_in{b}") for b in range(NB)]
            row_used = sem6("row_used")
            index_ok = sem6("index_ready")
            dot_ok = sem6("dots_kept")
            hid_ok = sem6("hidden_ready")
            act_ok = sem6("gelu_ready")
            h2_in = sem6("h2_in")
            x1_in = sem6("x1_in")
            rows_in = sem6("rows_in6")
            out_ok = sem6("out_ready")
            out_st = sem6("out_stored")
            dch = sem6("dve_chain6")

            def rows_before(t, side_n, b):
                first_tile = 2 * SLOTS // RINGS[0] if b < RINGS[0] else 0
                if t == 0:
                    return side_n * SLOTS // RINGS[0] if b < RINGS[0] else 0
                return first_tile + (2 * (t - 1) + side_n) * SLOTS // NB

            with nc.Block() as block:
                @block.sync
                def _(sp):
                    load_panels(sp, first["out"] + RING, where["qp", 0] + 1)
                    sp.wait_ge(x1_ok, 1)
                    sp.dma_start(x1_v[:, 0, :], resid[:, 0, :]).then_inc(x1_st, 16)
                    load_panels(sp, where["qp", 0] + 1, where["qp", 8] + 1)
                    for t in range(1, TT):
                        sp.wait_ge(x1_ok, t + 1)
                        sp.dma_start(x1_v[:, t, :], resid[:, t, :]).then_inc(x1_st, 16)
                    load_panels(sp, where["qp", 8] + 1, where["qp", 8] + 2)
                    for t in range(1, TT):
                        sp.wait_ge(h2_ok, t + 1)
                        sp.dma_start(h2_v[:, t, :], h2_work[t % 2]).then_inc(h2_st[t % 2], 16)
                    load_panels(sp, where["qp", 8] + 2, first["end"])
                    sp.wait_ge(panel_used, first["end"])
                    for dst, src in ((row_g2, mod_flat[:, 80 * P:80 * P + D]), (row_lg2, ln2_g), (row_lb2, ln2_b)):
                        sp.dma_start(dst, src.broadcast_to([P, D])).then_inc(rows_in, 16)
                    sp.wait_ge(x1_st, 16 * TT)
                    sp.wait_ge(h2_st[1], 32)
                    sp.wait_ge(h2_st[0], 16)
                    for t in range(TT):
                        sp.dma_start(x1_cur, x1_v[:, t, :]).then_inc(x1_in, 16)
                        if t + 1 < TT:
                            sp.wait_ge(hid_ok, t + 1)
                            sp.dma_start(h2_cur, h2_v[:, t + 1, :]).then_inc(h2_in, 16)
                        sp.wait_ge(out_ok, t + 1)
                        sp.dma_start(out_v[:, t, :], outb).then_inc(out_st, 16)
                    sp.wait_ge(out_st, 16 * TT)

                @block.tensor
                def _(pe):
                    def score(grp, m):
                        n = 16 * grp + m
                        pe.wait_ge(q_ok, n + 1)
                        if m >= 2:
                            pe.wait_ge(k_ok, n - 1)
                        for j in range(len(GROUPS[grp])):
                            mm = pe.matmul(ps[:, 6 + m % 2, P * j:P * (j + 1)], qm[:, m % 2, P * j:P * (j + 1)],
                                           keysT[:, m % 2, :], start=True, stop=True)
                        mm.then_inc(k_ps, 1)

                    for grp, tiles in enumerate(GROUPS):
                        if grp:
                            pe.wait_ge(q_ok, 16)
                            pe.wait_ge(k_ok, 16)
                        for pn in range(8):
                            w = panel(pe, where["out", 8 * grp + pn])
                            for j, t in enumerate(tiles):
                                n = pn if grp == 0 else 8 + 3 * pn + j
                                if n >= 4:
                                    pe.wait_ge(scaled, n - 3)
                                for k in range(KD):
                                    lhs = attnT[:, k, P * t:P * (t + 1)] if k < 8 else y2T[:, k - 8, P * t:P * (t + 1)]
                                    mm = pe.matmul(ps[:, 4 + n % 4, 0:PC], lhs, w[:, k, :], start=(k == 0), stop=(k == KD - 1))
                                mm.then_inc(mix_ps, 1)
                            pe.wait_ge(mix_ps, n + 1)
                            pe.nop().then_inc(panel_used, 1)
                        pe.wait_ge(x1_ok, tiles[-1] + 1)
                        pe.nop().then_inc(panel_used, 1)
                        for t in tiles:
                            src = h2_cur if t == 0 else h2_work[t % 2]
                            pe.wait_ge(xh_ok, t + 1)
                            for b in range(4):
                                if t >= 1:
                                    pe.wait_ge(ev_ok, 4 * (t - 1) + b + 1)
                                for k in range(4):
                                    mm = pe.transpose(ps[:, b, P * k:P * (k + 1)], src[:, P * (4 * b + k):P * (4 * b + k + 1)], ident)
                                mm.then_inc(tr_ok, 1)
                        pe.wait_ge(ev_ok, 4 * (tiles[-1] + 1))
                        hT2 = h2T_rest if grp else h2T_first
                        width = P * len(tiles)
                        for m in range(2 * PH):
                            n = 16 * grp + m
                            w = panel(pe, where["qp", 8 * grp + m // 2])
                            if m >= 2:
                                pe.wait_ge(q_ok, n - 1)
                            if m == 0:
                                pe.wait_ge(scaled, 8 if grp == 0 else 32)
                            for k in range(KD):
                                mm = pe.matmul(ps[:, 4 + m % 2, 0:width], w[:, k, P * (m % 2):P * (m % 2) + P], hT2[:, k, :],
                                               start=(k == 0), stop=(k == KD - 1))
                            mm.then_inc(q_ps, 1)
                            if m % 2:
                                pe.wait_ge(q_ps, n + 1)
                                if m == 1:
                                    pe.wait_ge(h2_ok, tiles[-1] + 1)
                                    pe.nop().then_inc(panel_used, 1)
                                pe.nop().then_inc(panel_used, 1)
                            if m >= 1:
                                score(grp, m - 1)
                        score(grp, 2 * PH - 1)

                @block.scalar
                def _(act):
                    def roots(n, ts):
                        act.wait_ge(ask, n + 1)
                        act.activation(rstd[:, ts], rstd[:, ts], ACT.Sqrt).then_inc(root, 1)

                    def h2_columns(t):
                        for b in range(4):
                            act.wait_ge(tr_ok, 4 * t + b + 1)
                            for k in range(4 * b, 4 * b + 4):
                                dst = h2T_first[:, k, :] if t == 0 else h2T_rest[:, k, P * (t - 1):P * t]
                                ins = act.activation(dst, ps[:, b, P * (k % 4):P * (k % 4 + 1)], ACT.Identity,
                                                     bias=modT[:, 48 + k:49 + k], scale=modT[:, 64 + k:65 + k])
                            ins.then_inc(ev_ok, 1)

                    def queries(grp):
                        tiles = GROUPS[grp]
                        width = P * len(tiles)
                        for m in range(2 * PH + 1):
                            n = 16 * grp + m
                            if m < 2 * PH:
                                act.wait_ge(q_ps, n + 1)
                                if n >= 2:
                                    act.wait_ge(k_ps, n - 1)
                                act.copy(qm[:, m % 2, 0:width], ps[:, 4 + m % 2, 0:width]).then_inc(q_ok, 1)
                            if m == 1:
                                act.wait_ge(x1_st, 16 * (tiles[-1] + 1))
                            if m >= 1:
                                act.wait_ge(k_ps, n)
                                act.copy(scores[:, tiles[0]:tiles[-1] + 1, m - 1, :],
                                         ps[:, 6 + (m - 1) % 2, 0:width].rearrange("p (t k) -> p t k", k=NK)).then_inc(k_ok, 1)

                    def gate_exponentials(t):
                        act.wait_ge(gate_a, t + 1)
                        act.activation(best[:, :, :], best[:, :, :], ACT.Exp).then_inc(gate_e, 1)

                    roots(0, slice(0, 1))
                    roots(1, slice(0, 1))
                    h2_columns(0)
                    queries(0)
                    gate_exponentials(0)
                    roots(2, slice(1, 4))
                    roots(3, slice(1, 4))
                    for t in range(1, TT):
                        h2_columns(t)
                    for t in range(TT):
                        act.wait_ge(hid_ok, t + 1)
                        act.activation(hidden[:, :], hidden[:, :], ACT.Gelu).then_inc(act_ok, 1)
                        if t == 0:
                            queries(1)
                        if t + 1 < TT:
                            gate_exponentials(t + 1)
                        roots(4 + t, slice(0, 1))

                @block.gpsimd
                def _(pool):
                    pool.memset(spare[:, :], 0.0).then_inc(spare_ok, 1)
                    pool.wait_ge(spare_ok, 1)
                    for t in range(TT):
                        ring = RINGS[t]
                        pool.wait_ge(picked, t + 1)
                        if t == 1:
                            pool.wait_ge(h2_st[1], 32)
                        for side_n, table in enumerate(tables):
                            before = (2 * t + side_n) * SLOTS

                            def gather(it, older):
                                for b in range(ring):
                                    if older[b]:
                                        pool.wait_ge(row_used, it * ring + (before + b - older[b] + 1))
                                    pool.tensor_copy(index[:, b:b + 1], picks[:, t, bass.ds(it * ring + b, 1)]).then_inc(index_ok, 1)
                                    pool.wait_ge(index_ok, it * ring + (before + b + 1))
                                    pool.tensor_tensor(spare[:, 0:1], spare[:, 1:2], spare[:, 1:2], ALU.add)
                                    pool.indirect_dma_start(expert_rows[b], None, table,
                                                            bass.IndirectOffsetOnAxis(ap=index[:, b:b + 1], axis=0))\
                                        .then_inc(row_in[b], 16)

                            if side_n == 0 and t == 0:
                                older = [0] * ring
                            elif side_n == 0 and RINGS[t - 1] < ring:
                                older = [RINGS[t - 1] if b < RINGS[t - 1] else 0 for b in range(ring)]
                            else:
                                older = [ring] * ring
                            gather(0, older)
                            with pool.Fori(1, SLOTS // ring) as it:
                                gather(it, [ring] * ring)

                @block.vector
                def _(dve):
                    v = Chain(dve, dch)

                    def mix_out(grp, pn, row):
                        cols = slice(PC * pn, PC * (pn + 1))
                        for j, t in enumerate(GROUPS[grp]):
                            n = pn if grp == 0 else 8 + 3 * pn + j
                            dve.wait_ge(mix_ps, n + 1)
                            if n >= 2:
                                dve.wait_ge(mix_ok, n - 1)
                            dve.tensor_tensor(mixw[:, n % 2, :], ps[:, 4 + n % 4, 0:PC], row[:, cols], ALU.mult).then_inc(scaled, 1)
                            dve.wait_ge(scaled, n + 1)
                            dve.scalar_tensor_tensor(resid[:, t, cols], resid[:, t, cols], ALPHA, mixw[:, n % 2, :],
                                                     ALU.mult, ALU.add).then_inc(mix_ok, 1)
                        dve.wait_ge(mix_ok, n + 1)

                    def statistics(n, tiles, srcs):
                        for t, src in zip(tiles, srcs):
                            for q in range(4):
                                ins = dve.bn_stats(stats[:, q, :], src[:, 512 * q:512 * (q + 1)])
                            v(ins)
                            v(dve.bn_aggr(mv[:, t, :], stats[:, :, :]))
                        r = rstd[:, tiles[0]:tiles[-1] + 1]
                        v(dve.tensor_scalar(r, mv[:, tiles[0]:tiles[-1] + 1, 1], EPS, None, ALU.add))
                        dve.nop().then_inc(ask, 1)

                    def inverse(n, tiles):
                        r = rstd[:, tiles[0]:tiles[-1] + 1]
                        dve.wait_ge(root, n + 1)
                        v(dve.reciprocal(r, r))

                    def standardise(dst, src, t):
                        return dve.tensor_scalar(dst, src, mv[:, t, 0:1], rstd[:, t:t + 1], ALU.subtract, ALU.mult)

                    def first_norm(grp, t):
                        rows = panel(dve, where["rows", 2 * grp]).rearrange("p k c -> p (k c)")
                        r = resid[:, t, :]
                        v(standardise(r, r, t))
                        v(dve.tensor_tensor(r, r, rows[:, 0:D], ALU.mult))
                        dve.tensor_tensor(r, r, rows[:, D:2 * D], ALU.add).then_inc(x1_ok, 1)
                        dve.wait_ge(x1_ok, t + 1)

                    def second_norm(t):
                        if t == 3:
                            dve.wait_ge(h2_st[1], 16)
                        dst = h2_cur if t == 0 else h2_work[t % 2]
                        standardise(dst, resid[:, t, :], t).then_inc(xh_ok, 1)

                    def modulate(grp, t):
                        rows = panel(dve, where["rows", 2 * grp + 1]).rearrange("p k c -> p (k c)")
                        h = h2_cur if t == 0 else h2_work[t % 2]
                        dve.wait_ge(tr_ok, 4 * (t + 1))
                        v(dve.tensor_tensor(h, h, rows[:, D:2 * D], ALU.mult))
                        dve.tensor_tensor(h, h, rows[:, 0:D], ALU.add).then_inc(h2_ok, 1)

                    def largest(t, m):
                        s = scores[:, t, m, :]
                        dve.wait_ge(k_ok, m + 1 if t == 0 else 16 + m + 1)
                        v(dve.max(top[:, m, 0:8], s))
                        v(dve.max_index(topi[:, m, 0:8], top[:, m, 0:8], s))
                        v(dve.match_replace(s, top[:, m, 0:8], s, -3.0e38))
                        v(dve.max(top[:, m, 8:16], s))
                        v(dve.max_index(topi[:, m, 8:16], top[:, m, 8:16], s))

                    def pair_sums():
                        v(dve.tensor_copy(topf[:, :, :], topi[:, :, :]))
                        pair = top[:, :, :].rearrange("p (h i) s -> p h i s", i=2)
                        v(dve.tensor_tensor(cand, pair[:, :, 0, :].unsqueeze(3).broadcast_to([P, PH, TOPK, TOPK]),
                                            pair[:, :, 1, :].unsqueeze(2).broadcast_to([P, PH, TOPK, TOPK]), ALU.add))

                    def largest_pairs(h):
                        s = cand[:, h].rearrange("p a b -> p (a b)")
                        v(dve.max(best[:, h, 0:8], s))
                        v(dve.max_index(besti[:, h, 0:8], best[:, h, 0:8], s))
                        v(dve.match_replace(s, best[:, h, 0:8], s, -3.0e38))
                        v(dve.max(best[:, h, 8:16], s))
                        v(dve.max_index(besti[:, h, 8:16], best[:, h, 8:16], s))

                    def keys_of_pairs(n):
                        if n == 0:
                            v(dve.tensor_scalar(half_u[:, :, :], besti[:, :, :], 4, None, ALU.logical_shift_right))
                        else:
                            v(dve.tensor_scalar(half_u[:, :, :], besti[:, :, :], 15, None, ALU.bitwise_and))
                        v(dve.tensor_copy(half_f[:, :, :], half_u[:, :, :]))
                        iota = kc[:, K_IOTA:K_IOTA + TOPK].unsqueeze(1).unsqueeze(1).broadcast_to([P, PH, TOPK, TOPK])
                        v(dve.tensor_tensor(cand, half_f[:, :, :].unsqueeze(3).broadcast_to([P, PH, TOPK, TOPK]), iota, ALU.is_equal))
                        fi = topf[:, :, :].rearrange("p (h i) s -> p h i s", i=2)[:, :, n, :]
                        v(dve.tensor_tensor(cand, cand, fi.unsqueeze(2).broadcast_to([P, PH, TOPK, TOPK]), ALU.mult))
                        v(dve.tensor_reduce(side[n], cand, AX, ALU.add))

                    def softmax_top():
                        v(dve.tensor_copy(gsum, best[:, :, 0:1]))
                        v(dve.tensor_tensor(best[:, :, :], best[:, :, :], gsum.broadcast_to([P, PH, TOPK]), ALU.subtract))
                        dve.nop().then_inc(gate_a, 1)

                    def finish_choice(t):
                        v(dve.scalar_tensor_tensor(side[0], side[0], float(NK), side[1], ALU.mult, ALU.add))
                        dve.tensor_copy(picks[:, t, :].rearrange("p (h s) -> p h s", h=PH), side[0]).then_inc(picked, 1)
                        dve.wait_ge(gate_e, t + 1)
                        v(dve.tensor_reduce(gsum, best[:, :, :], AX, ALU.add))
                        v(dve.reciprocal(gsum, gsum))
                        v(dve.tensor_tensor(gates[:, t, :].rearrange("p (h s) -> p h s", h=PH), best[:, :, :],
                                            gsum.broadcast_to([P, PH, TOPK]), ALU.mult))

                    def choose_pairs(n):
                        if n == 0:
                            pair_sums()
                        if n < 4:
                            largest_pairs(2 * n)
                            largest_pairs(2 * n + 1)
                        if n == 4:
                            softmax_top()
                        if n in (4, 5):
                            keys_of_pairs(n - 4)

                    def dot_products(t, lo, hi):
                        ring = RINGS[t]
                        before = 2 * t * SLOTS
                        turns_before = 0 if t == 0 else SLOTS // RINGS[0] + (t - 1) * (SLOTS // NB)
                        with dve.Fori(lo, hi) as it:
                            for b in range(ring):
                                dve.wait_ge(row_in[b], (it + (rows_before(t, 0, b) + 1)) * 16)
                                dve.tensor_tensor_reduce(expert_rows[b], expert_rows[b], h2_cur, 1.0, 0.0, ALU.mult, ALU.add,
                                                         dots[:, b:b + 1]).then_inc(row_used, 1)
                            dve.wait_ge(row_used, it * ring + (before + ring))
                            dve.tensor_copy(hidden[:, bass.ds(it * ring, ring)], dots[:, 0:ring]).then_inc(dot_ok, 1)
                            dve.wait_ge(dot_ok, it + (turns_before + 1))

                    def coefficients(t):
                        dve.nop().then_inc(hid_ok, 1)
                        for a in acc:
                            v(dve.memset(a, 0.0))
                        dve.wait_ge(act_ok, t + 1)
                        v(dve.tensor_tensor(coef[:, :], hidden[:, :], gates[:, t, :], ALU.mult))

                    def weighted_rows(t, lo, hi):
                        ring = RINGS[t]
                        before = (2 * t + 1) * SLOTS
                        with dve.Fori(lo, hi) as it:
                            for b in range(ring):
                                dve.wait_ge(row_in[b], (it + (rows_before(t, 1, b) + 1)) * 16)
                                a = acc[b % 2]
                                dve.wait_ge(row_used, it * ring + (before + b - 1))
                                dve.scalar_tensor_tensor(a, expert_rows[b], coef[:, bass.ds(it * ring + b, 1)], a,
                                                         ALU.mult, ALU.add).then_inc(row_used, 1)

                    def last_norm(t):
                        dve.wait_ge(row_used, (2 * t + 2) * SLOTS)
                        if t == 0:
                            dve.wait_ge(rows_in, 48)
                        dve.wait_ge(x1_in, 16 * (t + 1))
                        a = acc[0]
                        v(dve.tensor_tensor(a, acc[0], acc[1], ALU.add))
                        v(dve.tensor_tensor(a, a, row_g2, ALU.mult))
                        v(dve.scalar_tensor_tensor(a, x1_cur, ALPHA, a, ALU.mult, ALU.add))
                        statistics(4 + t, (0,), (a,))
                        inverse(4 + t, (0,))
                        if t >= 1:
                            dve.wait_ge(out_st, 16 * t)
                        v(standardise(outb, a, 0))
                        v(dve.tensor_tensor(outb, outb, row_lg2, ALU.mult))
                        dve.tensor_tensor(outb, outb, row_lb2, ALU.add).then_inc(out_ok, 1)

                    dve.wait_ge(row_in1, 16)
                    dve.wait_ge(x_in2, 16 * TT)
                    for pn in range(8):
                        mix_out(0, pn, row_g1)
                    statistics(0, (0,), (resid[:, 0, :],))
                    inverse(0, (0,))
                    first_norm(0, 0)
                    statistics(1, (0,), (resid[:, 0, :],))
                    inverse(1, (0,))
                    second_norm(0)
                    modulate(0, 0)
                    for m in range(2 * PH):
                        largest(0, m)
                    for n in range(6):
                        choose_pairs(n)
                    finish_choice(0)

                    rest = GROUPS[1]
                    sources = [resid[:, t, :] for t in rest]
                    for pn in range(8):
                        dot_products(0, 2 * pn, 2 * pn + 2)
                        mix_out(1, pn, row_g1)
                    statistics(2, rest, sources)
                    dot_products(0, 16, 18)
                    inverse(2, rest)
                    for t in rest:
                        first_norm(1, t)
                        dot_products(0, 16 + 2 * t, 18 + 2 * t)
                    statistics(3, rest, sources)
                    dot_products(0, 24, 26)
                    inverse(3, rest)
                    for t in rest:
                        second_norm(t)
                        dot_products(0, 24 + 2 * t, 26 + 2 * t)
                        modulate(1, t)
                    dve.wait_ge(h2_st[0], 16)
                    coefficients(0)
                    weighted_rows(0, 0, 4)
                    for n in range(8):
                        largest(1, 2 * n)
                        largest(1, 2 * n + 1)
                        weighted_rows(0, 4 + 2 * n, 6 + 2 * n)
                    for n in range(6):
                        choose_pairs(n)
                        weighted_rows(0, 20 + 2 * n, 22 + 2 * n)
                    finish_choice(1)
                    last_norm(0)

                    for t in rest:
                        dve.wait_ge(h2_in, 16 * t)
                        if t + 1 == TT:
                            dot_products(t, 0, 16)
                            coefficients(t)
                            weighted_rows(t, 0, 16)
                        else:
                            for n in range(8):
                                dot_products(t, 2 * n, 2 * n + 2)
                                largest(t + 1, 2 * n)
                                largest(t + 1, 2 * n + 1)
                            coefficients(t)
                            weighted_rows(t, 0, 2)
                            for n in range(6):
                                choose_pairs(n)
                                weighted_rows(t, 2 + 2 * n, 4 + 2 * n)
                            finish_choice(t + 1)
                            weighted_rows(t, 14, 16)
                        last_norm(t)


_INS = ['x', 'c', 'positions', 'w_ada', 'b_ada', 'w_in', 'lam_re', 'lam_im', 'log_dt', 'ssm_b_re', 'ssm_b_im',
        'ssm_c_re', 'ssm_c_im', 'ssm_d', 'w_glu', 'b_glu', 'g_attn', 'g_ssm', 'w_out', 'ln1_g', 'ln1_b', 'w_qp',
        'sub_keys', 'expert_u', 'expert_v', 'ln2_g', 'ln2_b']


def kernel(**inputs):
    import concourse.bacc as _bacc
    from concourse.bass_utils import run_bass_kernel_spmd as _run

    nc = _bacc.Bacc("TRN2", target_bir_lowering=False, num_devices=1)
    arrays, args = {}, []
    for name in _INS:
        a = np.ascontiguousarray(inputs[name])
        arrays[f"in_{name}"] = a
        args.append(nc.dram_tensor(f"in_{name}", a.shape, mybir.dt.from_np(a.dtype), kind="ExternalInput").ap())
    arrays["in_constants"] = constants()
    consts = nc.dram_tensor("in_constants", (P, K_END), F32, kind="ExternalInput").ap()
    mod_rows = nc.dram_tensor("mod_rows", (96, P), F32, kind="Internal").ap()
    x1_rows = nc.dram_tensor("x1_rows", (T, D), F32, kind="Internal").ap()
    h2_rows = nc.dram_tensor("h2_rows", (T, D), F32, kind="Internal").ap()
    out = nc.dram_tensor("out_x", (1, T, D), F32, kind="ExternalOutput").ap()
    hybrid_layer(nc, consts, *args, mod_rows, x1_rows, h2_rows, out)
    r = _run(nc, [arrays], core_ids=[0])
    return r.results[0]["out_x"]
```

```python
from contextlib import ExitStack

import numpy as np

import concourse.bass as bass
from concourse import mybir

F32 = mybir.dt.float32
I32 = mybir.dt.int32
U32 = mybir.dt.uint32
ALU = mybir.AluOpType
ACT = mybir.ActivationFunctionType
AX = mybir.AxisListType.X

P = 128
T = 512
TT = T // P
D = 2048
KD = D // P
HEADS, HD = 16, 64
AW = HEADS * HD
SW = D - AW
G, GP, NS = 64, 16, 64
ST = G * NS // P
SC = SW // P
PH, TOPK, NK = 8, 16, 128
SLOTS = PH * TOPK
EPS = 1e-5
ALPHA = 2.0 ** 0.25
NEG = -1e30
TWO_PI = 6.283185307179586
C1 = 6.28125
C2 = 0.0019350051879882812
C3 = TWO_PI - C1 - C2
PI_LOW = 3.1415925
HALF_TURN = 0.49999997
ROUND = 12582912.0
ROUND13 = 1536.0
PC = 256
RING = 3
NB = 4
QROWS = 32

K_ID = 0
K_MASK = K_ID + P
K_SWAP = K_MASK + TT * T
K_TIME = K_SWAP + P
K_FREQ = K_TIME + T
K_IOTA = K_FREQ + 1
K_ONE = K_IOTA + NK
K_END = K_ONE + P


def constants():
    a = np.zeros((P, K_END), np.float32)
    a[:, K_ID:K_ID + P] = np.eye(P)
    t = np.arange(T)[:, None]
    s = np.arange(T)[None, :]
    d = t - s
    count = ((d >= 0) & (d <= 128)).astype(np.int64)
    count += (d >= 0) & (d % 4 == 0)
    count += (d >= 0) & (d % 16 == 0)
    bias = np.where(count > 0, HD ** 0.5 * np.log(np.maximum(count, 1)), NEG).astype(np.float32)
    for i in range(TT):
        a[:, K_MASK + i * T:K_MASK + (i + 1) * T] = bias[i * P:(i + 1) * P]
    for m in range(P):
        half = HD // 2
        if m % HD < half:
            a[m + half, K_SWAP + m] = -1.0
        else:
            a[m - half, K_SWAP + m] = 1.0
    a[:, K_TIME:K_TIME + T] = np.arange(T)
    half = HD // 2
    a[:, K_FREQ] = np.power(np.float32(10000.0), -np.arange(half, dtype=np.float32) / np.float32(half))[np.arange(P) % half]
    a[:, K_IOTA:K_IOTA + NK] = np.arange(NK)
    a[:, K_ONE:K_ONE + P] = 1.0
    return a


def hybrid_layer(nc, consts, x, c, positions, w_ada, b_ada, w_in, lam_re, lam_im, log_dt, ssm_b_re, ssm_b_im,
                 ssm_c_re, ssm_c_im, ssm_d, w_glu, b_glu, g_attn, g_ssm, w_out, ln1_g, ln1_b, w_qp, sub_keys,
                 expert_u, expert_v, ln2_g, ln2_b, mod_rows, x1_rows, h2_rows, out):
    ctx = ExitStack()

    def sb(name, shape, dt=F32):
        return ctx.enter_context(nc.sbuf_tensor(name, shape, dt))

    def sem(name):
        return ctx.enter_context(nc.semaphore(name))

    with ctx:
        kc = sb("kc", [P, K_END])
        ident = kc[:, K_ID:K_ID + P]
        ones = kc[:, K_ONE:K_ONE + P]
        swap = kc[:, K_SWAP:K_SWAP + P]
        times = kc[:, K_TIME:K_TIME + T]
        small = sb("small", [P, 1024])
        resid = sb("resid", [P, TT, D])
        area = sb("area", [P, 16384])
        region_a = area[:, 0:8192]
        region_c = area[:, 8192:16384]
        ada_acc = sb("ada_acc", [P, 2, PC])
        wring = sb("wring", [P, RING, KD, PC])
        region_b = sb("region_b", [P, 8192])
        ps = ctx.enter_context(nc.psum_tensor("ps", [P, 8, 512], F32))

        modT = small[:, 0:96]
        cT = small[:, 96:112]
        csig = small[:, 112:128]
        vecs = small[:, 128:160]
        g_attn_c, g_ssm_c, b_glu_c, d_c = (vecs[:, 8 * n:8 * n + 8] for n in range(4))
        lam = small[:, 160:256]
        s5c = small[:, 256:256 + 32 * 16].rearrange("p (n s) -> p n s", s=32)
        stats = small[:, 768:792].rearrange("p (n s) -> p n s", s=6)
        mv = small[:, 792:800].rearrange("p (n s) -> p n s", s=2)
        rstd = small[:, 800:804]

        hT = region_a[:, :].rearrange("p (k t) -> p k t", k=KD)
        xhat = region_b[:, :].rearrange("p (t d) -> p t d", t=TT)
        v_tok = region_c[:, 0:4096].rearrange("p (t d) -> p t d", t=TT)
        uT = region_c[:, 4096:8192].rearrange("p (m t) -> p m t", m=SC)

        def panels_of(w, cols, rows=KD):
            v = w.rearrange("(k p) n -> p k n", p=P)
            return [(v[:, :, n:n + PC], rows) for n in cols]

        ada = w_ada.rearrange("l a b -> (l a) b")
        win = w_in.rearrange("l a b -> (l a) b")
        ADA1 = panels_of(ada, range(0, 2 * D, PC))
        UP = panels_of(win, range(3 * AW, 3 * AW + SW, PC))
        ADA2 = panels_of(ada, range(2 * D, 6 * D, PC))
        QKV = panels_of(win, range(0, 3 * AW, PC))
        GLU = panels_of(w_glu.rearrange("l a b -> (l a) b"), range(0, SW, PC), SC)
        OUT = panels_of(w_out.rearrange("l a b -> (l a) b"), range(0, D, PC))
        QP = panels_of(w_qp.rearrange("l a b -> (l a) b"), range(0, PH * 2 * P, PC))
        order = [("ada", n) for n in range(len(ADA1))]
        for n in range(len(UP)):
            order += [("u", n), ("ada", 16 + n)]
        for n in range(8):
            order += [("qkv", n), ("ada", 20 + n)]
        for n in range(4):
            order += [("qkv", 8 + n), ("ada", 28 + n)]
        order += [("ada", n) for n in range(32, 48)]
        order += [("glu", n) for n in range(len(GLU))]
        for grp in range(2):
            order += [("out", 8 * grp + n) for n in range(8)]
            order += [("rows", 2 * grp), ("rows", 2 * grp + 1)]
            order += [("qp", 8 * grp + n) for n in range(8)]
        mod_flat = mod_rows.rearrange("a b -> (a b)").rearrange("(o n) -> o n", o=1)
        ROWS = [((ln1_g, ln1_b), 0), ((mod_flat[:, 48 * P:48 * P + 2 * D],), 0)]
        lots = {"ada": ADA1 + ADA2, "u": UP, "qkv": QKV, "glu": GLU, "out": OUT + OUT, "qp": QP + QP, "rows": ROWS + ROWS}
        panels = [lots[kind][n] for kind, n in order]
        where = {key: g for g, key in enumerate(order)}
        first = {"u": where["u", 0], "glu": where["glu", 0], "out": where["out", 0], "qp": where["qp", 0],
                 "ada3": where["ada", 32], "end": len(order)}
        by_pe = (2, 5, 8, 11, 13, 15)
        ada_sum = sem("ada_summed")
        panel_in = [sem(f"panel_in{s}") for s in range(RING)]
        panel_used = sem("panel_used")

        def load_panels(sp, lo, hi):
            for g in range(lo, min(hi, len(panels))):
                src, rows = panels[g]
                if g >= RING:
                    sp.wait_ge(panel_used, g - RING + 1)
                if rows:
                    sp.dma_start(wring[:, g % RING, 0:rows, :], src).then_inc(panel_in[g % RING], 16)
                else:
                    flat = wring[:, g % RING, :, :].rearrange("p k c -> p (k c)")
                    width = 2 * D // len(src)
                    for n, row in enumerate(src):
                        sp.dma_start(flat[:, width * n:width * (n + 1)], row.broadcast_to([P, width]))\
                            .then_inc(panel_in[g % RING], 16)

        def panel(eng, g):
            loads = sum(1 if panels[m][1] else len(panels[m][0]) for m in range(g % RING, g + 1, RING))
            eng.wait_ge(panel_in[g % RING], 16 * loads)
            return wring[:, g % RING, :, :]

        def ada_columns(pe, n):
            g = where["ada", n]
            w = panel(pe, g)
            if n in by_pe:
                for c2 in range(2):
                    for k in range(KD):
                        mm = pe.matmul(ps[:, 7, 2 * n + c2:2 * n + c2 + 1], w[:, k, c2 * P:(c2 + 1) * P], csig[:, k:k + 1],
                                       start=False, stop=(k == KD - 1), skip_group_check=True)
            else:
                pe.wait_ge(ada_sum, len([m for m in range(n + 1) if m not in by_pe]))
                for c2 in range(2):
                    mm = pe.matmul(ps[:, 7, 2 * n + c2:2 * n + c2 + 1], w[:, 0, c2 * P:(c2 + 1) * P], ones[:, 0:1],
                                   start=(n == 0 and c2 == 0), stop=True, skip_group_check=True)
            mm.then_inc(panel_used, 1)

        def ada_sums(dve, v, n, lo=0, hi=KD):
            w = panel(dve, where["ada", n])
            before = len([m for m in range(n) if m not in by_pe])
            if before and lo == 0:
                dve.wait_ge(ada_sum, before)
            for k in range(lo, hi):
                if k < 2:
                    ins = dve.tensor_scalar(ada_acc[:, k, :], w[:, k, :], csig[:, k:k + 1], None, ALU.mult)
                else:
                    dve.wait_ge(v.s, v.n - 1)
                    ins = dve.scalar_tensor_tensor(ada_acc[:, k % 2, :], w[:, k, :], csig[:, k:k + 1],
                                                   ada_acc[:, k % 2, :], ALU.mult, ALU.add)
                ins.then_inc(v.s, 1)
                v.n += 1
            if hi < KD:
                return
            dve.wait_ge(v.s, v.n)
            dve.tensor_tensor(w[:, 0, :], ada_acc[:, 0, :], ada_acc[:, 1, :], ALU.add).then_inc(ada_sum, 1)

        class Chain:

            def __init__(self, eng, s):
                self.eng, self.s, self.n = eng, s, 0

            def __call__(self, ins):
                ins.then_inc(self.s, 1)
                self.n += 1
                self.eng.wait_ge(self.s, self.n)
                return self.n

        x_v = x.rearrange("b (t p) d -> p (b t) d", p=P)
        BT = [region_c[:, 1024 * n:1024 * (n + 1)].rearrange("p (q s) -> p q s", q=SC) for n in (0, 1)]
        CT = [region_c[:, 1024 * n:1024 * (n + 1)].rearrange("p (q s) -> p q s", q=SC) for n in (2, 3)]

        with ExitStack() as one:
            def sem1(name):
                return one.enter_context(nc.semaphore(name))

            rows_in = sem1("rows_in")
            const_in = sem1("const_in")
            x_in = sem1("x_in")
            b_in = sem1("b_in")
            c_in = sem1("c_in")
            cz = sem1("cd_zeroed")
            ldt_wide = sem1("ldt_wide")
            rows_T = sem1("rows_T")
            rows_c = sem1("rows_copied")
            silu_e = sem1("silu_exp")
            silu_d = sem1("silu_done")
            dch = sem1("dve_chain1")
            var_ok = sem1("var_ready")
            sq_ok = sem1("sqrt_ready")
            xh_ok = sem1("xhat_ready")
            tr_ok = sem1("xT_in_psum")
            ev_ok = sem1("xT_copied")
            s5_ask = sem1("s5_asks_act")
            s5_act = sem1("s5_act_done")
            bd_ok = sem1("bd_ready")
            bt_ps = sem1("bt_in_psum")
            bt_ev = sem1("bt_copied")
            ct_ps = sem1("ct_in_psum")
            h_ok = sem1("hT_ready")
            rows = one.enter_context(nc.sbuf_tensor("rows", [P, 3, P], F32))
            Bn = one.enter_context(nc.sbuf_tensor("Bn", [P, 2, ST, GP], F32))
            Bt = region_a[:, 0:2048].rearrange("p (n f) -> p n f", n=4)
            Bd = region_a[:, 2048:4096].rearrange("p (n i e) -> p n i e", n=2, e=2 * GP)
            Cd = region_a[:, 4096:6144].rearrange("p (n q e) -> p n q e", n=2, e=P)

            with nc.Block() as block:
                @block.sync
                def _(sp):
                    sp.dma_start(kc[:, :], consts).then_inc(const_in, 16)
                    sp.dma_start(rows[0:96, 0, :], b_ada.rearrange("l (j p) -> (l j) p", p=P)).then_inc(rows_in, 16)
                    sp.dma_start(rows[96:112, 0, :], c.rearrange("b (j p) -> (b j) p", p=P)).then_inc(rows_in, 16)
                    sp.dma_start(rows[0:32, 1, :], lam_re.rearrange("l (i g) n -> (l i) (g n)", g=2)).then_inc(rows_in, 16)
                    sp.dma_start(rows[32:64, 1, :], lam_im.rearrange("l (i g) n -> (l i) (g n)", g=2)).then_inc(rows_in, 16)
                    sp.dma_start(small[64:96, 804:806], log_dt.rearrange("l (i g) -> (l i) g", g=2)).then_inc(rows_in, 16)
                    for n, vec in enumerate((g_attn, g_ssm, b_glu)):
                        sp.dma_start(rows[8 * n:8 * n + 8, 2, :], vec.rearrange("l (j p) -> (l j) p", p=P)).then_inc(rows_in, 16)
                    sp.dma_start(rows[24:32, 2, :], ssm_d.rearrange("l (j g) q -> (l j) (g q)", j=8)).then_inc(rows_in, 16)
                    load_panels(sp, 0, 1)
                    for t in range(TT):
                        sp.dma_start(resid[:, t, :], x_v[:, t, :]).then_inc(x_in, 16)
                    for n, b in enumerate((ssm_b_re, ssm_b_im)):
                        sp.dma_start(Bn[:, n], b.rearrange("l (i g) n q -> (g n) (l i) q", g=2)).then_inc(b_in, 16)
                    load_panels(sp, 1, 6)
                    sp.wait_ge(cz, 1)
                    for n, cc in enumerate((ssm_c_re, ssm_c_im)):
                        for r in range(8):
                            sp.dma_start(Cd[GP * r:GP * (r + 1), n, :, NS * (r % 2):NS * (r % 2) + NS],
                                         cc.rearrange("l (q r) e n -> r e (l q) n", r=8)[r]).then_inc(c_in, 16)
                    load_panels(sp, 6, first["u"] + RING)

                @block.gpsimd
                def _(pool):
                    pool.memset(Cd[:, :, :, :], 0.0).then_inc(cz, 1)
                    pool.memset(Bd[:, :, :, :], 0.0).then_inc(cz, 1)

                @block.scalar
                def _(act):
                    act.wait_ge(rows_T, 1)
                    act.copy(cT, ps[:, 0, 96:112]).then_inc(rows_c, 1)
                    act.wait_ge(rows_c, 1)
                    act.activation(csig, cT, ACT.Exp, scale=-1.0).then_inc(silu_e, 1)
                    act.wait_ge(s5_ask, 1)
                    act.activation(s5c[:, 0, :], lam[:, 64:96], ACT.Exp).then_inc(s5_act, 1)
                    act.wait_ge(s5_ask, 2)
                    act.activation(s5c[:, 3, :], s5c[:, 1, :], ACT.Exp).then_inc(s5_act, 1)
                    act.wait_ge(s5_ask, 3)
                    act.activation(s5c[:, 5, :], s5c[:, 4, :], ACT.Sin).then_inc(s5_act, 1)
                    act.activation(s5c[:, 6, :], s5c[:, 4, :], ACT.Sin, scale=0.5).then_inc(s5_act, 1)
                    act.wait_ge(var_ok, 1)
                    act.activation(rstd, rstd, ACT.Sqrt).then_inc(sq_ok, 1)
                    for n in range(16):
                        act.wait_ge(bt_ps, n + 1)
                        act.copy(BT[n // 8][:, n % 8, :], ps[:, n % 2, 0:P]).then_inc(bt_ev, 1)
                    for n in range(16):
                        act.wait_ge(ct_ps, n + 1)
                        q = n % 8
                        act.activation(CT[n // 8][:, q, :], ps[:, n % 2, 0:P], ACT.Copy,
                                       scale=1.0 - 2.0 * (n // 8)).then_inc(bt_ev, 1)
                    for k in range(KD):
                        act.wait_ge(tr_ok, k + 1)
                        act.copy(hT[:, k, :], ps[:, 2 + k % 4, :]).then_inc(ev_ok, 1)

                @block.vector
                def _(dve):
                    v = Chain(dve, dch)
                    dve.wait_ge(rows_in, 9 * 16)
                    for g in range(2):
                        ins = dve.tensor_copy(rows[64:96, 1, NS * g:NS * (g + 1)],
                                              small[64:96, 804 + g:805 + g].to_broadcast([32, NS]))
                        ins.then_inc(ldt_wide, 1)
                    dve.wait_ge(rows_T, 3)
                    v(dve.tensor_copy(lam, ps[:, 1, 0:96]))
                    v(dve.tensor_copy(vecs, ps[:, 2, 0:32]))
                    dve.wait_ge(silu_e, 1)
                    v(dve.tensor_scalar(csig, csig, 1.0, None, ALU.add))
                    v(dve.reciprocal(csig, csig))
                    v(dve.tensor_tensor(csig, csig, cT, ALU.mult))
                    v(dve.tensor_copy(modT, ps[:, 0, 0:96]))
                    dve.nop().then_inc(silu_d, 1)
                    ada_sums(dve, v, 0)
                    ada_sums(dve, v, 1)
                    dt, lrdt, th, mag, r = (s5c[:, n, :] for n in range(5))
                    sn, hs, w0, w1, w2, cr, ci, fh, fl, ar, ai = (s5c[:, n, :] for n in range(5, 16))
                    lr, li = lam[:, 0:32], lam[:, 32:64]
                    dve.nop().then_inc(s5_ask, 1)
                    dve.wait_ge(s5_act, 1)
                    v(dve.tensor_tensor(lrdt, lr, dt, ALU.mult))
                    dve.nop().then_inc(s5_ask, 1)
                    v(dve.tensor_tensor(th, li, dt, ALU.mult))
                    v(dve.tensor_scalar(w0, th, 1.0 / TWO_PI, ROUND, ALU.mult, ALU.add))
                    v(dve.tensor_scalar(w0, w0, -ROUND, None, ALU.add))
                    v(dve.scalar_tensor_tensor(r, w0, -C1, th, ALU.mult, ALU.add))
                    v(dve.scalar_tensor_tensor(r, w0, -C2, r, ALU.mult, ALU.add))
                    v(dve.scalar_tensor_tensor(r, w0, -C3, r, ALU.mult, ALU.add))
                    v(dve.tensor_scalar(r, r, PI_LOW, -PI_LOW, ALU.min, ALU.max))
                    dve.nop().then_inc(s5_ask, 1)
                    v(dve.tensor_scalar(w1, r, 1.0 / TWO_PI, None, ALU.mult))
                    v(dve.tensor_scalar(fh, w1, ROUND13, -ROUND13, ALU.add, ALU.add))
                    v(dve.tensor_tensor(fl, w1, fh, ALU.subtract))
                    dve.wait_ge(s5_act, 4)
                    v(dve.tensor_tensor(w0, hs, hs, ALU.mult))
                    v(dve.tensor_scalar(w0, w0, -2.0, 1.0, ALU.mult, ALU.add))
                    v(dve.tensor_tensor(ar, mag, w0, ALU.mult))
                    v(dve.tensor_tensor(ai, mag, sn, ALU.mult))
                    v(dve.tensor_scalar(ar, ar, -1.0, None, ALU.add))
                    v(dve.tensor_tensor(w0, lr, lr, ALU.mult))
                    v(dve.tensor_tensor(w1, li, li, ALU.mult))
                    v(dve.tensor_tensor(w0, w0, w1, ALU.add))
                    v(dve.reciprocal(w0, w0))
                    v(dve.tensor_tensor(w1, ar, lr, ALU.mult))
                    v(dve.tensor_tensor(w2, ai, li, ALU.mult))
                    v(dve.tensor_tensor(w1, w1, w2, ALU.add))
                    v(dve.tensor_tensor(cr, w1, w0, ALU.mult))
                    v(dve.tensor_tensor(w1, ai, lr, ALU.mult))
                    v(dve.tensor_tensor(w2, ar, li, ALU.mult))
                    v(dve.tensor_tensor(w1, w1, w2, ALU.subtract))
                    v(dve.tensor_tensor(ci, w1, w0, ALU.mult))
                    ada_sums(dve, v, 3)
                    ada_sums(dve, v, 4)
                    dve.wait_ge(b_in, 32)
                    dve.wait_ge(cz, 2)
                    wide = [z.unsqueeze(2).broadcast_to([P, ST, GP]) for z in (cr, ci)]
                    bt = [Bt[:, n].rearrange("p (i q) -> p i q", q=GP) for n in range(4)]
                    dve.tensor_tensor(bt[0], Bn[:, 0], wide[0], ALU.mult)
                    dve.tensor_tensor(bt[1], Bn[:, 1], wide[1], ALU.mult)
                    dve.tensor_tensor(bt[2], Bn[:, 1], wide[0], ALU.mult)
                    v(dve.tensor_tensor(bt[3], Bn[:, 0], wide[1], ALU.mult))
                    for g in range(2):
                        rr = slice(64 * g, 64 * g + 64)
                        dve.tensor_tensor(Bd[rr, 0, :, GP * g:GP * (g + 1)], bt[0][rr], bt[1][rr], ALU.subtract)\
                           .then_inc(bd_ok, 1)
                        dve.tensor_tensor(Bd[rr, 1, :, GP * g:GP * (g + 1)], bt[2][rr], bt[3][rr], ALU.add)\
                           .then_inc(bd_ok, 1)
                    for t in range(TT):
                        dve.wait_ge(x_in, 16 * TT)
                        for n in range(4):
                            ins = dve.bn_stats(stats[:, n, :], resid[:, t, 512 * n:512 * (n + 1)])
                        v(ins)
                        v(dve.bn_aggr(mv[:, t, :], stats[:, :, :]))
                        ada_sums(dve, v, (6, 7, 9, 10)[t])
                    v(dve.tensor_scalar(rstd, mv[:, :, 1], EPS, None, ALU.add))
                    dve.nop().then_inc(var_ok, 1)
                    dve.wait_ge(sq_ok, 1)
                    v(dve.reciprocal(rstd, rstd))
                    for t in range(TT):
                        dve.tensor_scalar(xhat[:, t, :], resid[:, t, :], mv[:, t, 0:1], rstd[:, t:t + 1],
                                          ALU.subtract, ALU.mult).then_inc(xh_ok, 1)
                    ada_sums(dve, v, 12)
                    ada_sums(dve, v, 14)
                    dve.wait_ge(panel_used, first["u"])
                    v(dve.tensor_tensor(modT[:, 0:32], modT[:, 0:32], ps[:, 7, 0:32], ALU.add))
                    v(dve.tensor_scalar(modT[:, 16:32], modT[:, 16:32], 1.0, None, ALU.add))
                    for k in range(KD):
                        dve.wait_ge(ev_ok, k + 1)
                        dve.tensor_scalar(hT[:, k, :], hT[:, k, :], modT[:, 16 + k:17 + k], modT[:, k:k + 1],
                                          ALU.mult, ALU.add).then_inc(h_ok, 1)

                @block.tensor
                def _(pe):
                    pe.wait_ge(const_in, 16)
                    pe.wait_ge(rows_in, 9 * 16)
                    pe.transpose(ps[:, 0, 0:112], rows[0:112, 0, :], ident[0:112, 0:112]).then_inc(rows_T, 1)
                    pe.wait_ge(ldt_wide, 2)
                    pe.transpose(ps[:, 1, 0:96], rows[0:96, 1, :], ident[0:96, 0:96]).then_inc(rows_T, 1)
                    pe.transpose(ps[:, 2, 0:32], rows[0:32, 2, :], ident[0:32, 0:32]).then_inc(rows_T, 1)
                    pe.wait_ge(silu_d, 1)
                    for g in range(first["u"]):
                        ada_columns(pe, g)
                        if g == 8:
                            pe.wait_ge(bd_ok, 4)
                            for n in range(16):
                                if n >= 2:
                                    pe.wait_ge(bt_ev, n - 1)
                                pe.transpose(ps[:, n % 2, 0:P], Bd[:, n // 8, 4 * (n % 8):4 * (n % 8) + 4, :]
                                             .rearrange("p a b -> p (a b)"), ident).then_inc(bt_ps, 1)
                            pe.wait_ge(c_in, 16 * 16)
                            for n in range(16):
                                pe.wait_ge(bt_ev, 15 + n)
                                pe.transpose(ps[:, n % 2, 0:P], Cd[:, n // 8, n % 8, :], ident).then_inc(ct_ps, 1)
                        if g == 12:
                            pe.wait_ge(xh_ok, TT)
                            for k in range(KD):
                                if k >= 4:
                                    pe.wait_ge(ev_ok, k - 3)
                                if k == 0:
                                    pe.wait_ge(bt_ev, 32)
                                for t in range(TT):
                                    mm = pe.transpose(ps[:, 2 + k % 4, P * t:P * (t + 1)], xhat[:, t, P * k:P * (k + 1)], ident)
                                mm.then_inc(tr_ok, 1)

        qT = resid[:, 0:2, :].rearrange("p a (m t) -> p (a m) t", t=T)
        kT = resid[:, 2:4, :].rearrange("p a (m t) -> p (a m) t", t=T)
        with ExitStack() as two:
            def sem2(name):
                return two.enter_context(nc.semaphore(name))

            u_ps = sem2("u_in_psum")
            u_ok = sem2("u_copied")
            turns = sem2("turns_ready")
            frac = sem2("fraction_ready")
            trig = sem2("trig_ready")
            act_in = sem2("act_chain2")
            bu_ps = sem2("bu_in_psum")
            rot_in = sem2("bu_rotated")
            summed = sem2("rotated_summed")
            scanned = sem2("state_scanned")
            rot_out = sem2("state_times_cos_and_sin")
            rot_pool = sem2("state_times_sin_and_cos")
            state = sem2("state_rotated_back")
            y_ps = sem2("y_in_psum")
            y_ok = sem2("y_ready")
            dch = sem2("dve_chain2")
            gelu = sem2("gelu_done")
            pos_in = sem2("positions_in")
            angle = sem2("angle_ready")
            sines = sem2("sines_ready")
            z_ps = sem2("z_in_psum")
            raw_ok = sem2("raw_copied")
            swap_ps = sem2("swapped_in_psum")
            roped = sem2("rotary_done")
            v_ps = sem2("v_in_psum")
            v_ok = sem2("v_copied")
            mag, fh, fl = (s5c[:, n, :] for n in (3, 12, 13))
            work = [[region_b[:, (8 * b + n) * T:(8 * b + n + 1) * T] for n in range(8)] for b in (0, 1)]
            rope = two.enter_context(nc.sbuf_tensor("rope", [P, 5, T], F32))
            sinT, cosT = rope[:, 0, :], rope[:, 1, :]
            raw = [rope[:, 2 + n, :] for n in range(2)]
            prod = rope[:, 4, :]

            with nc.Block() as block:
                @block.sync
                def _(sp):
                    sp.dma_start(prod.bitcast(I32), positions.broadcast_to([P, T])).then_inc(pos_in, 16)
                    load_panels(sp, first["u"] + RING, first["ada3"] + RING)

                @block.tensor
                def _(pe):
                    for m in range(SC):
                        w = panel(pe, where["u", m // 2])
                        if m >= 2:
                            pe.wait_ge(u_ok, m - 1)
                        for k in range(KD):
                            mm = pe.matmul(ps[:, m % 2, :], w[:, k, P * (m % 2):P * (m % 2) + P], hT[:, k, :],
                                           start=(k == 0), stop=(k == KD - 1))
                        mm.then_inc(u_ps, 1)
                        if m % 2:
                            pe.wait_ge(u_ps, m + 1)
                            pe.nop().then_inc(panel_used, 1)
                            ada_columns(pe, 16 + m // 2)

                    def project_in(i):
                        q, j = divmod(i, 4)
                        r = slice(32 * j, 32 * j + 32)
                        if i >= 2:
                            pe.wait_ge(rot_in, 4 * (i - 1))
                        for n in range(2):
                            mm = pe.matmul(ps[:, 2 * (i % 2) + n, :], BT[n][r, q, :], uT[r, q, :], start=True, stop=True)
                        mm.then_inc(bu_ps, 1)

                    def project_out(i):
                        q, j = divmod(i, 4)
                        w = work[i % 2]
                        pe.wait_ge(state, 2 * (i + 1))
                        if j == 0 and q >= 1:
                            pe.wait_ge(y_ok, q)
                        r = slice(32 * j, 32 * j + 32)
                        for n, s in enumerate((5, 4)):
                            mm = pe.matmul(ps[r, 4, :], CT[n][:, q, 32 * j:32 * j + 32], w[s], start=(n == 0), stop=(n == 1))
                        mm.then_inc(y_ps, 1)

                    def project_qk(m, half):
                        w = panel(pe, where["qkv", m // 2])
                        if half == 0 and m >= 2:
                            pe.wait_ge(roped, m - 1)
                        for k in range(8 * half, 8 * half + 8):
                            mm = pe.matmul(ps[:, 5 + m % 2, :], w[:, k, P * (m % 2):P * (m % 2) + P], hT[:, k, :],
                                           start=(k == 0), stop=(k == KD - 1))
                        if half:
                            mm.then_inc(z_ps, 1)

                    def turn_pairs(m):
                        pe.wait_ge(raw_ok, m + 1)
                        pe.matmul(ps[:, 5 + m % 2, :], swap, raw[m % 2], start=True, stop=True).then_inc(swap_ps, 1)

                    pe.wait_ge(u_ok, SC)
                    project_in(0)
                    for i in range(ST):
                        m = i // 2
                        if i + 1 < ST:
                            project_in(i + 1)
                        if i >= 1:
                            project_out(i - 1)
                        project_qk(m, i % 2)
                        if i % 2 == 0 and m >= 1:
                            turn_pairs(m - 1)
                        if i % 4 == 3:
                            pe.wait_ge(z_ps, m + 1)
                            pe.nop().then_inc(panel_used, 1)
                        if i % 4 == 2 and i >= 6:
                            ada_columns(pe, 20 + i // 4 - 1)
                    project_out(ST - 1)
                    turn_pairs(15)
                    ada_columns(pe, 27)
                    pe.wait_ge(y_ps, ST)
                    for n in range(16):
                        pv, t = divmod(n, TT)
                        w = panel(pe, where["qkv", 8 + pv])
                        if n >= 2:
                            pe.wait_ge(v_ok, n - 1)
                        if n == 0:
                            pe.wait_ge(roped, 16)
                        bank = 5 if n % 2 == 0 else 3
                        for k in range(KD):
                            mm = pe.matmul(ps[:, bank, 0:PC], hT[:, k, P * t:P * (t + 1)], w[:, k, :],
                                           start=(k == 0), stop=(k == KD - 1))
                        mm.then_inc(v_ps, 1)
                        if t == TT - 1:
                            pe.wait_ge(v_ps, n + 1)
                            pe.nop().then_inc(panel_used, 1)
                            ada_columns(pe, 28 + pv)

                @block.scalar
                def _(act):
                    act.wait_ge(angle, 1)
                    act.activation(cosT, sinT, ACT.Sin, scale=0.5).then_inc(sines, 1)
                    act.wait_ge(sines, 1)
                    act.activation(sinT, sinT, ACT.Sin).then_inc(sines, 1)

                    def whole_turns(i):
                        w = work[i % 2]
                        if i >= 2:
                            act.wait_ge(trig, 4 * (i - 1))
                        act.activation(w[0], times, ACT.Copy, bias=ROUND, scale=s5c[:, 14, i:i + 1]).then_inc(act_in, 1)
                        act.wait_ge(act_in, i + 1)
                        act.activation(w[0], w[0], ACT.Copy, bias=-ROUND).then_inc(turns, 1)

                    def sine_cosine(i):
                        w = work[i % 2]
                        act.wait_ge(frac, i + 1)
                        act.activation(w[0], w[1], ACT.Sin, scale=TWO_PI / 2).then_inc(trig, 1)
                        if i >= 2:
                            act.wait_ge(rot_out, 2 * (i - 1))
                            act.wait_ge(rot_pool, 2 * (i - 1))
                        act.activation(w[2], w[1], ACT.Sin, scale=TWO_PI).then_inc(trig, 1)
                        act.wait_ge(trig, 4 * i + 2)
                        act.activation(w[0], w[0], ACT.Square).then_inc(trig, 1)
                        act.wait_ge(trig, 4 * i + 3)
                        act.activation(w[3], w[0], ACT.Copy, bias=1.0, scale=-2.0).then_inc(trig, 1)

                    act.wait_ge(dch, 1)
                    whole_turns(0)
                    whole_turns(1)
                    sine_cosine(0)
                    for m in range(SC):
                        act.wait_ge(u_ps, m + 1)
                        act.copy(uT[:, m, :], ps[:, m % 2, :]).then_inc(u_ok, 1)
                    for i in range(ST):
                        if i + 1 < ST:
                            sine_cosine(i + 1)
                        if i + 2 < ST:
                            whole_turns(i + 2)
                        if i % 2:
                            m = i // 2
                            act.wait_ge(z_ps, m + 1)
                            if m >= 2:
                                act.wait_ge(roped, m - 1)
                                act.wait_ge(swap_ps, m - 1)
                            act.copy(raw[m % 2], ps[:, 5 + m % 2, :]).then_inc(raw_ok, 1)
                    for n in range(16):
                        act.wait_ge(v_ps, n + 1)
                        pv, t = divmod(n, TT)
                        act.copy(v_tok[:, t, PC * pv:PC * (pv + 1)], ps[:, 5 if n % 2 == 0 else 3, 0:PC]).then_inc(v_ok, 1)
                    act.wait_ge(y_ok, SC)
                    for q in range(SC):
                        act.activation(uT[:, q, :], uT[:, q, :], ACT.Gelu).then_inc(gelu, 1)

                @block.gpsimd
                def _(pool):
                    for i in range(ST):
                        w = work[i % 2]
                        pool.wait_ge(rot_in, 4 * (i + 1))
                        pool.tensor_tensor(w[4], w[4], w[5], ALU.add).then_inc(summed, 1)
                        pool.tensor_tensor(w[6], w[6], w[7], ALU.subtract).then_inc(summed, 1)
                        pool.wait_ge(rot_out, 2 * (i + 1))
                        pool.tensor_tensor(w[4], w[2], w[4], ALU.mult).then_inc(rot_pool, 1)
                        pool.tensor_tensor(w[6], w[3], w[6], ALU.mult).then_inc(rot_pool, 1)
                        pool.tensor_tensor(w[5], w[5], w[7], ALU.subtract).then_inc(state, 1)
                        pool.wait_ge(rot_pool, 2 * (i + 1))
                        pool.tensor_tensor(w[4], w[4], w[6], ALU.add).then_inc(state, 1)

                @block.vector
                def _(dve):
                    v = Chain(dve, dch)
                    v(dve.tensor_tensor(s5c[:, 14, :], fh, fl, ALU.add))

                    def fraction(i):
                        w = work[i % 2]
                        dve.wait_ge(turns, i + 1)
                        v(dve.scalar_tensor_tensor(w[1], times, fh[:, i:i + 1], w[0], ALU.mult, ALU.subtract))
                        v(dve.scalar_tensor_tensor(w[1], times, fl[:, i:i + 1], w[1], ALU.mult, ALU.add))
                        dve.tensor_scalar(w[1], w[1], HALF_TURN, -HALF_TURN, ALU.min, ALU.max).then_inc(frac, 1)

                    dve.wait_ge(pos_in, 16)
                    a, w = raw[0], raw[1]
                    v(dve.tensor_copy(a, prod.bitcast(I32)))
                    v(dve.tensor_scalar(a, a, kc[:, K_FREQ:K_FREQ + 1], None, ALU.mult))
                    v(dve.tensor_scalar(w, a, 1.0 / TWO_PI, ROUND, ALU.mult, ALU.add))
                    v(dve.tensor_scalar(w, w, -ROUND, None, ALU.add))
                    for part in (C1, C2, C3):
                        v(dve.scalar_tensor_tensor(a, w, -part, a, ALU.mult, ALU.add))
                    dve.tensor_scalar(sinT, a, PI_LOW, -PI_LOW, ALU.min, ALU.max).then_inc(angle, 1)
                    dve.wait_ge(sines, 2)
                    v(dve.tensor_tensor(cosT, cosT, cosT, ALU.mult))
                    v(dve.tensor_scalar(cosT, cosT, -2.0, 1.0, ALU.mult, ALU.add))
                    fraction(0)
                    fraction(1)
                    for n in range(16, 20):
                        ada_sums(dve, v, n)

                    def rotate_in(i):
                        w = work[i % 2]
                        dve.wait_ge(trig, 4 * (i + 1))
                        dve.wait_ge(bu_ps, i + 1)
                        if i >= 2:
                            dve.wait_ge(y_ps, i - 1)
                        br, bi = ps[:, 2 * (i % 2), :], ps[:, 2 * (i % 2) + 1, :]
                        for dst, tr, b in ((4, 3, br), (5, 2, bi), (6, 3, bi), (7, 2, br)):
                            dve.tensor_tensor(w[dst], w[tr], b, ALU.mult).then_inc(rot_in, 1)

                    def scan(i):
                        w = work[i % 2]
                        dve.wait_ge(summed, 2 * (i + 1))
                        m = mag[:, i:i + 1].to_broadcast([P, T])
                        for s in (4, 6):
                            dve.tensor_tensor_scan(w[s], m, w[s], 0.0, ALU.mult, ALU.add).then_inc(scanned, 1)

                    def rotate_out(i):
                        w = work[i % 2]
                        dve.wait_ge(scanned, 2 * (i + 1))
                        dve.tensor_tensor(w[5], w[3], w[4], ALU.mult).then_inc(rot_out, 1)
                        dve.tensor_tensor(w[7], w[2], w[6], ALU.mult).then_inc(rot_out, 1)

                    def rotary(m):
                        dst = (qT if m < 8 else kT)[:, m % 8, :]
                        dve.wait_ge(raw_ok, m + 1)
                        if m >= 1:
                            dve.wait_ge(roped, m)
                        v(dve.tensor_tensor(prod, raw[m % 2], cosT, ALU.mult))
                        dve.wait_ge(swap_ps, m + 1)
                        v(dve.tensor_tensor(dst, ps[:, 5 + m % 2, :], sinT, ALU.mult))
                        dve.tensor_tensor(dst, prod, dst, ALU.add).then_inc(roped, 1)

                    def add_skip(q):
                        dve.wait_ge(y_ps, 4 * (q + 1))
                        dve.scalar_tensor_tensor(uT[:, q, :], uT[:, q, :], d_c[:, q:q + 1], ps[:, 4, :],
                                                 ALU.mult, ALU.add).then_inc(y_ok, 1)

                    rotate_in(0)
                    for i in range(ST):
                        scan(i)
                        rotate_out(i)
                        if i % 4 == 0 and i >= 4:
                            add_skip(i // 4 - 1)
                        if i + 1 < ST:
                            rotate_in(i + 1)
                        if i + 2 < ST:
                            fraction(i + 2)
                        if i % 2 == 1 and i >= 3:
                            rotary(i // 2 - 1)
                        if i >= 1:
                            ada_sums(dve, v, 20 + (i - 1) // 4, 4 * ((i - 1) % 4), 4 * ((i - 1) % 4) + 4)
                    ada_sums(dve, v, 27, 12)
                    rotary(15)
                    add_skip(SC - 1)
                    for n in range(28, 32):
                        ada_sums(dve, v, n)

        attn = region_a[:, 0:4096].rearrange("p (t d) -> p t d", t=TT)
        attnT = region_a[:, 4096:8192].rearrange("p (m t) -> p m t", m=8)
        with ExitStack() as four:
            def sem4(name):
                return four.enter_context(nc.semaphore(name))

            prob = [region_b[:, T * n:T * (n + 1)] for n in range(4)]
            probT = [region_b[:, T * n:T * (n + 1)] for n in range(4, 8)]
            s_ps = sem4("scores_in_psum")
            masked = sem4("scores_masked")
            negmax = sem4("negmax_ready")
            p_ok = sem4("probs_ready")
            t_ps = sem4("probsT_in_psum")
            t_ok = sem4("probsT_copied")
            o_ps = sem4("out_in_psum")
            o_ok = sem4("out_scaled")
            inv = sem4("inverse_sum")
            dch = sem4("dve_chain4")
            var_ok = sem4("attn_square_mean")
            sq_ok = sem4("attn_root")
            norm_ok = sem4("attn_normed")
            mod_rT = sem4("mod_turned")
            mod_ev = sem4("mod_rows_copied")
            mod_st = sem4("mod_rows_stored")
            modr = four.enter_context(nc.sbuf_tensor("modr", [96, P], F32))
            aT_ps = sem4("attnT_in_psum")
            aT_ok = sem4("attnT_copied")
            N = HEADS * TT
            mx, nm, lsum, linv = (small[:, 824 + 8 * n:832 + 8 * n] for n in range(4))

            with nc.Block() as block:
                @block.sync
                def _(sp):
                    load_panels(sp, first["ada3"] + RING, first["glu"] + RING)
                    sp.wait_ge(mod_ev, 1)
                    sp.dma_start(mod_rows, modr[:, :]).then_inc(mod_st, 16)
                    sp.wait_ge(mod_st, 16)

                @block.tensor
                def _(pe):
                    def scores(n):
                        h, i = divmod(n, TT)
                        r = slice(HD * (h % 2), HD * (h % 2) + HD)
                        if n >= 2:
                            pe.wait_ge(masked, n - 1)
                        pe.matmul(ps[:, n % 2, 0:P * (i + 1)], qT[r, h // 2, P * i:P * (i + 1)],
                                  kT[r, h // 2, 0:P * (i + 1)], start=True, stop=True).then_inc(s_ps, 1)

                    def turn(n):
                        i = n % TT
                        pe.wait_ge(p_ok, n + 1)
                        if n >= 2:
                            pe.wait_ge(t_ok, n - 1)
                        for b in range(i + 1):
                            mm = pe.transpose(ps[:, 2 + n % 2, P * b:P * (b + 1)], prob[n % 4][:, P * b:P * (b + 1)], ident)
                        mm.then_inc(t_ps, 1)

                    def weigh(n):
                        h, i = divmod(n, TT)
                        pe.wait_ge(t_ok, n + 1)
                        if n >= 2:
                            pe.wait_ge(o_ok, n - 1)
                        for b in range(i + 1):
                            mm = pe.matmul(ps[:, 4 + n % 2, 0:HD], probT[n % 4][:, P * b:P * (b + 1)],
                                           v_tok[:, b, HD * h:HD * (h + 1)], start=(b == 0), stop=(b == i))
                        mm.then_inc(o_ps, 1)

                    for n in range(N + 3):
                        if n < N:
                            scores(n)
                        if 2 <= n < N + 2:
                            turn(n - 2)
                        if n >= 3:
                            weigh(n - 3)
                        if n % 4 == 1 and 5 <= n < N + 4:
                            ada_columns(pe, 32 + n // 4 - 1)
                    pe.wait_ge(mod_rT, 1)
                    pe.transpose(ps[0:96, 6, 0:P], modT, ident).then_inc(mod_rT, 1)
                    pe.wait_ge(norm_ok, TT)
                    for m in range(8):
                        if m >= 2:
                            pe.wait_ge(aT_ok, m - 1)
                        for t in range(TT):
                            mm = pe.transpose(ps[:, m % 2, P * t:P * (t + 1)], attn[:, t, P * m:P * (m + 1)], ident)
                        mm.then_inc(aT_ps, 1)

                @block.scalar
                def _(act):
                    for n in range(N + 2):
                        if n < N:
                            w = P * (n % TT + 1)
                            act.wait_ge(negmax, n + 1)
                            if n >= 8:
                                act.wait_ge(inv, n - 7)
                            act.activation(prob[n % 4][:, 0:w], prob[n % 4][:, 0:w], ACT.Exp, bias=nm[:, n % 8:n % 8 + 1],
                                           accum_out=lsum[:, n % 8:n % 8 + 1]).then_inc(p_ok, 1)
                        m = n - 2
                        if m >= 0:
                            w = P * (m % TT + 1)
                            act.wait_ge(t_ps, m + 1)
                            if m >= 4:
                                act.wait_ge(o_ps, m - 3)
                            act.copy(probT[m % 4][:, 0:w], ps[:, 2 + m % 2, 0:w]).then_inc(t_ok, 1)
                    act.wait_ge(mod_rT, 2)
                    act.copy(modr[:, :], ps[0:96, 6, 0:P]).then_inc(mod_ev, 1)
                    act.wait_ge(var_ok, 1)
                    act.activation(rstd, rstd, ACT.Sqrt).then_inc(sq_ok, 1)
                    for m in range(8):
                        act.wait_ge(aT_ps, m + 1)
                        act.activation(attnT[:, m, :], ps[:, m % 2, :], ACT.Copy, scale=g_attn_c[:, m:m + 1]).then_inc(aT_ok, 1)

                @block.vector
                def _(dve):
                    v = Chain(dve, dch)

                    def mask(n):
                        i = n % TT
                        w = P * (i + 1)
                        dve.wait_ge(s_ps, n + 1)
                        if n >= 4:
                            dve.wait_ge(t_ps, n - 3)
                        if n >= 8:
                            dve.wait_ge(p_ok, n - 7)
                        dve.tensor_tensor_reduce(prob[n % 4][:, 0:w], ps[:, n % 2, 0:w],
                                                 kc[:, K_MASK + T * i:K_MASK + T * i + w], HD ** -0.5, 3.0 * NEG,
                                                 ALU.add, ALU.max, mx[:, n % 8:n % 8 + 1]).then_inc(masked, 1)
                        dve.wait_ge(masked, n + 1)
                        dve.tensor_scalar(nm[:, n % 8:n % 8 + 1], mx[:, n % 8:n % 8 + 1], -1.0, None, ALU.mult).then_inc(negmax, 1)

                    def scale(n):
                        h, i = divmod(n, TT)
                        dve.wait_ge(p_ok, n + 1)
                        dve.reciprocal(linv[:, n % 8:n % 8 + 1], lsum[:, n % 8:n % 8 + 1]).then_inc(inv, 1)
                        dve.wait_ge(inv, n + 1)
                        dve.wait_ge(o_ps, n + 1)
                        dve.tensor_scalar(attn[:, i, HD * h:HD * (h + 1)], ps[:, 4 + n % 2, 0:HD], linv[:, n % 8:n % 8 + 1],
                                          None, ALU.mult).then_inc(o_ok, 1)

                    for n in range(N + 4):
                        if n < N:
                            mask(n)
                        if n >= 4:
                            scale(n - 4)
                        if n < N:
                            ada_sums(dve, v, 32 + n // 4, 4 * (n % 4), 4 * (n % 4) + 4)
                    dve.wait_ge(panel_used, first["glu"])
                    v(dve.tensor_tensor(modT[:, 32:96], modT[:, 32:96], ps[:, 7, 32:96], ALU.add))
                    v(dve.tensor_scalar(modT[:, 32:48], modT[:, 32:48], 1.0, None, ALU.add))
                    v(dve.tensor_scalar(modT[:, 64:96], modT[:, 64:96], 1.0, None, ALU.add))
                    dve.nop().then_inc(mod_rT, 1)
                    dve.wait_ge(o_ok, N)
                    dve.wait_ge(t_ps, N)
                    junk = region_b[:, 8 * T:8 * T + AW]
                    for t in range(TT):
                        v(dve.tensor_tensor_reduce(junk, attn[:, t, :], attn[:, t, :], 1.0 / AW, 0.0, ALU.mult, ALU.add,
                                                   rstd[:, t:t + 1]))
                    v(dve.tensor_scalar(rstd, rstd, EPS, None, ALU.add))
                    dve.nop().then_inc(var_ok, 1)
                    dve.wait_ge(sq_ok, 1)
                    v(dve.reciprocal(rstd, rstd))
                    for t in range(TT):
                        dve.tensor_scalar(attn[:, t, :], attn[:, t, :], rstd[:, t:t + 1], None, ALU.mult).then_inc(norm_ok, 1)

        y2T = region_c[:, 0:4096].rearrange("p (m t) -> p m t", m=SC)
        row_g1 = region_a[:, 0:D]
        keysT = sb("keysT", [P, 2, NK])
        x_in2 = sem("x_in_again")
        row_in1 = sem("gate1_row_in")
        with ExitStack() as five:
            def sem5(name):
                return five.enter_context(nc.semaphore(name))

            buf = five.enter_context(nc.sbuf_tensor("glu_buf", [P, 4, T], F32))
            keys = five.enter_context(nc.sbuf_tensor("keys", [P, 2, NK], F32))
            sg = [buf[:, n, :] for n in range(2)]
            sq = [buf[:, 2 + n, :] for n in range(2)]
            gate_ps = sem5("gate_in_psum")
            gate_ok = sem5("gate_ready")
            y2_ok = sem5("gated")
            sq2_ok = sem5("squares_ready")
            sum_ps = sem5("square_sums")
            dch = sem5("dve_chain5")
            ask = sem5("root_asked")
            root = sem5("root_ready")
            keys_in = sem5("keys_in")
            keys_ps = sem5("keysT_in_psum")
            keys_ok = sem5("keysT_copied")

            with nc.Block() as block:
                @block.sync
                def _(sp):
                    sp.dma_start(keys[:, :, :], sub_keys.rearrange("l i k c -> k (l i) c")).then_inc(keys_in, 16)
                    load_panels(sp, first["glu"] + RING, first["glu"] + 4)
                    for t in range(TT):
                        sp.dma_start(resid[:, t, :], x_v[:, t, :]).then_inc(x_in2, 16)
                    sp.dma_start(row_g1, mod_flat[:, 32 * P:32 * P + D].broadcast_to([P, D])).then_inc(row_in1, 16)
                    load_panels(sp, first["glu"] + 4, first["out"] + RING)

                @block.tensor
                def _(pe):
                    def sum_squares(m):
                        pe.wait_ge(sq2_ok, m + 1)
                        mm = pe.matmul(ps[:, 2, :], ones, sq[m % 2], start=(m == 0), stop=(m == SC - 1))
                        mm.then_inc(sum_ps, 1)

                    pe.wait_ge(keys_in, 16)
                    for n in range(2):
                        pe.transpose(ps[:, 4 + n, 0:NK], keys[:, n, :], ident).then_inc(keys_ps, 1)
                    for m in range(SC):
                        w = panel(pe, where["glu", m // 2])
                        if m >= 2:
                            pe.wait_ge(gate_ok, m - 1)
                        for k in range(SC):
                            mm = pe.matmul(ps[:, m % 2, :], w[:, k, P * (m % 2):P * (m % 2) + P], uT[:, k, :],
                                           start=(k == 0), stop=(k == SC - 1))
                        mm.then_inc(gate_ps, 1)
                        if m % 2:
                            pe.wait_ge(gate_ps, m + 1)
                            pe.nop().then_inc(panel_used, 1)
                        if m >= 1:
                            sum_squares(m - 1)
                    sum_squares(SC - 1)

                @block.scalar
                def _(act):
                    for n in range(2):
                        act.wait_ge(keys_ps, n + 1)
                        act.copy(keysT[:, n, :], ps[:, 4 + n, 0:NK]).then_inc(keys_ok, 1)
                    for m in range(SC):
                        act.wait_ge(gate_ps, m + 1)
                        if m >= 2:
                            act.wait_ge(y2_ok, m - 1)
                        act.activation(sg[m % 2], ps[:, m % 2, :], ACT.Sigmoid, bias=b_glu_c[:, m:m + 1]).then_inc(gate_ok, 1)
                        act.wait_ge(y2_ok, m + 1)
                        if m >= 2:
                            act.wait_ge(sum_ps, m - 1)
                        act.activation(sq[m % 2], y2T[:, m, :], ACT.Square).then_inc(sq2_ok, 1)
                    act.wait_ge(ask, 1)
                    act.activation(sq[0], sq[0], ACT.Sqrt).then_inc(root, 1)

                @block.vector
                def _(dve):
                    v = Chain(dve, dch)
                    for m in range(SC):
                        dve.wait_ge(gate_ok, m + 1)
                        dve.tensor_tensor(y2T[:, m, :], uT[:, m, :], sg[m % 2], ALU.mult).then_inc(y2_ok, 1)
                    dve.wait_ge(sum_ps, SC)
                    v(dve.tensor_scalar(sq[0], ps[:, 2, :], 1.0 / SW, EPS, ALU.mult, ALU.add))
                    dve.nop().then_inc(ask, 1)
                    dve.wait_ge(root, 1)
                    v(dve.reciprocal(sq[0], sq[0]))
                    for m in range(SC):
                        dve.scalar_tensor_tensor(y2T[:, m, :], y2T[:, m, :], g_ssm_c[:, m:m + 1], sq[0], ALU.mult, ALU.mult)\
                           .then_inc(y2_ok, 1)

        GROUPS = ((0,), (1, 2, 3))
        acc = [region_a[:, D * n:D * (n + 1)] for n in range(2)]
        h2_cur = region_c[:, 4096:4096 + D]
        h2T_first = region_c[:, 4096 + D:8192].rearrange("p (k t) -> p k t", k=KD)
        h2T_rest = area[:, 4096:4096 + KD * 3 * P].rearrange("p (k t) -> p k t", k=KD)
        h2_at = [h2_cur, region_a[:, 0:D], h2_cur, h2_cur]
        h2_work = [region_a[:, D:2 * D], region_c[:, D:2 * D]]
        scores = resid[:, :, :].rearrange("p t (m k) -> p t m k", k=NK)
        wflat = wring[:, :, :, :].rearrange("p r k c -> p (r k c)")
        row_g2, row_lg2, row_lb2, x1_cur = (wflat[:, D * n:D * (n + 1)] for n in range(4))
        outb = acc[1]
        expert_rows = [region_b[:, D * n:D * (n + 1)] for n in range(NB)]
        v_buf = [resid[:, n, :] for n in range(2)] + [wflat[:, 4 * D:5 * D]]
        VB = len(v_buf)
        hot_b = [wflat[:, 5 * D + 1024 * n:5 * D + 1024 * (n + 1)].rearrange("p (t b) -> p t b", t=8) for n in range(2)]
        hot_a = kc[:, K_MASK:K_MASK + 64 * QROWS].rearrange("p (h t a) -> p h t a", h=2, a=QROWS)
        slot_rows = kc[:, K_MASK:K_MASK + 6 * P].rearrange("p (n t s) -> p n t s", n=3, t=2)
        matrix = area[:, 4096:4096 + QROWS * 2 * P].rearrange("p (a t) -> p a t", a=QROWS)
        late = [kc[:, K_TIME:K_TIME + 512], ada_acc[:, :, :].rearrange("p a b -> p (a b)")]
        dense_sum = [h2_cur, region_c[:, 4096 + D:8192]]
        dense_x1 = [resid[:, n, :] for n in range(2)]
        mixw = ada_acc
        gates = small[:, 256:256 + TT * SLOTS].rearrange("p (t s) -> p t s", t=TT)
        x1_v = x1_rows.rearrange("(t p) d -> p t d", p=P)
        h2_v = h2_rows.rearrange("(t p) d -> p t d", p=P)
        out_v = out.rearrange("b (t p) d -> p (b t) d", p=P)
        tables = (expert_u.rearrange("l e d -> (l e) d"), expert_v.rearrange("l e d -> (l e) d"))
        with ExitStack() as six:
            def sem6(name):
                return six.enter_context(nc.semaphore(name))

            def sb6(name, shape, dt=F32):
                return six.enter_context(nc.sbuf_tensor(name, shape, dt))

            picks = sb6("picks", [P, TT, SLOTS], U32)
            qm = sb6("qm", [P, 2, 3 * P])
            slot_T = qm[:, :, :].rearrange("p a b -> p (a b)").rearrange("p (n t) -> p n t", n=3)
            cand = sb6("cand", [P, 2, TOPK, TOPK])[:, :, :, :]
            topi = sb6("topi", [P, 2 * PH, TOPK], U32)
            top = sb6("top", [P, 2 * PH, TOPK])
            topf = sb6("topf", [P, 2, TOPK])
            best = sb6("best", [P, PH, TOPK])
            besti = sb6("besti", [P, PH, TOPK], U32)
            half_u = sb6("half_u", [P, 2, TOPK], U32)
            half_f = sb6("half_f", [P, 2, TOPK])
            side = sb6("side", [P, 2, TOPK])[:, :, :]
            gsum = sb6("gsum", [P, PH, 1])[:, :, :]
            dots = sb6("dots", [P, NB])
            hiddens = [sb6(f"hidden{n}", [P, SLOTS])[:, :] for n in range(2)]
            coef = small[:, 128:128 + SLOTS]
            index = sb6("index", [P, NB], U32)
            spare = sb6("spare", [1, 2])
            mix_ps = sem6("mix_in_psum")
            scaled = sem6("mix_scaled")
            mix_ok = sem6("mix_used")
            ask = sem6("root_asked6")
            root = sem6("root_ready6")
            x1_ok = sem6("x1_ready")
            x1_st = sem6("x1_stored")
            xh_ok = sem6("xhat2_ready")
            tr_ok = sem6("h2T_in_psum")
            ev_ok = sem6("h2T_copied")
            h2_ok = sem6("h2_ready")
            h2_st = [sem6(f"h2_stored{n}") for n in range(2)]
            slots_ok = sem6("slot_rows_ready")
            slots_ps = sem6("slots_in_psum")
            slots_T_ok = sem6("slots_turned")
            square_ok = sem6("squared_distances")
            b_ok = sem6("hot_b_ready")
            b_used = sem6("hot_b_used")
            a_ok = sem6("hot_a_ready")
            m_ok = sem6("matrix_copied")
            v_in = [sem6(f"v_rows_in{n}") for n in range(VB)]
            v_used = sem6("v_rows_used")
            block_ps = sem6("block_in_psum")
            late_ok = sem6("late_banks_added")
            dense_x1_in = sem6("dense_x1_in")
            dense_ok = sem6("dense_out_ready")
            dense_st = sem6("dense_out_stored")
            q_ps = sem6("query_in_psum")
            q_ok = sem6("query_copied")
            k_ps = sem6("key_scores_in_psum")
            k_ok = sem6("key_scores_copied")
            gate_a = sem6("gate_asked")
            gate_e = sem6("gate_exp")
            picked = sem6("head_experts_picked")
            spare_ok = sem6("spare_zeroed")
            row_in = [sem6(f"row_in{b}") for b in range(NB)]
            row_used = sem6("row_used")
            index_ok = sem6("index_ready")
            dot_ok = sem6("dots_kept")
            hid_ok = sem6("hidden_ready")
            act_ok = sem6("gelu_ready")
            h2_in = [sem6(f"h2_in{t}") for t in range(TT)]
            x1_in = sem6("x1_in")
            rows_in = sem6("rows_in6")
            out_ok = sem6("out_ready")
            out_st = sem6("out_stored")
            dch = sem6("dve_chain6")

            MATRIX_STEPS = (((0, 1, 3, 4), 12), ((12, 13, 16, 18), 26), ((26, 27, 28, 29), 40), ((40, 41, 43, 44), 53))
            PASSES = ((0, 0), (1, 0), (2, 0), (2, 1), (3, 0), (3, 1))
            TURNS = SLOTS // NB

            with nc.Block() as block:
                @block.sync
                def _(sp):
                    load_panels(sp, first["out"] + RING, where["qp", 0] + 1)
                    sp.wait_ge(x1_ok, 1)
                    sp.dma_start(x1_v[:, 0, :], resid[:, 0, :]).then_inc(x1_st, 16)
                    load_panels(sp, where["qp", 0] + 1, where["qp", 8] + 1)
                    for t in range(1, TT):
                        sp.wait_ge(x1_ok, t + 1)
                        sp.dma_start(x1_v[:, t, :], resid[:, t, :]).then_inc(x1_st, 16)
                    load_panels(sp, where["qp", 8] + 1, where["qp", 8] + 2)
                    for t in range(1, TT):
                        sp.wait_ge(h2_ok, t + 1)
                        sp.dma_start(h2_v[:, t, :], h2_work[t % 2]).then_inc(h2_st[t % 2], 16)
                    load_panels(sp, where["qp", 8] + 2, where["qp", 8] + 3)
                    sp.wait_ge(h2_st[1], 32)
                    sp.wait_ge(h2_st[0], 16)
                    sp.dma_start(h2_at[1], h2_v[:, 1, :]).then_inc(h2_in[1], 16)
                    load_panels(sp, where["qp", 8] + 3, first["end"])
                    sp.wait_ge(panel_used, first["end"])
                    for dst, src in ((row_g2, mod_flat[:, 80 * P:80 * P + D]), (row_lg2, ln2_g), (row_lb2, ln2_b)):
                        sp.dma_start(dst, src.broadcast_to([P, D])).then_inc(rows_in, 16)
                    sp.wait_ge(x1_st, 16 * TT)
                    sp.wait_ge(hid_ok, 1)
                    sp.dma_start(h2_at[2], h2_v[:, 2, :]).then_inc(h2_in[2], 16)
                    sp.wait_ge(picked, 2 * PH)
                    for b in range(VB):
                        sp.dma_start(v_buf[b], tables[1][P * b:P * (b + 1), :]).then_inc(v_in[b], 16)
                    with sp.Fori(1, NK // VB) as it:
                        for b in range(VB):
                            sp.wait_ge(v_used, it * VB + (b - VB + 1))
                            sp.dma_start(v_buf[b], tables[1][bass.ds(it * (VB * P) + P * b, P), :]).then_inc(v_in[b], 16)
                    for a in range(NK // VB * VB, NK):
                        sp.wait_ge(v_used, a - VB + 1)
                        sp.dma_start(v_buf[a % VB], tables[1][P * a:P * (a + 1), :]).then_inc(v_in[a % VB], 16)
                    sp.wait_ge(v_used, NK)
                    for n in range(2):
                        sp.dma_start(dense_x1[n], x1_v[:, n, :]).then_inc(dense_x1_in, 16)
                    for n in range(2):
                        sp.wait_ge(dense_ok, n + 1)
                        sp.dma_start(out_v[:, n, :], dense_sum[n]).then_inc(dense_st, 16)
                    sp.wait_ge(dense_st, 32)

                @block.tensor
                def _(pe):
                    def score(grp, m):
                        n = 16 * grp + m
                        pe.wait_ge(q_ok, n + 1)
                        if m >= 2:
                            pe.wait_ge(k_ok, n - 1)
                        for j in range(len(GROUPS[grp])):
                            mm = pe.matmul(ps[:, 6 + m % 2, P * j:P * (j + 1)], qm[:, m % 2, P * j:P * (j + 1)],
                                           keysT[:, m % 2, :], start=True, stop=True)
                        mm.then_inc(k_ps, 1)

                    for grp, tiles in enumerate(GROUPS):
                        if grp:
                            pe.wait_ge(q_ok, 16)
                            pe.wait_ge(k_ok, 16)
                        for pn in range(8):
                            w = panel(pe, where["out", 8 * grp + pn])
                            for j, t in enumerate(tiles):
                                n = pn if grp == 0 else 8 + 3 * pn + j
                                if n >= 4:
                                    pe.wait_ge(scaled, n - 3)
                                for k in range(KD):
                                    lhs = attnT[:, k, P * t:P * (t + 1)] if k < 8 else y2T[:, k - 8, P * t:P * (t + 1)]
                                    mm = pe.matmul(ps[:, 4 + n % 4, 0:PC], lhs, w[:, k, :], start=(k == 0), stop=(k == KD - 1))
                                mm.then_inc(mix_ps, 1)
                            pe.wait_ge(mix_ps, n + 1)
                            pe.nop().then_inc(panel_used, 1)
                        pe.wait_ge(x1_ok, tiles[-1] + 1)
                        pe.nop().then_inc(panel_used, 1)
                        for t in tiles:
                            src = h2_cur if t == 0 else h2_work[t % 2]
                            pe.wait_ge(xh_ok, t + 1)
                            for b in range(4):
                                if t >= 1:
                                    pe.wait_ge(ev_ok, 4 * (t - 1) + b + 1)
                                for k in range(4):
                                    mm = pe.transpose(ps[:, b, P * k:P * (k + 1)], src[:, P * (4 * b + k):P * (4 * b + k + 1)], ident)
                                mm.then_inc(tr_ok, 1)
                        pe.wait_ge(ev_ok, 4 * (tiles[-1] + 1))
                        hT2 = h2T_rest if grp else h2T_first
                        width = P * len(tiles)
                        for m in range(2 * PH):
                            n = 16 * grp + m
                            w = panel(pe, where["qp", 8 * grp + m // 2])
                            if m >= 2:
                                pe.wait_ge(q_ok, n - 1)
                            if m == 0:
                                pe.wait_ge(scaled, 8 if grp == 0 else 32)
                            for k in range(KD):
                                mm = pe.matmul(ps[:, 4 + m % 2, 0:width], w[:, k, P * (m % 2):P * (m % 2) + P], hT2[:, k, :],
                                               start=(k == 0), stop=(k == KD - 1))
                            mm.then_inc(q_ps, 1)
                            if m % 2:
                                pe.wait_ge(q_ps, n + 1)
                                if m == 1:
                                    pe.wait_ge(h2_ok, tiles[-1] + 1)
                                    pe.nop().then_inc(panel_used, 1)
                                pe.nop().then_inc(panel_used, 1)
                            if m >= 1:
                                score(grp, m - 1)
                        score(grp, 2 * PH - 1)

                    pe.wait_ge(slots_ok, 2)
                    for n in range(6):
                        mm = pe.transpose(ps[:, n // 4, P * (n % 4):P * (n % 4 + 1)], slot_rows[:, n // 2, n % 2, :], ident)
                    mm.then_inc(slots_ps, 1)
                    pe.wait_ge(k_ok, 32)
                    pe.wait_ge(q_ok, 32)
                    pe.nop().then_inc(b_used, 2)
                    for q in range(NK // QROWS):
                        if q:
                            pe.wait_ge(late_ok, q)
                        with pe.Fori(0, 4) as it:
                            for n in range(4):
                                h, x = divmod(n, 2)
                                if x == 0:
                                    pe.wait_ge(a_ok, it * 2 + (8 * q + h + 1))
                                pe.wait_ge(m_ok, it * 4 + (16 * q + n + 1))
                                for y in range(2):
                                    pe.wait_ge(b_ok, it * 8 + (32 * q + 2 * n + y + 1))
                                    for j in range(8 * y, 8 * y + 8):
                                        mm = pe.matmul(ps[:, 6 + x, QROWS * j:QROWS * (j + 1)], hot_b[y][:, j % 8, :],
                                                       hot_a[:, h, 16 * x + j, :], start=True, stop=True)
                                    mm.then_inc(b_used, 1)
                        pe.wait_ge(m_ok, 16 * (q + 1) + 2)

                        for a in range(QROWS):
                            turn, b = divmod(QROWS * q + a, VB)
                            pe.wait_ge(v_in[b], 16 * (turn + 1))
                            for n in range(8):
                                fresh = a == 0 and (q == 0 or n >= 6)
                                mm = pe.matmul(ps[:, n, :], matrix[:, a, P * (n // 4):P * (n // 4 + 1)],
                                               v_buf[b][:, 512 * (n % 4):512 * (n % 4 + 1)],
                                               start=fresh, stop=True, skip_group_check=True)
                            mm.then_inc(v_used, 1)
                        pe.wait_ge(v_used, QROWS * (q + 1))
                        pe.nop().then_inc(block_ps, 1)

                @block.scalar
                def _(act):
                    def roots(n, ts):
                        act.wait_ge(ask, n + 1)
                        act.activation(rstd[:, ts], rstd[:, ts], ACT.Sqrt).then_inc(root, 1)

                    def h2_columns(t):
                        for b in range(4):
                            act.wait_ge(tr_ok, 4 * t + b + 1)
                            for k in range(4 * b, 4 * b + 4):
                                dst = h2T_first[:, k, :] if t == 0 else h2T_rest[:, k, P * (t - 1):P * t]
                                ins = act.activation(dst, ps[:, b, P * (k % 4):P * (k % 4 + 1)], ACT.Identity,
                                                     bias=modT[:, 48 + k:49 + k], scale=modT[:, 64 + k:65 + k])
                            ins.then_inc(ev_ok, 1)

                    def queries(grp):
                        tiles = GROUPS[grp]
                        width = P * len(tiles)
                        for m in range(2 * PH + 1):
                            n = 16 * grp + m
                            if m < 2 * PH:
                                act.wait_ge(q_ps, n + 1)
                                if n >= 2:
                                    act.wait_ge(k_ps, n - 1)
                                act.copy(qm[:, m % 2, 0:width], ps[:, 4 + m % 2, 0:width]).then_inc(q_ok, 1)
                            if m == 1:
                                act.wait_ge(x1_st, 16 * (tiles[-1] + 1))
                            if m >= 1:
                                act.wait_ge(k_ps, n)
                                act.copy(scores[:, tiles[0]:tiles[-1] + 1, m - 1, :],
                                         ps[:, 6 + (m - 1) % 2, 0:width].rearrange("p (t k) -> p t k", k=NK)).then_inc(k_ok, 1)

                    def gate_exponentials(t):
                        act.wait_ge(gate_a, t + 1)
                        act.activation(best[:, :, :], best[:, :, :], ACT.Exp).then_inc(gate_e, 1)

                    roots(0, slice(0, 1))
                    roots(1, slice(0, 1))
                    h2_columns(0)
                    queries(0)
                    gate_exponentials(0)
                    roots(2, slice(1, 4))
                    roots(3, slice(1, 4))
                    for t in range(1, TT):
                        h2_columns(t)
                    def gelu(t):
                        act.wait_ge(hid_ok, t + 1)
                        act.activation(hiddens[t % 2], hiddens[t % 2], ACT.Gelu).then_inc(act_ok, 1)

                    def columns_one_hot(q, lo, hi):
                        def copy_bank(it, n):
                            act.wait_ge(b_used, it * 8 + (32 * q + 2 * n + 4))
                            act.copy(matrix[:, :, bass.ds(it * 64 + 16 * n, 16)].rearrange("p a t -> p t a"),
                                     ps[:, 6 + n % 2, :].rearrange("p (t a) -> p t a", a=QROWS)).then_inc(m_ok, 1)

                        with act.Fori(lo, hi) as it:
                            for n in range(4):
                                for y in range(2):
                                    act.wait_ge(b_used, it * 8 + (32 * q + 2 * n + y + 1))
                                    for j in range(8):
                                        ins = act.activation(hot_b[y][:, j, :], kc[:, K_IOTA:K_IOTA + NK], ACT.Square,
                                                             bias=slot_T[:, 1, bass.ds(it * 64 + (16 * n + 8 * y + j), 1)])
                                    ins.then_inc(square_ok, 1)
                                    act.wait_ge(square_ok, it * 8 + (32 * q + 2 * n + y + 1))
                                    act.activation(hot_b[y], hot_b[y], ACT.Relu, bias=ones[:, 0:1], scale=-1.0).then_inc(b_ok, 1)
                                if n:
                                    copy_bank(it, n - 1)
                            copy_bank(it, 3)

                    queries(1)
                    gelu(0)
                    gate_exponentials(1)
                    gelu(1)
                    act.wait_ge(slots_ps, 1)
                    flat = ps[:, 0:2, :].rearrange("p a b -> p (a b)")
                    for n in range(3):
                        act.activation(slot_T[:, n, :], flat[:, 256 * n:256 * (n + 1)], ACT.Copy,
                                       scale=-1.0 if n == 1 else 1.0).then_inc(slots_T_ok, 1)
                    act.wait_ge(slots_T_ok, 3)
                    act.wait_ge(h2_st[1], 32)
                    act.nop().then_inc(m_ok, 2)
                    columns_one_hot(0, 0, 4)
                    gate_exponentials(2)
                    columns_one_hot(1, 0, 2)
                    gelu(2)
                    columns_one_hot(1, 2, 4)
                    gate_exponentials(3)
                    columns_one_hot(2, 0, 4)
                    roots(4, slice(0, 1))
                    columns_one_hot(3, 0, 4)
                    gelu(3)
                    for n in range(5, 8):
                        roots(n, slice(0, 1))

                @block.gpsimd
                def _(pool):
                    pool.memset(spare[:, :], 0.0).then_inc(spare_ok, 1)
                    pool.wait_ge(spare_ok, 1)
                    for n, (t, table) in enumerate(PASSES):
                        def gather(h):
                            if table == 0:
                                pool.wait_ge(picked, h + (PH * t + 1))
                            for s in range(TOPK):
                                b = s % NB
                                if not (n == 0 and isinstance(h, int) and s < NB):
                                    pool.wait_ge(row_used, h * TOPK + (SLOTS * n + s - NB + 1))
                                pool.tensor_copy(index[:, b:b + 1], picks[:, t, bass.ds(h * TOPK + s, 1)]).then_inc(index_ok, 1)
                                pool.wait_ge(index_ok, h * TOPK + (SLOTS * n + s + 1))
                                pool.tensor_tensor(spare[:, 0:1], spare[:, 1:2], spare[:, 1:2], ALU.add)
                                pool.indirect_dma_start(expert_rows[b], None, tables[table],
                                                        bass.IndirectOffsetOnAxis(ap=index[:, b:b + 1], axis=0))\
                                    .then_inc(row_in[b], 16)

                        gather(0)
                        if (t, table) == (2, 1):
                            pool.wait_ge(hid_ok, 3)
                            pool.dma_start(h2_at[3], h2_v[:, 3, :]).then_inc(h2_in[3], 16)
                            pool.wait_ge(x1_st, 16 * TT)
                            pool.dma_start(x1_cur, x1_v[:, 2, :]).then_inc(x1_in, 16)
                        if (t, table) == (3, 0):
                            pool.wait_ge(out_ok, 1)
                            pool.dma_start(out_v[:, 2, :], outb).then_inc(out_st, 16)
                            pool.dma_start(x1_cur, x1_v[:, 3, :]).then_inc(x1_in, 16)
                        with pool.Fori(1, PH) as h:
                            gather(h)
                    pool.wait_ge(out_ok, 2)
                    pool.dma_start(out_v[:, 3, :], outb).then_inc(out_st, 16)
                    pool.wait_ge(out_st, 32)

                @block.vector
                def _(dve):
                    v = Chain(dve, dch)

                    def mix_out(grp, pn, row):
                        cols = slice(PC * pn, PC * (pn + 1))
                        for j, t in enumerate(GROUPS[grp]):
                            n = pn if grp == 0 else 8 + 3 * pn + j
                            dve.wait_ge(mix_ps, n + 1)
                            if n >= 2:
                                dve.wait_ge(mix_ok, n - 1)
                            dve.tensor_tensor(mixw[:, n % 2, :], ps[:, 4 + n % 4, 0:PC], row[:, cols], ALU.mult).then_inc(scaled, 1)
                            dve.wait_ge(scaled, n + 1)
                            dve.scalar_tensor_tensor(resid[:, t, cols], resid[:, t, cols], ALPHA, mixw[:, n % 2, :],
                                                     ALU.mult, ALU.add).then_inc(mix_ok, 1)
                        dve.wait_ge(mix_ok, n + 1)

                    def statistics(n, tiles, srcs):
                        for t, src in zip(tiles, srcs):
                            for q in range(4):
                                ins = dve.bn_stats(stats[:, q, :], src[:, 512 * q:512 * (q + 1)])
                            v(ins)
                            v(dve.bn_aggr(mv[:, t, :], stats[:, :, :]))
                        r = rstd[:, tiles[0]:tiles[-1] + 1]
                        v(dve.tensor_scalar(r, mv[:, tiles[0]:tiles[-1] + 1, 1], EPS, None, ALU.add))
                        dve.nop().then_inc(ask, 1)

                    def inverse(n, tiles):
                        r = rstd[:, tiles[0]:tiles[-1] + 1]
                        dve.wait_ge(root, n + 1)
                        v(dve.reciprocal(r, r))

                    def standardise(dst, src, t):
                        return dve.tensor_scalar(dst, src, mv[:, t, 0:1], rstd[:, t:t + 1], ALU.subtract, ALU.mult)

                    def first_norm(grp, t):
                        rows = panel(dve, where["rows", 2 * grp]).rearrange("p k c -> p (k c)")
                        r = resid[:, t, :]
                        v(standardise(r, r, t))
                        v(dve.tensor_tensor(r, r, rows[:, 0:D], ALU.mult))
                        dve.tensor_tensor(r, r, rows[:, D:2 * D], ALU.add).then_inc(x1_ok, 1)
                        dve.wait_ge(x1_ok, t + 1)

                    def second_norm(t):
                        if t == 3:
                            dve.wait_ge(h2_st[1], 16)
                        dst = h2_cur if t == 0 else h2_work[t % 2]
                        standardise(dst, resid[:, t, :], t).then_inc(xh_ok, 1)

                    def modulate(grp, t):
                        rows = panel(dve, where["rows", 2 * grp + 1]).rearrange("p k c -> p (k c)")
                        h = h2_cur if t == 0 else h2_work[t % 2]
                        dve.wait_ge(tr_ok, 4 * (t + 1))
                        v(dve.tensor_tensor(h, h, rows[:, D:2 * D], ALU.mult))
                        dve.tensor_tensor(h, h, rows[:, 0:D], ALU.add).then_inc(h2_ok, 1)

                    def choose_head(t, h):
                        largest_keys(t, h)
                        largest_sums(t, h)

                    def largest_keys(t, h):
                        dve.wait_ge(k_ok, 2 * h + 2 if t == 0 else 16 + 2 * h + 2)
                        both = (2 * h, 2 * h + 1)

                        def each(op):
                            for m in both:
                                op(m, scores[:, t, m, :]).then_inc(dch, 1)
                                v.n += 1
                            dve.wait_ge(dch, v.n)

                        each(lambda m, s: dve.max(top[:, m, 0:8], s))
                        each(lambda m, s: dve.max_index(topi[:, m, 0:8], top[:, m, 0:8], s))
                        each(lambda m, s: dve.match_replace(s, top[:, m, 0:8], s, -3.0e38))
                        each(lambda m, s: dve.max(top[:, m, 8:16], s))
                        each(lambda m, s: dve.max_index(topi[:, m, 8:16], top[:, m, 8:16], s))
                        square = [P, TOPK, TOPK]
                        dve.tensor_copy(topf[:, :, :], topi[:, 2 * h:2 * h + 2, :]).then_inc(dch, 1)
                        v.n += 1
                        v(dve.tensor_tensor(cand[:, 0], top[:, 2 * h, :].unsqueeze(2).broadcast_to(square),
                                            top[:, 2 * h + 1, :].unsqueeze(1).broadcast_to(square), ALU.add))

                    def largest_sums(t, h):
                        s = cand[:, 0].rearrange("p a b -> p (a b)")
                        v(dve.max(best[:, h, 0:8], s))
                        v(dve.max_index(besti[:, h, 0:8], best[:, h, 0:8], s))
                        v(dve.match_replace(s, best[:, h, 0:8], s, -3.0e38))
                        v(dve.max(best[:, h, 8:16], s))
                        v(dve.max_index(besti[:, h, 8:16], best[:, h, 8:16], s))
                        dve.tensor_scalar(half_u[:, 0, :], besti[:, h, :], 4, None, ALU.logical_shift_right).then_inc(dch, 1)
                        v.n += 1
                        v(dve.tensor_scalar(half_u[:, 1, :], besti[:, h, :], 15, None, ALU.bitwise_and))
                        v(dve.tensor_copy(half_f[:, :, :], half_u[:, :, :]))
                        squares = [P, 2, TOPK, TOPK]
                        iota = kc[:, K_IOTA:K_IOTA + TOPK].unsqueeze(1).unsqueeze(1).broadcast_to(squares)
                        v(dve.tensor_tensor(cand, half_f[:, :, :].unsqueeze(3).broadcast_to(squares), iota, ALU.is_equal))
                        v(dve.tensor_tensor(cand, cand, topf[:, :, :].unsqueeze(2).broadcast_to(squares), ALU.mult))
                        v(dve.tensor_reduce(side, cand, AX, ALU.add))
                        v(dve.scalar_tensor_tensor(side[:, 0, :], side[:, 0, :], float(NK), side[:, 1, :], ALU.mult, ALU.add))
                        dve.tensor_copy(picks[:, t, TOPK * h:TOPK * (h + 1)], side[:, 0, :]).then_inc(picked, 1)

                    def gate_values(t):
                        v(dve.tensor_copy(gsum, best[:, :, 0:1]))
                        v(dve.tensor_tensor(best[:, :, :], best[:, :, :], gsum.broadcast_to([P, PH, TOPK]), ALU.subtract))
                        dve.nop().then_inc(gate_a, 1)
                        dve.wait_ge(gate_e, t + 1)
                        v(dve.tensor_reduce(gsum, best[:, :, :], AX, ALU.add))
                        v(dve.reciprocal(gsum, gsum))
                        v(dve.tensor_tensor(gates[:, t, :].rearrange("p (h s) -> p h s", h=PH), best[:, :, :],
                                            gsum.broadcast_to([P, PH, TOPK]), ALU.mult))

                    def dot_products(t, lo, hi):
                        n = PASSES.index((t, 0))
                        with dve.Fori(lo, hi) as it:
                            for b in range(NB):
                                dve.wait_ge(row_in[b], (it + (n * TURNS + 1)) * 16)
                                dve.tensor_tensor_reduce(expert_rows[b], expert_rows[b], h2_at[t], 1.0, 0.0, ALU.mult, ALU.add,
                                                         dots[:, b:b + 1]).then_inc(row_used, 1)
                            dve.wait_ge(row_used, it * NB + (n * SLOTS + NB))
                            dve.tensor_copy(hiddens[t % 2][:, bass.ds(it * NB, NB)], dots[:, :]).then_inc(dot_ok, 1)
                            dve.wait_ge(dot_ok, it + (t * TURNS + 1))

                    def coefficients(t, dst):
                        dve.wait_ge(act_ok, t + 1)
                        v(dve.tensor_tensor(dst, hiddens[t % 2], gates[:, t, :], ALU.mult))

                    def slots(t):
                        coefficients(t, slot_rows[:, 2, t, :])
                        half = besti[:, :, :].rearrange("p h s -> p (h s)")
                        v(dve.tensor_scalar(half, picks[:, t, :], 7, None, ALU.logical_shift_right))
                        v(dve.tensor_copy(slot_rows[:, 0, t, :], half))
                        v(dve.tensor_scalar(half, picks[:, t, :], NK - 1, None, ALU.bitwise_and))
                        v(dve.tensor_copy(slot_rows[:, 1, t, :], half))
                        dve.nop().then_inc(slots_ok, 1)

                    def rows_one_hot(q, r):
                        iota = kc[:, K_IOTA + QROWS * q:K_IOTA + QROWS * (q + 1)].unsqueeze(1).broadcast_to([P, 32, QROWS])
                        for h in range(2):
                            n = 8 * q + 2 * r + h
                            if n >= 2:
                                dve.wait_ge(b_used, 4 * (n - 1) + 2)
                            first_t = 64 * r + 32 * h
                            wide = [slot_T[:, z, first_t:first_t + 32].unsqueeze(2).broadcast_to([P, 32, QROWS]) for z in (0, 2)]
                            v(dve.tensor_tensor(hot_a[:, h], wide[0], iota, ALU.is_equal))
                            dve.tensor_tensor(hot_a[:, h], hot_a[:, h], wide[1], ALU.mult).then_inc(a_ok, 1)

                    def add_late_banks(q):
                        dve.wait_ge(block_ps, q + 1)
                        for n in range(2):
                            if q == 0:
                                ins = dve.tensor_copy(late[n], ps[:, 6 + n, :])
                            else:
                                ins = dve.tensor_tensor(late[n], late[n], ps[:, 6 + n, :], ALU.add)
                        v(ins)
                        dve.nop().then_inc(late_ok, 1)

                    def weighted_rows(t, lo, hi):
                        n = PASSES.index((t, 1))
                        with dve.Fori(lo, hi) as it:
                            for b in range(NB):
                                dve.wait_ge(row_in[b], (it + (n * TURNS + 1)) * 16)
                                a = acc[b % 2]
                                dve.wait_ge(row_used, it * NB + (n * SLOTS + b - 1))
                                dve.scalar_tensor_tensor(a, expert_rows[b], coef[:, bass.ds(it * NB + b, 1)], a,
                                                         ALU.mult, ALU.add).then_inc(row_used, 1)

                    def last_norm(t):
                        dve.wait_ge(row_used, SLOTS * (PASSES.index((t, 1)) + 1))
                        dve.wait_ge(x1_in, 16 * (t - 1))
                        a = acc[0]
                        v(dve.tensor_tensor(a, acc[0], acc[1], ALU.add))
                        v(dve.tensor_tensor(a, a, row_g2, ALU.mult))
                        v(dve.scalar_tensor_tensor(a, x1_cur, ALPHA, a, ALU.mult, ALU.add))
                        n = 4 if t == 2 else 7
                        statistics(n, (0,), (a,))
                        inverse(n, (0,))
                        v(standardise(outb, a, 0))
                        v(dve.tensor_tensor(outb, outb, row_lg2, ALU.mult))
                        dve.tensor_tensor(outb, outb, row_lb2, ALU.add).then_inc(out_ok, 1)

                    def dense_norm(t, step):
                        a = dense_sum[t]
                        if step == 0:
                            whole = 4 - 2 * t
                            dve.wait_ge(dense_x1_in, 32)
                            v(dve.tensor_tensor(a[:, 0:512 * whole], ps[:, 4 * t:4 * t + whole, :].rearrange("p a b -> p (a b)"),
                                                row_g2[:, 0:512 * whole], ALU.mult))
                            for n in range(2 * t):
                                cols = slice(512 * (2 + n), 512 * (3 + n))
                                v(dve.tensor_tensor(a[:, cols], late[n], row_g2[:, cols], ALU.mult))
                            v(dve.scalar_tensor_tensor(a, dense_x1[t], ALPHA, a, ALU.mult, ALU.add))
                        if step == 1:
                            statistics(5 + t, (0,), (a,))
                        if step == 2:
                            inverse(5 + t, (0,))
                            v(standardise(a, a, 0))
                        if step == 3:
                            v(dve.tensor_tensor(a, a, row_lg2, ALU.mult))
                            dve.tensor_tensor(a, a, row_lb2, ALU.add).then_inc(dense_ok, 1)

                    def side_work(n):
                        for q, (parts, end) in enumerate(MATRIX_STEPS):
                            if n in parts:
                                rows_one_hot(q, parts.index(n))
                            if n == end:
                                add_late_banks(q)
                        if n in (2, 6, 7, 8, 10):
                            choose_head(2, 3 + (2, 6, 7, 8, 10).index(n))
                        if n == 11:
                            gate_values(2)
                        if 17 <= n < 25:
                            choose_head(3, n - 17)
                        if n == 25:
                            gate_values(3)
                        if 54 <= n < 62:
                            dense_norm((n - 54) // 4, (n - 54) % 4)

                    dve.wait_ge(row_in1, 16)
                    dve.wait_ge(x_in2, 16 * TT)
                    for pn in range(8):
                        mix_out(0, pn, row_g1)
                    statistics(0, (0,), (resid[:, 0, :],))
                    inverse(0, (0,))
                    first_norm(0, 0)
                    statistics(1, (0,), (resid[:, 0, :],))
                    inverse(1, (0,))
                    second_norm(0)
                    modulate(0, 0)
                    choose_head(0, 0)

                    rest = GROUPS[1]
                    sources = [resid[:, t, :] for t in rest]
                    for pn in range(8):
                        if pn < 7:
                            largest_keys(0, pn + 1)
                        dot_products(0, 2 * pn, 2 * pn + 1)
                        if pn < 7:
                            largest_sums(0, pn + 1)
                        else:
                            gate_values(0)
                        dot_products(0, 2 * pn + 1, 2 * pn + 2)
                        mix_out(1, pn, row_g1)
                    statistics(2, rest, sources)
                    dot_products(0, 16, 17)
                    inverse(2, rest)
                    for t in rest:
                        first_norm(1, t)
                        dot_products(0, 16 + t, 17 + t)
                    statistics(3, rest, sources)
                    dot_products(0, 20, 21)
                    inverse(3, rest)
                    for t in rest:
                        second_norm(t)
                        dot_products(0, 20 + t, 21 + t)
                        modulate(1, t)
                    for n in range(3):
                        dot_products(0, 24 + 2 * n, 25 + 2 * n)
                        largest_keys(1, n)
                        dot_products(0, 25 + 2 * n, 26 + 2 * n)
                        largest_sums(1, n)
                    dot_products(0, 30, 32)
                    dve.nop().then_inc(hid_ok, 1)

                    dve.wait_ge(h2_in[1], 16)
                    for n in range(5):
                        largest_keys(1, 3 + n)
                        dot_products(1, 2 * n, 2 * n + 1)
                        largest_sums(1, 3 + n)
                        dot_products(1, 2 * n + 1, 2 * n + 2)
                    gate_values(1)
                    for n in range(3):
                        dot_products(1, 10 + 4 * n, 12 + 4 * n)
                        largest_keys(2, n)
                        dot_products(1, 12 + 4 * n, 14 + 4 * n)
                        largest_sums(2, n)
                    dot_products(1, 22, 26)
                    slots(0)
                    dot_products(1, 26, TURNS)
                    dve.nop().then_inc(hid_ok, 1)
                    slots(1)
                    dve.wait_ge(slots_T_ok, 3)

                    for t in (2, 3):
                        dve.wait_ge(h2_in[t], 16)
                        for n in range(TURNS // 2):
                            dot_products(t, 2 * n, 2 * n + 2)
                            side_work(n + (t - 2) * TURNS)
                        dve.nop().then_inc(hid_ok, 1)
                        coefficients(t, coef)
                        if t == 2:
                            dve.wait_ge(rows_in, 48)
                        else:
                            dve.wait_ge(out_st, 16)
                        for a in acc:
                            v(dve.memset(a, 0.0))
                        for n in range(TURNS // 2):
                            weighted_rows(t, 2 * n, 2 * n + 2)
                            side_work(n + (t - 2) * TURNS + TURNS // 2)
                        last_norm(t)


_INS = ['x', 'c', 'positions', 'w_ada', 'b_ada', 'w_in', 'lam_re', 'lam_im', 'log_dt', 'ssm_b_re', 'ssm_b_im',
        'ssm_c_re', 'ssm_c_im', 'ssm_d', 'w_glu', 'b_glu', 'g_attn', 'g_ssm', 'w_out', 'ln1_g', 'ln1_b', 'w_qp',
        'sub_keys', 'expert_u', 'expert_v', 'ln2_g', 'ln2_b']


def kernel(**inputs):
    import concourse.bacc as _bacc
    from concourse.bass_utils import run_bass_kernel_spmd as _run

    nc = _bacc.Bacc("TRN2", target_bir_lowering=False, num_devices=1)
    arrays, args = {}, []
    for name in _INS:
        a = np.ascontiguousarray(inputs[name])
        arrays[f"in_{name}"] = a
        args.append(nc.dram_tensor(f"in_{name}", a.shape, mybir.dt.from_np(a.dtype), kind="ExternalInput").ap())
    arrays["in_constants"] = constants()
    consts = nc.dram_tensor("in_constants", (P, K_END), F32, kind="ExternalInput").ap()
    mod_rows = nc.dram_tensor("mod_rows", (96, P), F32, kind="Internal").ap()
    x1_rows = nc.dram_tensor("x1_rows", (T, D), F32, kind="Internal").ap()
    h2_rows = nc.dram_tensor("h2_rows", (T, D), F32, kind="Internal").ap()
    out = nc.dram_tensor("out_x", (1, T, D), F32, kind="ExternalOutput").ap()
    hybrid_layer(nc, consts, *args, mod_rows, x1_rows, h2_rows, out)
    r = _run(nc, [arrays], core_ids=[0])
    return r.results[0]["out_x"]
```
